# Optimizing a Trainium2 kernel written in Bass

```python
import jax, jax.numpy as jnp
from jax import lax
import numpy as np
import math

D_MODEL = 2048
BATCH = 1
SEQ = 256
DEPTH = 1

HEAD_DIM = 64
ATTN_HEADS = D_MODEL // 128
KV_HEADS = ATTN_HEADS // 4
Q_DIM = ATTN_HEADS * HEAD_DIM
KV_DIM = KV_HEADS * HEAD_DIM
WINDOW = 128
ATTN_BLOCK = 128
ROPE_THETA = 10000.0
D_INNER = D_MODEL
SSM_HEAD_DIM = 64
SSM_HEADS = D_INNER // SSM_HEAD_DIM
SSM_GROUPS = 4
D_STATE = 128
CONV_WIDTH = 4
CHUNK = 128
CONV_DIM = D_INNER + 2 * SSM_GROUPS * D_STATE
FFN_HIDDEN = -(-(8 * D_MODEL) // (3 * 256)) * 256
PLE_DIM = 256
IN_DIM = Q_DIM + 2 * KV_DIM + D_INNER + CONV_DIM + SSM_HEADS + 2 * D_MODEL
NORM_EPS = 1e-6
SSM_NORM_EPS = 1e-5


def rmsnorm(x, g, eps=NORM_EPS):
    xf = x.astype(jnp.float32)
    y = xf * lax.rsqrt(jnp.mean(xf * xf, axis=-1, keepdims=True) + eps)
    return (y * g.astype(jnp.float32)).astype(x.dtype)

def apply_rope(t, positions):
    half = HEAD_DIM // 2
    inv_freq = ROPE_THETA ** (-jnp.arange(half, dtype=jnp.float32) * 2.0 / HEAD_DIM)
    ang = positions.astype(jnp.float32)[..., None] * inv_freq
    cos, sin = jnp.cos(ang)[:, :, None, :], jnp.sin(ang)[:, :, None, :]
    t1, t2 = t[..., :half], t[..., half:]
    return jnp.concatenate([t1 * cos - t2 * sin, t2 * cos + t1 * sin], axis=-1)

def sliding_window_sink_attention(q, k, v, sinks):
    b, s = q.shape[0], q.shape[1]
    nb = s // ATTN_BLOCK
    grp = ATTN_HEADS // KV_HEADS
    qb = q.reshape(b, nb, ATTN_BLOCK, KV_HEADS, grp, HEAD_DIM)

    def banded(t):
        tb = t.reshape(b, nb, ATTN_BLOCK, KV_HEADS, HEAD_DIM)
        prev = jnp.pad(tb, ((0, 0), (1, 0), (0, 0), (0, 0), (0, 0)))[:, :-1]
        return jnp.concatenate([prev, tb], axis=2)

    kw, vw = banded(k), banded(v)
    scores = jnp.einsum('bnqhgd,bnkhd->bnhgqk', qb, kw) * (HEAD_DIM ** -0.5)
    qi = jnp.arange(ATTN_BLOCK)[:, None] + ATTN_BLOCK
    kj = jnp.arange(2 * ATTN_BLOCK)[None, :]
    dist = qi - kj
    key_pos = (jnp.arange(nb) * ATTN_BLOCK)[:, None, None] - ATTN_BLOCK + kj[None]
    valid = (dist >= 0)[None] & (dist < WINDOW)[None] & (key_pos >= 0)
    scores = jnp.where(valid[None, :, None, None], scores, -jnp.inf)
    sink = sinks.astype(jnp.float32).reshape(KV_HEADS, grp)[None, None, :, :, None]
    m = jnp.maximum(scores.max(axis=-1), sink)
    e = jnp.exp(scores - m[..., None])
    probs = e / (e.sum(axis=-1) + jnp.exp(sink - m))[..., None]
    out = jnp.einsum('bnhgqk,bnkhd->bnqhgd', probs, vw)
    return out.reshape(b, s, Q_DIM)

def causal_depthwise_conv(x, w, bias):
    out = lax.conv_general_dilated(
        x, w[:, None, :], window_strides=(1,), padding=[(CONV_WIDTH - 1, 0)],
        dimension_numbers=('NWC', 'WIO', 'NWC'), feature_group_count=x.shape[-1])
    return out + bias

def ssd_chunked(xh, dt, a_neg, bm, cm):
    b, s = xh.shape[0], xh.shape[1]
    nc = s // CHUNK
    e_per = SSM_HEADS // SSM_GROUPS
    xd = (xh * dt[..., None]).reshape(b, nc, CHUNK, SSM_GROUPS, e_per, SSM_HEAD_DIM)
    a = jnp.transpose((dt * a_neg).reshape(b, nc, CHUNK, SSM_GROUPS, e_per), (0, 1, 3, 4, 2))
    a_cs = jnp.cumsum(a, axis=-1)
    bc = bm.reshape(b, nc, CHUNK, SSM_GROUPS, D_STATE)
    cc = cm.reshape(b, nc, CHUNK, SSM_GROUPS, D_STATE)
    tril = jnp.tril(jnp.ones((CHUNK, CHUNK), dtype=bool))
    diff = a_cs[..., :, None] - a_cs[..., None, :]
    decay = jnp.where(tril, jnp.exp(jnp.where(tril, diff, 0.0)), 0.0)
    cb = jnp.einsum('bclgn,bcsgn->bcgls', cc, bc)
    y_diag = jnp.einsum('bcgels,bcsgep->bclgep', cb[:, :, :, None] * decay, xd)
    decay_states = jnp.exp(a_cs[..., -1:] - a_cs)
    states = jnp.einsum('bclgn,bcgel,bclgep->bcgepn', bc, decay_states, xd)
    chunk_decay = jnp.exp(a_cs[..., -1])

    def step(carry, inp):
        st, dec = inp
        return carry * dec[..., None, None] + st, carry

    init = jnp.zeros((b, SSM_GROUPS, e_per, SSM_HEAD_DIM, D_STATE), jnp.float32)
    _, prev = lax.scan(step, init, (jnp.moveaxis(states, 1, 0), jnp.moveaxis(chunk_decay, 1, 0)))
    prev = jnp.moveaxis(prev, 0, 1)
    y_off = jnp.einsum('bclgn,bcgepn,bcgel->bclgep', cc, prev, jnp.exp(a_cs))
    return (y_diag + y_off).reshape(b, s, SSM_HEADS, SSM_HEAD_DIM)

def _dense(key, shape, fan_in):
    return jax.random.normal(key, shape, jnp.float32) * (fan_in ** -0.5)

def first_inputs(seed: int = 0) -> dict:
    key = jax.random.key(seed)
    ks = jax.random.split(key, 24)
    L = DEPTH
    ones_noise = lambda k, shape: 1.0 + 0.05 * jax.random.normal(k, shape, jnp.float32)
    dt0 = jnp.exp(jax.random.uniform(ks[5], (L, SSM_HEADS), jnp.float32, np.log(1e-3), np.log(1e-1)))
    return {
        "x": jax.random.normal(ks[0], (BATCH, SEQ, D_MODEL), jnp.float32),
        "p": jax.random.normal(ks[1], (DEPTH, BATCH, SEQ, PLE_DIM), jnp.float32),
        "positions": jnp.tile(jnp.arange(SEQ, dtype=jnp.int32)[None], (BATCH, 1)),
        "g_mix": ones_noise(ks[2], (L, D_MODEL)),
        "w_in": _dense(ks[3], (L, D_MODEL, IN_DIM), D_MODEL),
        "conv_w": _dense(ks[4], (L, CONV_WIDTH, CONV_DIM), CONV_WIDTH),
        "conv_b": 0.02 * jax.random.normal(ks[6], (L, CONV_DIM), jnp.float32),
        "dt_bias": dt0 + jnp.log(-jnp.expm1(-dt0)),
        "a_log": jnp.log(jax.random.uniform(ks[7], (L, SSM_HEADS), jnp.float32, 1.0, 16.0)),
        "d_skip": ones_noise(ks[8], (L, SSM_HEADS)),
        "g_ssd": ones_noise(ks[9], (L, D_INNER)),
        "sinks": 0.5 * jax.random.normal(ks[10], (L, ATTN_HEADS), jnp.float32),
        "w_attn_br": _dense(ks[11], (L, Q_DIM, D_MODEL), Q_DIM),
        "w_ssd_br": _dense(ks[12], (L, D_INNER, D_MODEL), D_INNER),
        "w_o": _dense(ks[13], (L, D_MODEL, D_MODEL), D_MODEL),
        "g_ffn": ones_noise(ks[14], (L, D_MODEL)),
        "w_gate": _dense(ks[15], (L, D_MODEL, FFN_HIDDEN), D_MODEL),
        "w_up": _dense(ks[16], (L, D_MODEL, FFN_HIDDEN), D_MODEL),
        "w_down": _dense(ks[17], (L, FFN_HIDDEN, D_MODEL), FFN_HIDDEN),
        "g_ple": ones_noise(ks[18], (L, D_MODEL)),
        "w_ple_gate": _dense(ks[19], (L, D_MODEL, D_MODEL), D_MODEL),
        "w_ple_proj": _dense(ks[20], (L, PLE_DIM, D_MODEL), PLE_DIM),
        "g_final": ones_noise(ks[21], (D_MODEL,)),
    }

def first_block(x, p, positions, g_mix, w_in, conv_w, conv_b, dt_bias, a_log, d_skip, g_ssd,
              sinks, w_attn_br, w_ssd_br, w_o, g_ffn, w_gate, w_up, w_down, g_ple,
              w_ple_gate, w_ple_proj, g_final):
    b, s = x.shape[0], x.shape[1]
    f32 = jnp.float32
    sizes = [Q_DIM, KV_DIM, KV_DIM, D_INNER, CONV_DIM, SSM_HEADS, D_MODEL, D_MODEL]
    offsets = [int(o) for o in np.cumsum(sizes)[:-1]]
    h = x
    for i in range(DEPTH):
        u = rmsnorm(h, g_mix[i])
        proj = u @ w_in[i]
        q, k, v, z, xbc, dt_raw, g_a, g_s = jnp.split(proj, offsets, axis=-1)

        q = apply_rope(q.astype(f32).reshape(b, s, ATTN_HEADS, HEAD_DIM), positions)
        k = apply_rope(k.astype(f32).reshape(b, s, KV_HEADS, HEAD_DIM), positions)
        v = v.astype(f32).reshape(b, s, KV_HEADS, HEAD_DIM)
        attn = sliding_window_sink_attention(q, k, v, sinks[i]).astype(x.dtype)
        out_a = attn @ w_attn_br[i]

        xbc = jax.nn.silu(causal_depthwise_conv(xbc, conv_w[i], conv_b[i])).astype(f32)
        xs, bm, cm = jnp.split(xbc, [D_INNER, D_INNER + SSM_GROUPS * D_STATE], axis=-1)
        xh = xs.reshape(b, s, SSM_HEADS, SSM_HEAD_DIM)
        dt = jax.nn.softplus(dt_raw.astype(f32) + dt_bias[i].astype(f32))
        a_neg = -jnp.exp(a_log[i].astype(f32))
        y = ssd_chunked(xh, dt, a_neg,
                        bm.reshape(b, s, SSM_GROUPS, D_STATE),
                        cm.reshape(b, s, SSM_GROUPS, D_STATE))
        y = (y + d_skip[i].astype(f32)[:, None] * xh).reshape(b, s, D_INNER)
        y = rmsnorm(y * jax.nn.silu(z.astype(f32)), g_ssd[i], SSM_NORM_EPS).astype(x.dtype)
        out_s = y @ w_ssd_br[i]

        merged = jax.nn.sigmoid(g_a) * out_a + jax.nn.sigmoid(g_s) * out_s
        h = h + merged @ w_o[i]

        f = rmsnorm(h, g_ffn[i])
        h = h + (jax.nn.silu(f @ w_gate[i]) * (f @ w_up[i])) @ w_down[i]

        gate = jax.nn.sigmoid(rmsnorm(h, g_ple[i]) @ w_ple_gate[i])
        h = h + gate * (p[i] @ w_ple_proj[i])
    return rmsnorm(h, g_final)


ATTN_WIDTH = D_MODEL // 2
N_Q_HEADS = ATTN_WIDTH // HEAD_DIM
N_KV_HEADS = N_Q_HEADS // 4
GQA_GROUP = N_Q_HEADS // N_KV_HEADS
N_BRANCH = 3
CMP_LEN = 32
CMP_STRIDE = 16
CMP_OVERLAP = CMP_LEN // CMP_STRIDE
SLC_LEN = 64
SLC_TOPK = 16
WINDOW_2 = 512
Q_BLOCK = 64
CONV_CHANNELS = D_MODEL - ATTN_WIDTH
CONV_TAPS = 31
D_MIX = ATTN_WIDTH + CONV_CHANNELS
D_FF = ((8 * D_MODEL // 3 + 255) // 256) * 256
FFN_CONV_TAPS = 3
N_BUCKETS = 32
MAX_DISTANCE = 128
NEG_INF = -1e30

Q_COLS = ATTN_WIDTH
KV_COLS = N_BRANCH * 2 * N_KV_HEADS * HEAD_DIM
GATE_COLS = N_BRANCH * N_Q_HEADS
CONV_IN_COLS = 2 * CONV_CHANNELS
IN_COLS = Q_COLS + KV_COLS + GATE_COLS + CONV_IN_COLS


def rms_norm(x, g):
    xf = x.astype(jnp.float32)
    y = xf * lax.rsqrt(jnp.mean(xf * xf, axis=-1, keepdims=True) + NORM_EPS)
    return (y * g.astype(jnp.float32)).astype(x.dtype)

def layer_norm(x, g, b):
    xf = x.astype(jnp.float32)
    mu = jnp.mean(xf, axis=-1, keepdims=True)
    xc = xf - mu
    var = jnp.mean(xc * xc, axis=-1, keepdims=True)
    y = xc * lax.rsqrt(var + NORM_EPS) * g.astype(jnp.float32) + b.astype(jnp.float32)
    return y.astype(x.dtype)

def t5_bucket(dist):
    n = jnp.maximum(dist, 0)
    max_exact = N_BUCKETS // 2
    nf = jnp.maximum(n, 1).astype(jnp.float32)
    large = max_exact + (jnp.log(nf / max_exact) / math.log(MAX_DISTANCE / max_exact)
                         * (N_BUCKETS - max_exact)).astype(jnp.int32)
    large = jnp.minimum(large, N_BUCKETS - 1)
    return jnp.where(n < max_exact, n, large)

def masked_softmax(s, mask):
    s = jnp.where(mask, s.astype(jnp.float32), NEG_INF)
    p = jax.nn.softmax(s, axis=-1)
    return jnp.where(mask, p, 0.0)

def causal_depthwise_conv_2(x, w, b):
    taps, c = w.shape
    y = lax.conv_general_dilated(x, w[:, None, :].astype(x.dtype), window_strides=(1,),
                                 padding=[(taps - 1, 0)],
                                 dimension_numbers=('NWC', 'WIO', 'NWC'),
                                 feature_group_count=c)
    return y + b.astype(x.dtype)

def compress_tokens(tok, pos, w1, w2):
    b, t, h, d = tok.shape
    n_chunk = t // CMP_STRIDE
    n_cmp = n_chunk - CMP_OVERLAP + 1
    chunks = tok.reshape(b, n_chunk, CMP_STRIDE, h, d)
    blocks = jnp.concatenate([chunks[:, o:o + n_cmp] for o in range(CMP_OVERLAP)], axis=2)
    blocks = blocks + pos[None, None, :, None, :].astype(tok.dtype)
    flat = blocks.transpose(0, 1, 3, 2, 4).reshape(b, n_cmp, h, CMP_LEN * d)
    return jax.nn.silu(flat @ w1) @ w2

def nsa_attention(q, kv, gates, rel_bias, cmp_pos, cmp_w1, cmp_w2):
    b, t_len, hkv, g, dh = q.shape
    scale = HEAD_DIM ** -0.5
    k_cmp = compress_tokens(kv[:, :, 0, 0], cmp_pos[0], cmp_w1[0], cmp_w2[0])
    v_cmp = compress_tokens(kv[:, :, 0, 1], cmp_pos[1], cmp_w1[1], cmp_w2[1])
    n_cmp = k_cmp.shape[1]
    n_slc = t_len // SLC_LEN
    k_sel = min(SLC_TOPK, n_slc)
    k_slc = kv[:, :, 1, 0].reshape(b, n_slc, SLC_LEN, hkv, dh).transpose(0, 3, 1, 2, 4)
    v_slc = kv[:, :, 1, 1].reshape(b, n_slc, SLC_LEN, hkv, dh).transpose(0, 3, 1, 2, 4)
    pad = ((0, 0), (WINDOW_2, 0), (0, 0), (0, 0))
    k_win = jnp.pad(kv[:, :, 2, 0], pad)
    v_win = jnp.pad(kv[:, :, 2, 1], pad)
    ci_ = jnp.arange(n_cmp)[:, None]
    sj_ = jnp.arange(n_slc)[None, :]
    sel_map = ((ci_ * CMP_STRIDE < (sj_ + 1) * SLC_LEN) &
               (ci_ * CMP_STRIDE + CMP_LEN > sj_ * SLC_LEN)).astype(jnp.float32)
    cmp_end = jnp.arange(n_cmp, dtype=jnp.int32) * CMP_STRIDE + CMP_LEN - 1
    blk_ids = jnp.arange(n_slc, dtype=jnp.int32)[None, :]
    tab_t = rel_bias.reshape(N_BUCKETS, hkv, g).transpose(1, 0, 2)
    h_ar = jnp.arange(hkv)[None, :, None, None, None]
    gather_blocks = jax.vmap(jax.vmap(lambda blk, ii: blk[ii]))

    n_chunks = t_len // Q_BLOCK
    q_ch = q.reshape(b, n_chunks, Q_BLOCK, hkv, g, dh).transpose(1, 0, 3, 2, 4, 5)
    g_ch = gates.reshape(b, n_chunks, Q_BLOCK, hkv, g, N_BRANCH).transpose(1, 0, 3, 2, 4, 5)

    def chunk_fn(args):
        ci, qc, gc = args
        t = ci * Q_BLOCK + jnp.arange(Q_BLOCK, dtype=jnp.int32)
        qs = qc * scale
        s_cmp = jnp.einsum('bhqgd,bnhd->bhqgn', qs, k_cmp).astype(jnp.float32)
        bias_c = rel_bias[t5_bucket(t[:, None] - cmp_end[None, :])]
        bias_c = bias_c.reshape(Q_BLOCK, n_cmp, hkv, g).transpose(2, 0, 3, 1)
        valid_c = (cmp_end[None, :] <= t[:, None])[None, None, :, None, :]
        p_cmp = masked_softmax(s_cmp + bias_c.astype(jnp.float32), valid_c)
        o_cmp = jnp.einsum('bhqgn,bnhd->bhqgd', p_cmp.astype(v_cmp.dtype), v_cmp)
        imp = jnp.einsum('bhqgn,nj->bhqj', p_cmp, sel_map)
        cur = (t // SLC_LEN)[:, None]
        forced = (blk_ids == 0) | (blk_ids == cur) | (blk_ids == cur - 1)
        causal_blk = blk_ids * SLC_LEN <= t[:, None]
        imp = jnp.where(forced, jnp.inf, imp)
        imp = jnp.where(causal_blk, imp, -jnp.inf)
        _, idx = lax.top_k(imp, k_sel)
        kg = gather_blocks(k_slc, idx)
        vg = gather_blocks(v_slc, idx)
        pos = idx[..., None] * SLC_LEN + jnp.arange(SLC_LEN, dtype=jnp.int32)
        dist_s = t[None, None, :, None, None] - pos
        bias_s = jnp.moveaxis(tab_t[h_ar, t5_bucket(dist_s)], -1, 3)
        s_sel = jnp.einsum('bhqgd,bhqkld->bhqgkl', qs, kg).astype(jnp.float32)
        s_sel = (s_sel + bias_s.astype(jnp.float32)).reshape(b, hkv, Q_BLOCK, g, k_sel * SLC_LEN)
        valid_s = (dist_s >= 0).reshape(b, hkv, Q_BLOCK, 1, k_sel * SLC_LEN)
        p_sel = masked_softmax(s_sel, valid_s).reshape(b, hkv, Q_BLOCK, g, k_sel, SLC_LEN)
        o_sel = jnp.einsum('bhqgkl,bhqkld->bhqgd', p_sel.astype(vg.dtype), vg)
        kw = lax.dynamic_slice_in_dim(k_win, ci * Q_BLOCK, Q_BLOCK + WINDOW_2, axis=1)
        vw = lax.dynamic_slice_in_dim(v_win, ci * Q_BLOCK, Q_BLOCK + WINDOW_2, axis=1)
        kpos = ci * Q_BLOCK - WINDOW_2 + jnp.arange(Q_BLOCK + WINDOW_2, dtype=jnp.int32)
        dist_w = t[:, None] - kpos[None, :]
        valid_w = ((dist_w >= 0) & (dist_w < WINDOW_2) & (kpos[None, :] >= 0))[None, None, :, None, :]
        bias_w = rel_bias[t5_bucket(dist_w)].reshape(Q_BLOCK, Q_BLOCK + WINDOW_2, hkv, g).transpose(2, 0, 3, 1)
        s_win = jnp.einsum('bhqgd,bshd->bhqgs', qs, kw).astype(jnp.float32)
        p_win = masked_softmax(s_win + bias_w.astype(jnp.float32), valid_w)
        o_win = jnp.einsum('bhqgs,bshd->bhqgd', p_win.astype(vw.dtype), vw)
        return gc[..., 0:1] * o_cmp + gc[..., 1:2] * o_sel + gc[..., 2:3] * o_win

    out = lax.map(chunk_fn, (jnp.arange(n_chunks, dtype=jnp.int32), q_ch, g_ch))
    out = out.transpose(1, 0, 3, 2, 4, 5)
    return out.reshape(b, t_len, ATTN_WIDTH)

def conformer_conv(h2, conv_w, conv_b, ln_g, ln_b):
    a, gate = jnp.split(h2, 2, axis=-1)
    u = a * jax.nn.sigmoid(gate)
    u = causal_depthwise_conv_2(u, conv_w, conv_b)
    u = layer_norm(u, ln_g, ln_b)
    return jax.nn.silu(u)

def conv_glu_ffn(h, w_up, cw, cb, w_down):
    u = causal_depthwise_conv_2(h @ w_up, cw, cb)
    a, gate = jnp.split(u, 2, axis=-1)
    return (jax.nn.silu(gate) * a) @ w_down

def second_inputs(seed: int = 0) -> dict:
    key = jax.random.key(seed)
    ks = jax.random.split(key, 18)
    f32 = jnp.float32
    nrm = lambda k, shape, s: jax.random.normal(k, shape, f32) * s
    return {
        "x": nrm(ks[0], (BATCH, SEQ, D_MODEL), 1.0),
        "rel_bias": nrm(ks[1], (N_BUCKETS, N_Q_HEADS), 0.5),
        "mix_norm_g": 1.0 + nrm(ks[2], (DEPTH, D_MODEL), 0.02),
        "w_in": nrm(ks[3], (DEPTH, D_MODEL, IN_COLS), D_MODEL ** -0.5),
        "cmp_pos": nrm(ks[4], (DEPTH, 2, CMP_LEN, HEAD_DIM), 0.1),
        "cmp_w1": nrm(ks[5], (DEPTH, 2, CMP_LEN * HEAD_DIM, HEAD_DIM), (CMP_LEN * HEAD_DIM) ** -0.5),
        "cmp_w2": nrm(ks[6], (DEPTH, 2, HEAD_DIM, HEAD_DIM), HEAD_DIM ** -0.5),
        "conv_w": nrm(ks[7], (DEPTH, CONV_TAPS, CONV_CHANNELS), CONV_TAPS ** -0.5),
        "conv_b": nrm(ks[8], (DEPTH, CONV_CHANNELS), 0.01),
        "conv_ln_g": 1.0 + nrm(ks[9], (DEPTH, CONV_CHANNELS), 0.02),
        "conv_ln_b": nrm(ks[10], (DEPTH, CONV_CHANNELS), 0.01),
        "w_out": nrm(ks[11], (DEPTH, D_MIX, D_MODEL), D_MIX ** -0.5),
        "ffn_norm_g": 1.0 + nrm(ks[12], (DEPTH, D_MODEL), 0.02),
        "w_up": nrm(ks[13], (DEPTH, D_MODEL, 2 * D_FF), D_MODEL ** -0.5),
        "ffn_conv_w": nrm(ks[14], (DEPTH, FFN_CONV_TAPS, 2 * D_FF), FFN_CONV_TAPS ** -0.5),
        "ffn_conv_b": nrm(ks[15], (DEPTH, 2 * D_FF), 0.01),
        "w_down": nrm(ks[16], (DEPTH, D_FF, D_MODEL), D_FF ** -0.5),
        "final_norm_g": 1.0 + nrm(ks[17], (D_MODEL,), 0.02),
    }

def second_block(x, rel_bias, mix_norm_g, w_in, cmp_pos, cmp_w1, cmp_w2, conv_w, conv_b,
              conv_ln_g, conv_ln_b, w_out, ffn_norm_g, w_up, ffn_conv_w, ffn_conv_b,
              w_down, final_norm_g):
    b, t_len, _ = x.shape
    splits = [Q_COLS, Q_COLS + KV_COLS, Q_COLS + KV_COLS + GATE_COLS]
    for l in range(DEPTH):
        h = rms_norm(x, mix_norm_g[l])
        proj = h @ w_in[l]
        q, kv, gate_logits, conv_in = jnp.split(proj, splits, axis=-1)
        q = q.reshape(b, t_len, N_KV_HEADS, GQA_GROUP, HEAD_DIM)
        kv = kv.reshape(b, t_len, N_BRANCH, 2, N_KV_HEADS, HEAD_DIM)
        gates = jax.nn.sigmoid(gate_logits).reshape(b, t_len, N_KV_HEADS, GQA_GROUP, N_BRANCH)
        attn = nsa_attention(q, kv, gates, rel_bias, cmp_pos[l], cmp_w1[l], cmp_w2[l])
        conv = conformer_conv(conv_in, conv_w[l], conv_b[l], conv_ln_g[l], conv_ln_b[l])
        x = x + jnp.concatenate([attn, conv], axis=-1) @ w_out[l]
        h = rms_norm(x, ffn_norm_g[l])
        x = x + conv_glu_ffn(h, w_up[l], ffn_conv_w[l], ffn_conv_b[l], w_down[l])
    return rms_norm(x, final_norm_g)


def setup_inputs(seed=0):
    out = dict(first_inputs(seed))
    for name, value in second_inputs(seed + 1).items():
        if name != "x":
            out[name + "_2"] = value
    return out


def reference(
    x, p, positions, g_mix, w_in, conv_w, conv_b, dt_bias, a_log, d_skip, g_ssd, sinks,
    w_attn_br, w_ssd_br, w_o, g_ffn, w_gate, w_up, w_down, g_ple, w_ple_gate, w_ple_proj,
    g_final, rel_bias_2, mix_norm_g_2, w_in_2, cmp_pos_2, cmp_w1_2, cmp_w2_2, conv_w_2,
    conv_b_2, conv_ln_g_2, conv_ln_b_2, w_out_2, ffn_norm_g_2, w_up_2, ffn_conv_w_2,
    ffn_conv_b_2, w_down_2, final_norm_g_2,
):
    x = first_block(
        x, p, positions, g_mix, w_in, conv_w, conv_b, dt_bias, a_log, d_skip, g_ssd, sinks,
        w_attn_br, w_ssd_br, w_o, g_ffn, w_gate, w_up, w_down, g_ple, w_ple_gate, w_ple_proj,
        g_final,
    )
    return second_block(
        x, rel_bias_2, mix_norm_g_2, w_in_2, cmp_pos_2, cmp_w1_2, cmp_w2_2, conv_w_2, conv_b_2,
        conv_ln_g_2, conv_ln_b_2, w_out_2, ffn_norm_g_2, w_up_2, ffn_conv_w_2, ffn_conv_b_2,
        w_down_2, final_norm_g_2,
    )


_drawn_inputs = setup_inputs


def setup_inputs(seed=0):
    import zlib

    import numpy as np

    out = dict(_drawn_inputs(seed))
    spreads = {}
    factors = {'conv_b': 3.386,
     'd_skip': 3.203,
     'sinks': 7.612,
     'g_ple': 6.527,
     'mix_norm_g_2': 5.321,
     'cmp_pos_2': 2.846,
     'conv_b_2': 20.484,
     'conv_ln_g_2': 18.064,
     'conv_ln_b_2': 37.871,
     'ffn_norm_g_2': 3.89,
     'ffn_conv_b_2': 22.066,
     'final_norm_g_2': 22.075}
    for name, (base, spread) in spreads.items():
        noise = np.random.default_rng([zlib.crc32(name.encode()), seed]).standard_normal(out[name].shape)
        drawn = base * np.exp(spread * noise) if base else spread * noise
        out[name] = __import__('jax').numpy.asarray(drawn.astype(out[name].dtype))
    for name, factor in factors.items():
        out[name] = (out[name] * factor).astype(out[name].dtype)
    return out
```

```python
from collections import deque

import numpy as np

import concourse.bass as bass
from concourse import mybir

F32 = mybir.dt.float32
F32R = mybir.dt.float32r
I32 = mybir.dt.int32
ALU = mybir.AluOpType
ACT = mybir.ActivationFunctionType
AXX = mybir.AxisListType.X

P = 128
T = 256
D = 2048
KD = D // P
FFN = 5632
NEG = -1e30

NSUB = 4
NRAW = 6
NHL = 4
LEAD = 3
LAG = 1

MATS = ["ident", "rot", "dup0", "dup1", "rdup0", "rdup1", "triu", "negT", "ones", "anti"]

VECS = [("g_mix", 16), ("cw", 96), ("cb", 24), ("g_ssd", 16), ("dsk", 16), ("g_ffn", 16), ("g_ple", 16),
        ("g_fin", 16), ("gm2", 16), ("cw2", 248), ("cb2", 8), ("lng", 8), ("lnb", 8), ("gf2", 16),
        ("fcw", 264), ("fcb", 88), ("gfin2", 16), ("invf", 1)]
VOFF = {}
_o = 0
for _n, _w in VECS:
    VOFF[_n] = (_o, _w)
    _o += _w
NVEC = _o


class Queues:

    def __init__(self, sems):
        self.sems = sems
        self.q = {k: [] for k in ("pe", "act", "dve", "pool", "sp")}
        self.count = {k: 0 for k in sems}
        self.seen = {}

    def put(self, eng, fn, waits, inc=None, by=1):
        for w in waits:
            if w is None:
                continue
            name, value = w
            if self.seen.get((eng, name), 0) >= value:
                continue
            self.seen[(eng, name)] = value
            self.q[eng].append(("wait", self.sems[name], value))
        if inc is None:
            self.q[eng].append(("op", fn, None, 0))
            return None
        self.count[inc] += by
        self.q[eng].append(("op", fn, self.sems[inc], by))
        return (inc, self.count[inc])

    def run(self, eng, e):
        for item in self.q[eng]:
            if item[0] == "wait":
                e.wait_ge(item[1], item[2])
            else:
                _, fn, sem, by = item
                ins = fn(e)
                if sem is not None:
                    ins.then_inc(sem, by)


class Acts:

    def __init__(self, tensor, base, n):
        self.t, self.base, self.n = tensor, base, n
        self.ready = [None] * n
        self.read = None

    def hi(self, k):
        return self.t[:, self.base + k, 0:T]

    def lo(self, k):
        return self.t[:, self.base + k, T:2 * T]


def hybrid_block_kernel(nc, a, out):
    names = ["pe", "act", "dve", "pool"]
    sems = {n: nc.alloc_semaphore(f"s_{n}") for n in names}
    for i in range(NRAW):
        sems[f"w{i}"] = nc.alloc_semaphore(f"s_w{i}")
    for n in ("cm", "mk", "p1", "p2", "out1", "cv", "row", "pos", "x", "c33", "ohc", "rel", "bmw", "bmr", "p", "w1k", "w1v", "w2c", "out"):
        sems[n] = nc.alloc_semaphore(f"s_d_{n}")
    Q = Queues(sems)

    BASE = 16512
    top = [BASE]

    def place(name, shape, dt=F32, at=None):
        n = 4
        for s in shape[1:]:
            n *= s
        if at is None:
            at = top[0]
            top[0] += (n + 31) // 32 * 32
        return nc.alloc_sbuf_tensor_at(name, shape, dt, offset=at)

    RAW = [place(f"raw{i}", [P, NSUB, 256]) for i in range(NRAW)]
    WH = [place(f"wh{i}", [P, NSUB, 256], F32R) for i in range(NHL)]
    WL = [place(f"wl{i}", [P, NSUB, 256], F32R) for i in range(NHL)]
    at_ah = top[0]
    AHt = place("AHt", [P, 16, 512], F32R)
    at_ch = top[0]
    CHt = place("CHt", [P, 16, 512], F32R)
    at_big = top[0]
    BIGt = place("BIGt", [P, 22, 512], F32R)
    H = place("H", [P, 16, T])
    M9 = place("M9", [P, len(MATS), P])
    CV = place("CV", [P, NVEC])
    RB = [place("RB0", [P, T + 2]), place("RB1", [P, T + 2])]
    SQA = place("SQA", [P, 2, T])
    Z = [place("Z0", [P, 2, 286]), place("Z1", [P, 2, 286])]
    TA = place("TA", [P, 2, T])
    TB = place("TB", [P, 2, T])
    TC = place("TC", [P, 2, T])
    ROW = place("ROW", [P, 80])
    NAT = place("NAT", [P, 8, 2, 32])
    at_nat = top[0] - 2048
    W2 = nc.alloc_sbuf_tensor_at("W2C", [64, 2, 64], F32, offset=at_nat)
    GAT = nc.alloc_sbuf_tensor_at("GAT", [P, 2, 48], F32, offset=at_nat + 1024)
    CBI = place("CBI", [P, 30, 16])
    SM = place("SM", [P, 64])
    G12 = place("G12", [P, 16])
    assert top[0] <= 229368, top[0]

    XS = place("XS", [P, 16, T], at=at_ch)
    MG = place("MG", [P, 16, T], at=at_ch + 16384)
    QT = place("QT", [P, 8, T], at=at_ch + 16384)
    KDU = place("KDU", [P, 4, T], at=at_ch + 24576)
    VN = place("VN", [P, 2, T], at=at_ch + 28672)
    KT1 = place("KT1", [P, 2, T], at=at_ch + 30720)
    sc = at_big + 16384
    BCT = place("BCT", [P, 8, T], at=sc)
    COS = place("COS", [P, T], at=sc + 8192)
    SIN = place("SIN", [P, T], at=sc + 9216)
    MK1 = place("MK1", [P, 384], at=sc + 10240)
    SX1 = place("SX1", [P, 2, 384], at=sc + 12288)
    PT1 = place("PT1", [P, 2, 384], at=sc + 15360)
    RO = place("RO", [P, 2, 2, T], at=sc + 18432)
    PI = place("PI", [P, T], I32, at=sc + 22528)
    XD = place("XD", [P, 2, 512], at=sc + 8192)
    XDS = place("XDS", [P, 512], at=sc + 12288)
    STG = place("STG", [P, 512], at=sc + 14336)
    BNC = place("BNC", [P, 3, P], at=sc + 16384)
    DEC = place("DEC", [P, 4, P], at=sc + 17920)
    MMT = place("MMT", [P, 4, P], at=sc + 19968)
    CXE = place("CXE", [P, 4, P], at=sc + 22016)
    ECS = place("ECS", [P, 4, P], at=sc + 24064)
    C33 = place("C33", [33, 400], at=at_big)
    OHC = place("OHC", [33, 3840], at=at_ah)
    RV = place("RV", [16, 384], at=at_big + 2048)
    BM = place("BM", [P, 16, T], at=at_ch)
    Q2 = place("Q2", [P, 8, T], at=at_ch + 16384)
    KD2 = place("KD2", [P, 2, 4, T], at=at_ch + 24576)
    bg = at_big + 32768
    VN2 = place("VN2", [P, 2, 2, T], at=bg)
    VC = place("VC", [15, T], at=bg + 4096)
    KDC = place("KDC", [P, 4, 15], at=bg + 5120)
    SX2 = place("SX2", [P, 2, 384], at=bg + 5376)
    PT2 = place("PT2", [P, 2, 384], at=bg + 8448)
    SCM = place("SCM", [P, 2, 2, 15], at=bg + 11520)
    BLK = place("BLK", [P, 32, 30], at=bg + 5376)
    KTC = place("KTC", [P, 2, T], at=bg + 9216)
    GCM = place("GCM", [64, 60], at=bg + 11776)
    GTM = place("GTM", [64, 60], at=bg + 12032)
    W1 = [place("W1K", [P, 32, 64], at=at_ah), place("W1V", [P, 32, 64], at=at_ah + 8192)]
    
    BMR = place("BMR", [P, 16, T], at=at_ah + 16384)
    CC = [place(f"CC{i}", [P, T], at=at_ah + (8 + i) * 2048 + 1024) for i in range(8)]
    PPT = place("PPT", [P, 2, T], at=at_ch)
    PHL = place("PHL", [P, 2, 512], F32R, at=at_ch + 2048)
    FO = place("FO", [P, 2, 2, T], at=at_ch)

    PS = nc.alloc_psum_tensor("PS", [P, 8, 512], F32)
    GB = [0, 1, 2]
    scratch = nc.dram_tensor("bias_rows", [16, 384], F32).ap()

    def mat(n):
        return M9[:, MATS.index(n), :]

    def vec(n, i=0, w=1):
        o = VOFF[n][0] + i
        return CV[:, o:o + w]

    def pe(fn, *w, inc=False):
        return Q.put("pe", fn, w, "pe" if inc else None)

    def act(fn, *w):
        return Q.put("act", fn, (*w, ("act", Q.count["act"] + 1 - LAG)), "act")

    def dve(fn, *w):
        return Q.put("dve", fn, (*w, ("dve", Q.count["dve"] + 1 - LAG)), "dve")

    def pool(fn, *w):
        return Q.put("pool", fn, w, "pool")

    def load(eng, name, dst, src, *w):
        return Q.put(eng, lambda e: e.dma_start(dst, src), w, name, 16)

    def mm(o, l, r, start=True, stop=True):
        return lambda e: e.matmul(o, l, r, start=start, stop=stop, skip_group_check=True)

    def tr(o, i, ident):
        return lambda e: e.transpose(o, i, ident)

    def tt(o, x, y, op):
        return lambda e: e.tensor_tensor(o, x, y, op)

    def ts(o, x, s1, s2, o0, o1=None):
        if o1 is None:
            return lambda e: e.tensor_scalar(o, x, s1, None, o0)
        return lambda e: e.tensor_scalar(o, x, s1, s2, o0, o1)

    def stt(o, x, s, y, o0, o1):
        return lambda e: e.scalar_tensor_tensor(out=o, in0=x, scalar=s, in1=y, op0=o0, op1=o1)

    def af(o, x, f, **k):
        return lambda e: e.activation(o, x, f, **k)

    def cp(o, x):
        return lambda e: e.tensor_copy(o, x)

    ADD, SUB, MUL, MAX, MIN = ALU.add, ALU.subtract, ALU.mult, ALU.max, ALU.min

    def two(ap):
        return ap.unsqueeze(1).broadcast_to([ap.shape[0], 2, ap.shape[1]])

    def last(ap, n):
        return ap.unsqueeze(ap.ndim).broadcast_to(list(ap.shape) + [n])

    def bank(b):
        return PS[:, b, :].rearrange("p (m t) -> p m t", m=2)

    free = {b: None for b in range(8)}
    rd = {}

    def f32(ap):
        return ap.bitcast(F32)

    def split_to(dst, k, v, tok, scale=1.0, *w):
        hi = act(af(dst.hi(k), v, ACT.Copy, scale=scale), tok, *w)
        lo = dve(stt(dst.lo(k), v, scale, f32(dst.hi(k)), MUL, SUB), hi, tok, *w)
        dst.ready[k] = lo
        return lo

    units = []

    def unit(w, row0, nk, c0, rhs, evac, nc_=256, natural=False, gens=(), before=None, mid=None):
        units.append(dict(w=w, row0=row0, nk=nk, c0=c0, rhs=rhs, evac=evac, nc=nc_, nat=natural,
                          gens=list(gens), before=before, mid=mid))

    def run_stream(every):
        subs = []
        for u in units:
            k = 0
            while k < u["nk"]:
                n = min(NSUB, u["nk"] - k)
                subs.append((u, k, n))
                k += n
        hilo = {}
        rawfree = {}
        pesub = {}

        def fetch(s):
            u, k, n = subs[s]
            r0 = u["row0"] + k * P
            src = u["w"][r0:r0 + n * P, u["c0"]:u["c0"] + u["nc"]].rearrange("(t p) n -> p t n", p=P)
            tok = load("sp", f"w{s % NRAW}", RAW[s % NRAW][:, 0:n, 0:u["nc"]], src, rawfree.get(s - NRAW))
            hilo[s] = tok

        def split(s):
            u, k, n = subs[s]
            tok = hilo[s]
            raw = RAW[s % NRAW][:, 0:n, 0:u["nc"]]
            hi = WH[s % NHL][:, 0:n, 0:u["nc"]]
            lo = WL[s % NHL][:, 0:n, 0:u["nc"]]
            h = act(af(hi, raw, ACT.Copy), tok, pesub.get(s - NHL))
            d = dve(tt(lo, raw, f32(hi), SUB), tok, h)
            rawfree[s] = d
            hilo[s] = d

        nf = ns = 0
        side = deque()
        gb = 0
        slot = 0
        for s, (u, k, n) in enumerate(subs):
            while nf < len(subs) and nf < s + NRAW + LEAD - 2 and nf - NRAW < ns:
                fetch(nf)
                nf += 1
            while ns < len(subs) and ns <= s + LEAD:
                split(ns)
                ns += 1
                if nf < len(subs) and nf - NRAW < ns:
                    fetch(nf)
                    nf += 1
            if k == 0:
                if u["before"]:
                    u["before"](side)
                b = GB[gb % len(GB)]
                gb += 1
                u["bank"] = b
            b = u["bank"]
            rhs = u["rhs"]
            w = [hilo[s], free[b] if k == 0 else None]
            hi, lo = WH[s % NHL], WL[s % NHL]
            tok = None
            for t in range(n):
                kt = k + t
                w.append(rhs.ready[kt])
                firstk, lastk = kt == 0, kt == u["nk"] - 1
                if u["nat"]:
                    nco = u["nc"]
                    for bb in range(2):
                        o = PS[:, b, bb * nco:(bb + 1) * nco]
                        xh = rhs.hi(kt)[:, bb * P:(bb + 1) * P]
                        xl = rhs.lo(kt)[:, bb * P:(bb + 1) * P]
                        pe(mm(o, xh, hi[:, t, 0:nco], firstk and bb == 0, False), *w)
                        w = []
                        pe(mm(o, xl, hi[:, t, 0:nco], False, False))
                        fin = t == n - 1 and bb == 1
                        tok = pe(mm(o, xh, lo[:, t, 0:nco], False, lastk), inc=fin)
                else:
                    for m in range(2):
                        o = PS[:, b, m * T:(m + 1) * T]
                        wh, wl = hi[:, t, m * P:(m + 1) * P], lo[:, t, m * P:(m + 1) * P]
                        pe(mm(o, wh, rhs.hi(kt), firstk and m == 0, False), *w)
                        w = []
                        pe(mm(o, wh, rhs.lo(kt), False, False))
                        fin = t == n - 1 and m == 1
                        tok = pe(mm(o, wl, rhs.hi(kt), False, lastk), inc=fin)
            pesub[s] = tok
            if k + n == u["nk"]:
                rhs.read = tok
                if u["mid"]:
                    u["mid"]()
                free[b] = u["evac"](b, tok)
                side.extend(u["gens"])
            slot += 1
            if side and slot % every == 0:
                g = side[0]
                if next(g, "end") == "end":
                    side.popleft()
        for g in side:
            for _ in g:
                pass

    def drain(side):
        while side:
            g = side.popleft()
            for _ in g:
                pass

    class Norm:

        def __init__(self, i, n, eps):
            self.i, self.n, self.eps = i, n, eps
            self.tok = None
            self.first = True

        def add(self, src, tok, *w):
            s = act(af(TB[:, :, :], src, ACT.Square), tok, rd.get("TB"), *w)
            if self.first:
                t = dve(cp(SQA[:, :, :], TB[:, :, :]), s, rd.get("SQA"))
                self.first = False
            else:
                t = dve(tt(SQA[:, :, :], SQA[:, :, :], TB[:, :, :], ADD), s, self.last)
            rd["TB"] = t
            self.last = t

        def finish(self, b=7):
            o = PS[:, b, :]
            pe(mm(o[:, 0:T], mat("ones"), SQA[:, 0, :], True, False), self.last, free[b], cmt)
            pe(mm(o[:, 0:T], mat("ones"), SQA[:, 1, :], False, True))
            for c in range(2):
                pe(mm(o[:, T + c:T + c + 1], SQA[:, 0, c * P:(c + 1) * P], mat("ones")[:, 0:1], False, False))
                t = pe(mm(o[:, T + c:T + c + 1], SQA[:, 1, c * P:(c + 1) * P], mat("ones")[:, 0:1], False, True),
                       inc=True)
            rd["SQA"] = t
            r = RB[self.i]
            v = dve(ts(r[:, :], o[:, 0:T + 2], 1.0 / self.n, self.eps, MUL, ADD), t)
            free[b] = v
            v = act(af(r[:, :], r[:, :], ACT.Sqrt), v)
            self.tok = dve(lambda e: e.reciprocal(r[:, :], r[:, :]), v)
            return self.tok

        def rb(self):
            return RB[self.i][:, 0:T]

        def rn(self, c):
            return RB[self.i][:, T + c:T + c + 1]

    def gain(gen):
        gen()
        return
        yield

    cmt = load("sp", "cm", M9[:, :, :].rearrange("p a b -> p (a b)"), a["mats"])
    xt = load("sp", "x", H[:, :, :], a["xT"].rearrange("(t p) n -> p t n", p=P))
    cvt = load("sp", "cv", CV[:, :], a["vecs"])
    post = load("sp", "pos", PI[:, :], a["positions"].partition_broadcast(P))
    mkt = load("sp", "mk", MK1[:, :], a["mask1"])
    rowt = load("sp", "row", ROW[:, :], a["rows"].partition_broadcast(P))
    c33t = load("sp", "c33", C33[:, :], a["c33"])
    oht = load("sp", "ohc", OHC[:, :], a["ohc"])

    z0 = pool(lambda e: e.memset(Z[0][:, :, 0:30], 0.0))
    z0 = pool(lambda e: e.memset(Z[1][:, :, 0:30], 0.0))

    bt = pe(mm(PS[0:16, 6, 0:384], C33[:, 384:400], C33[:, 0:384]), c33t, inc=True)
    rv = dve(cp(RV[:, :], PS[0:16, 6, 0:384]), bt)
    free[6] = rv
    bmw = load("pool", "bmw", scratch, RV[:, :], rv)
    for i in range(30):
        ct = pe(mm(PS[:, 5, i * 16:(i + 1) * 16], OHC[:, i * P:(i + 1) * P], C33[:, 384:400]), oht, inc=i == 29)
    cbt = dve(cp(CBI[:, :, :].rearrange("p a b -> p (a b)"), PS[:, 5, 0:480]), ct)
    free[5] = cbt

    ang, kk, r0 = RO[:, 0, 0, :], RO[:, 0, 1, :], RO[:, 1, 0, :]
    v = dve(cp(ang, PI[:, :]), post)
    v = dve(ts(ang, ang, vec("invf"), None, MUL), v, cvt)
    BIGM = 12582912.0
    v = dve(ts(kk, ang, float(np.float32(1 / (2 * np.pi))), BIGM, MUL, ADD), v)
    v = dve(ts(kk, kk, -BIGM, None, ADD), v)
    c1, c2 = 6.25, 0.033203125
    c3 = float(np.float32(np.round((2 * np.pi - c1 - c2) * 2 ** 27) / 2 ** 27))
    c4 = float(np.float32(2 * np.pi - c1 - c2 - c3))
    src = ang
    for c in (c1, c2, c3, c4):
        v = dve(stt(r0, kk, -c, src, MUL, ADD), v)
        src = r0
    lim = 3.1415925
    v = dve(ts(r0, r0, lim, -lim, MIN, MAX), v)
    s1 = act(af(SIN[:, :], r0, ACT.Sin), v)
    v = dve(ts(kk, r0, -1.0, None, MUL), v)
    v = dve(tt(kk, kk, r0, MAX), v)
    v = dve(ts(kk, kk, -1.0, float(np.float32(np.pi / 2)), MUL, ADD), v)
    trig = act(af(COS[:, :], kk, ACT.Sin), v, s1)

    sinks, dtb, alog = ROW[:, 0:16], ROW[:, 16:48], ROW[:, 48:80]
    NSK = SM[:, 0:16]
    nsk = dve(ts(NSK, sinks, -1.0, None, MUL), rowt)
    aex = act(af(alog, alog, ACT.Exp), rowt)
    g12 = dve(tt(G12[:, :], vec("g_fin", 0, 16), vec("gm2", 0, 16), MUL), cvt)

    ACTS = lambda t, b, n: Acts(t, b, n)
    U1 = ACTS(AHt, 0, 16)
    N1 = Norm(0, D, 1e-6)
    for t in range(8):
        N1.add(H[:, 2 * t:2 * t + 2, :], xt)
        for k in (2 * t, 2 * t + 1):
            w0 = act(af(U1.hi(k), H[:, k, :], ACT.Copy, scale=vec("g_mix", k)), cvt, xt, ct)
            U1.ready[k] = dve(stt(U1.lo(k), H[:, k, :], vec("g_mix", k), f32(U1.hi(k)), MUL, SUB), w0)
    N1.finish()

    w_in = a["w_in"]
    st1 = {"q": [None] * 4, "kd": [None] * 4, "attn": None}

    def ev_q(i):
        def f(b, tok):
            o = QT[:, 2 * i:2 * i + 2, :]
            v = dve(stt(o, bank(b), 0.125, two(N1.rb()), MUL, MUL), tok, N1.tok)
            st1["q"][i] = v
            return v
        return f

    def rope_q(i):
        o = QT[:, 2 * i:2 * i + 2, :]
        b = 6
        pe(mm(PS[:, b, 0:T], mat("rot"), QT[:, 2 * i, :]), st1["q"][i], free[b], cmt)
        tok = pe(mm(PS[:, b, T:512], mat("rot"), QT[:, 2 * i + 1, :]), inc=True)
        yield
        x = RO[:, 0, :, :]
        v = dve(tt(x, bank(b), two(SIN[:, :]), MUL), tok, trig)
        free[b] = v
        y = dve(tt(o, o, two(COS[:, :]), MUL))
        st1["q"][i] = dve(tt(o, o, x, ADD), y)
        yield

    def ev_k(b, tok):
        v = dve(tt(KT1[:, :, :], bank(b), two(N1.rb()), MUL), tok, N1.tok)
        st1["k"] = v
        return v

    def rope_k(t):
        for b, n in ((5, "dup"), (6, "rdup")):
            for hp in range(2):
                tok = pe(mm(PS[:, b, hp * T:(hp + 1) * T], mat(f"{n}{hp}"), KT1[:, t, :]), st1["k"], free[b], inc=True)
        yield
        x, y = RO[:, 0, :, :], RO[:, 1, :, :]
        v1 = dve(tt(x, bank(5), two(COS[:, :]), MUL), tok, trig)
        v2 = dve(tt(y, bank(6), two(SIN[:, :]), MUL), tok)
        free[5], free[6] = v1, v2
        v = dve(tt(KDU[:, 2 * t:2 * t + 2, :], x, y, ADD), v2)
        st1["kd"][2 * t] = st1["kd"][2 * t + 1] = v
        yield

    def ev_v(b, tok):
        for c in range(2):
            v = dve(ts(VN[:, c, :], PS[:, b, c * T:(c + 1) * T], N1.rn(c), None, MUL), tok, N1.tok)
        st1["v"] = v
        return v

    AT = ACTS(BIGt, 0, 8)

    def attn1(t):
        j = t // 2
        for hh in range(2):
            q, k = QT[hh * 64:hh * 64 + 64, t, :], KDU[hh * 64:hh * 64 + 64, j, :]
            pe(mm(PS[:, 3 + hh, 0:128], q[:, 0:128], k[:, 0:128]), st1["q"][t // 2], st1["kd"][j], free[3], free[4])
            tok = pe(mm(PS[:, 3 + hh, 128:384], q[:, 128:256], k[:, 0:256]), inc=True)
        v = dve(tt(SX1[:, :, :], PS[:, 3:5, 0:384], two(MK1[:, :]), ADD), tok, mkt, rd.get("SX1"))
        free[3] = free[4] = v
        NM, DEN, ES, RC = (SM[:, 16 + 4 * i:20 + 4 * i].rearrange("p (h b) -> p h b", b=2) for i in range(4))
        for b, c0, c1_ in ((0, 0, 128), (1, 128, 384)):
            v = dve(lambda e, b=b, c0=c0, c1_=c1_: e.tensor_reduce(NM[:, :, b], SX1[:, :, c0:c1_], AXX, MAX,
                                                                 negate=True), v)
        v = dve(tt(NM, NM, last(NSK[:, 2 * t:2 * t + 2], 2), MIN), v, nsk)
        es = dve(tt(ES, NM, last(sinks[:, 2 * t:2 * t + 2], 2), ADD), v)
        for hh in range(2):
            for b, c0, c1_ in ((0, 0, 128), (1, 128, 384)):
                x = SX1[:, hh, c0:c1_]
                s = act(af(x, x, ACT.Exp, bias=NM[:, hh, b:b + 1], accum_out=DEN[:, hh, b:b + 1]), v)
        s = act(af(ES, ES, ACT.Exp), es)
        v = dve(tt(DEN, DEN, ES, ADD), s)
        v = dve(lambda e: e.reciprocal(RC, DEN), v)
        x0, x1 = SX1[:, :, 0:128], SX1[:, :, 128:384]
        v0 = dve(tt(x0, x0, last(RC[:, :, 0], 128), MUL), v)
        v = dve(tt(x1, x1, last(RC[:, :, 1], 256), MUL), v)
        yield
        for hh in range(2):
            for c in range(3):
                tok = pe(tr(PS[:, 3 + hh, c * 128:(c + 1) * 128], SX1[:, hh, c * 128:(c + 1) * 128], mat("ident")),
                         v, free[3 + hh], inc=True)
        rd["SX1"] = tok
        s = act(af(PT1[:, :, :], PS[:, 3:5, 0:384], ACT.Copy), tok, rd.get("PT1"))
        free[3] = free[4] = s
        yield
        for hh in range(2):
            o = PS[hh * 64:hh * 64 + 64, 5, :]
            vv = [VN[:, c, j * 64:(j + 1) * 64] for c in range(2)]
            pe(mm(o[:, 0:128], vv[0], PT1[:, hh, 0:128]), s, free[5], st1["v"])
            pe(mm(o[:, 128:256], vv[0], PT1[:, hh, 128:256], True, False))
            tok = pe(mm(o[:, 128:256], vv[1], PT1[:, hh, 256:384], False, True), inc=True)
        rd["PT1"] = tok
        free[5] = split_to(AT, t, PS[:, 5, 0:T], tok, 1.0, bmw)
        st1["attn"] = tok
        yield

    def n_(i):
        return NAT[:, i, :, :]

    DT, AN, NCS, DSE = n_(0), n_(1), n_(2), n_(3)[:, 0, :]

    def ev_dt(b, tok):
        x, ax, e_, s_, q_, w_ = DT, n_(4), n_(5), n_(6), n_(7), AN
        for c in range(2):
            v = dve(stt(x[:, c, :], PS[:, b, c * 32:(c + 1) * 32], N1.rn(c), dtb, MUL, ADD), tok, N1.tok, rowt)
        fr = v
        v = dve(ts(ax, x, -1.0, None, MUL), v)
        v = dve(tt(ax, ax, x, MAX), v)
        s = act(af(e_, ax, ACT.Exp, scale=-1.0), v)
        v = dve(ts(s_, e_, 2.0, None, ADD), s)
        v = dve(lambda e: e.reciprocal(s_, s_), v)
        v = dve(tt(s_, s_, e_, MUL), v)
        v = dve(tt(q_, s_, s_, MUL), v)
        v = dve(ts(w_, q_, 1.0 / 17, 1.0 / 15, MUL, ADD), v)
        for c in (13, 11, 9, 7, 5, 3, 1):
            v = dve(tt(w_, w_, q_, MUL), v)
            v = dve(ts(w_, w_, 1.0 / c, None, ADD), v)
        v = dve(tt(w_, w_, s_, MUL), v)
        v = dve(ts(x, x, 0.0, None, MAX), v)
        v = dve(stt(x, w_, 2.0, x, MUL, ADD), v)
        v = dve(stt(AN, x, -1.0, alog.unsqueeze(1).broadcast_to([P, 2, 32]), MUL, MUL), v, aex)
        st1["dt"] = v
        return fr

    def cums():
        o = PS[:, 7, :]
        for c in range(2):
            pe(mm(o[:, c * 32:(c + 1) * 32], mat("triu"), AN[:, c, :]), st1["dt"], free[7])
        tok = pe(mm(o[:, 64:96], mat("ones"), AN[:, 0, :]), inc=True)
        yield
        v = dve(ts(NCS, o[:, 0:64].rearrange("p (c h) -> p c h", c=2), -1.0, None, MUL), tok)
        v = dve(tt(DSE, o[:, 64:96], NCS[:, 0, :], ADD), v)
        free[7] = v
        st1["cs"] = act(af(DSE, DSE, ACT.Exp), v)
        yield

    xbc_ready = [None] * 12

    def ev_xbc(i):
        def f(b, tok):
            z = Z[i % 2]
            fr = v = dve(tt(z[:, :, 30:286], bank(b), two(N1.rb()), MUL), tok, N1.tok, z0, rd.get(f"Z{i % 2}"))
            for k in range(4):
                w = v
                for m in range(2):
                    c = 2 * i + m
                    x = z[:, m, 27 + k:27 + k + T]
                    if k == 0:
                        v = dve(ts(TA[:, m, :], x, vec("cw", 4 * c), vec("cb", c), MUL, ADD), w, rd.get("TA"))
                    else:
                        v = dve(stt(TA[:, m, :], x, vec("cw", 4 * c + k), TA[:, m, :], MUL, ADD), w)
            s = act(af(TB[:, :, :], TA[:, :, :], ACT.Tanh, scale=0.5), v, rd.get("TB"))
            v = dve(stt(TC[:, :, :], TB[:, :, :], 1.0, TA[:, :, :], ADD, MUL), s, rd.get("TC"))
            rd["TB"] = v
            dst = XS[:, 2 * i:2 * i + 2, :] if i < 8 else BCT[:, 2 * (i - 8):2 * (i - 8) + 2, :]
            xbc_ready[i] = rd["TC"] = act(af(dst, TC[:, :, :], ACT.Copy, scale=0.5), v)
            return fr
        return f

    y_ready = [None] * 8

    def ssd(g):
        rdy = [xbc_ready[2 * g], xbc_ready[2 * g + 1], xbc_ready[8 + g // 2], xbc_ready[10 + g // 2], st1["cs"]]
        Bt, Ct = BCT[:, g, :], BCT[:, 4 + g, :]
        for c in range(2):
            for i in range(4):
                tok = pe(tr(PS[:, 3 + c, i * P:(i + 1) * P], XS[:, 4 * g + i, c * P:(c + 1) * P], mat("ident")),
                         *rdy, free[3], free[4], inc=True)
        pe(tr(PS[:, 5, 0:P], Bt[:, 0:P], mat("ident")), free[5])
        for c in range(2):
            tk2 = pe(mm(PS[:, 5, (1 + c) * P:(2 + c) * P], Bt[:, c * P:(c + 1) * P], Ct[:, c * P:(c + 1) * P]),
                     inc=True)
        s0 = act(af(BNC[:, :, :].rearrange("p a b -> p (a b)"), PS[:, 5, 0:384], ACT.Copy), tk2, st1["attn"],
                 rd.get("BNC"))
        free[5] = s0
        for c in range(2):
            v = dve(tt(XD[:, c, :].rearrange("p (h d) -> p h d", d=64),
                       PS[:, 3 + c, :].rearrange("p (h d) -> p h d", d=64),
                       last(DT[:, c, 8 * g:8 * g + 8], 64), MUL), tok, st1["attn"], rd.get("XD"))
        free[3] = free[4] = v
        xd = v
        xds = dve(tt(XDS[:, :].rearrange("p (h d) -> p h d", d=64), XD[:, 0, :].rearrange("p (h d) -> p h d", d=64),
                     last(DSE[:, 8 * g:8 * g + 8], 64), MUL), v)
        yield
        tok = pe(mm(PS[:, 5, :], BNC[:, 0, :], XDS[:, :]), xds, s0, inc=True)
        stt_ = act(af(STG[:, :], PS[:, 5, :], ACT.Copy), tok, rd.get("STG"))
        free[5] = stt_
        for c in range(2):
            for hf in range(2):
                h0 = 8 * g + 4 * hf
                bb = 3 + hf
                for i in range(4):
                    tok = pe(mm(PS[:, bb, i * P:(i + 1) * P], AN[:, c, h0 + i:h0 + i + 1].broadcast_to([P, P]),
                                mat("triu")), free[bb], inc=True)
                bv = PS[:, bb, :].rearrange("p (i l) -> p i l", l=P)
                v = dve(tt(DEC[:, :, :], bv, mat("negT").unsqueeze(1).broadcast_to([P, 4, P]), ADD), tok,
                        rd.get("DEC"))
                free[bb] = v
                if c == 1:
                    s = act(af(ECS[:, :, :], bv, ACT.Exp), v, rd.get("ECS"))
                    free[bb] = s
                    rd["ECS"] = dve(tt(CXE[:, :, :], ECS[:, :, :],
                                       Ct[:, P:2 * P].unsqueeze(1).broadcast_to([P, 4, P]), MUL), s, rd.get("CXE"))
                for i in range(4):
                    s = act(af(DEC[:, i, :], DEC[:, i, :], ACT.Exp, bias=NCS[:, c, h0 + i:h0 + i + 1]), v)
                mt = dve(tt(MMT[:, :, :], DEC[:, :, :], BNC[:, 1 + c, :].unsqueeze(1).broadcast_to([P, 4, P]), MUL),
                         s, s0, rd.get("MMT"))
                rd["DEC"] = mt
                yield
                for i in range(4):
                    hh = 4 * hf + i
                    o = PS[(i % 2) * 64:(i % 2) * 64 + 64, 6, (i // 2) * P:(i // 2 + 1) * P]
                    tok = pe(mm(o, XD[:, c, hh * 64:(hh + 1) * 64], MMT[:, i, :], True, c == 0), mt, free[6], stt_,
                             inc=True)
                    if c == 1:
                        tok = pe(mm(o, STG[:, hh * 64:(hh + 1) * 64], CXE[:, i, :], False, True), inc=True)
                rd["MMT"] = tok
                if c == 1:
                    rd["CXE"] = tok
                for i in range(2):
                    tile = 4 * g + 2 * hf + i
                    y = XS[:, tile, c * P:(c + 1) * P]
                    v = dve(stt(y, y, vec("dsk", tile), PS[:, 6, i * P:(i + 1) * P], MUL, ADD), tok)
                free[6] = v
                if c == 1:
                    y_ready[2 * g + hf] = v
        rd["XD"] = rd["STG"] = rd["BNC"] = tok
        yield

    for i in range(4):
        unit(w_in, 0, 16, 256 * i, U1, ev_q(i), gens=[rope_q(i)])
    unit(w_in, 0, 16, 1024, U1, ev_k, gens=[rope_k(0), rope_k(1)])
    unit(w_in, 0, 16, 1280, U1, ev_v, natural=True, gens=[attn1(t) for t in range(8)])
    unit(w_in, 0, 16, 6656, U1, ev_dt, nc_=32, natural=True, gens=[cums()])
    for i in range(12):
        unit(w_in, 0, 16, 3584 + 256 * i, U1, ev_xbc(i))

    mg = [None] * 8

    def ev_ga(i):
        def f(b, tok):
            v = dve(tt(TA[:, :, :], bank(b), two(N1.rb()), MUL), tok, rd.get("TA"))
            rd["TA"] = s = act(af(MG[:, 2 * i:2 * i + 2, :], TA[:, :, :], ACT.Tanh, scale=0.5), v)
            mg[i] = s
            return v
        return f

    def ev_oa(i):
        def f(b, tok):
            o = MG[:, 2 * i:2 * i + 2, :]
            mg[i] = dve(stt(o, o, 1.0, bank(b), ADD, MUL), tok, mg[i])
            return mg[i]
        return f

    for i in range(8):
        unit(w_in, 0, 16, 6688 + 256 * i, U1, ev_ga(i), before=(lambda side: drain(side)) if i == 0 else None,
             gens=[ssd(g) for g in range(4)] if i == 0 else ())
        unit(a["w_attn_br"], 0, 8, 256 * i, AT, ev_oa(i))

    YH = ACTS(BIGt, 0, 16)
    N2 = Norm(1, D, 1e-5)

    def ev_z(i):
        def f(b, tok):
            z = Z[i % 2][:, :, 30:286]
            fr = v = dve(tt(z, bank(b), two(N1.rb()), MUL), tok)
            s = act(af(TA[:, :, :], z, ACT.Tanh, scale=0.5), v, rd.get("TA"))
            v = dve(stt(TA[:, :, :], TA[:, :, :], 1.0, z, ADD, MUL), s)
            v = dve(stt(TC[:, :, :], TA[:, :, :], 0.5, XS[:, 2 * i:2 * i + 2, :], MUL, MUL), v, rd.get("TC"),
                    y_ready[i])
            N2.add(TC[:, :, :], v)
            for m in range(2):
                k = 2 * i + m
                rd["TC"] = act(af(YH.hi(k), TC[:, m, :], ACT.Copy, scale=vec("g_ssd", k)), v, AT.read, st1["ssd"])
                YH.ready[k] = dve(stt(YH.lo(k), TC[:, m, :], vec("g_ssd", k), f32(YH.hi(k)), MUL, SUB), rd["TC"],
                                  AT.read, st1["ssd"])
            return fr
        return f

    def before_z(side):
        drain(side)
        st1["ssd"] = rd["XD"]

    for i in range(8):
        unit(w_in, 0, 16, 1536 + 256 * i, U1, ev_z(i), before=before_z if i == 0 else None)
    GSB = XS
    gs = [None] * 8

    def ev_gs(i):
        def f(b, tok):
            v = dve(tt(TA[:, :, :], bank(b), two(N1.rb()), MUL), tok, rd.get("TA"))
            rd["TA"] = gs[i] = act(af(GSB[:, 2 * i:2 * i + 2, :], TA[:, :, :], ACT.Tanh, scale=0.5), v)
            return v
        return f

    for i in range(8):
        unit(w_in, 0, 16, 8736 + 256 * i, U1, ev_gs(i), mid=N2.finish if i == 0 else None)
    MH = ACTS(AHt, 0, 16)

    def ev_os(i):
        def f(b, tok):
            s_ = slice(2 * i, 2 * i + 2)
            fr = v = dve(tt(TA[:, :, :], bank(b), two(N2.rb()), MUL), tok, N2.tok, rd.get("TA"))
            v = dve(stt(TA[:, :, :], GSB[:, s_, :], 1.0, TA[:, :, :], ADD, MUL), v, gs[i])
            v = dve(tt(TA[:, :, :], TA[:, :, :], MG[:, s_, :], ADD), v)
            for m in range(2):
                split_to(MH, 2 * i + m, TA[:, m, :], v, 0.5, U1.read)
            rd["TA"] = MH.ready[2 * i + 1]
            return fr
        return f

    for i in range(8):
        unit(a["w_ssd_br"], 0, 16, 256 * i, YH, ev_os(i))

    def ev_h(i, nxt=None, norms=(), prev=lambda: None):
        def f(b, tok):
            h = H[:, 2 * i:2 * i + 2, :]
            fr = v = dve(tt(h, h, bank(b), ADD), tok, rd.get("H"))
            if nxt is not None:
                finish_h(i, v, nxt, norms, prev())
            return fr
        return f

    def finish_h(i, v, nxt, norms, pw):
        h = H[:, 2 * i:2 * i + 2, :]
        dst, gv = nxt
        for m in range(2):
            k = 2 * i + m
            s = act(af(dst.hi(k), H[:, k, :], ACT.Copy, scale=gv(k)), v, pw)
            dst.ready[k] = dve(stt(dst.lo(k), H[:, k, :], gv(k), f32(dst.hi(k)), MUL, SUB), s, pw)
        for n in norms:
            n.add(h, v)

    F1 = ACTS(CHt, 0, 16)
    N3 = Norm(0, D, 1e-6)
    for i in range(8):
        unit(a["w_o"], 0, 16, 256 * i, MH, ev_h(i, (F1, lambda k: vec("g_ffn", k)), [N3], lambda: mhw()))

    def mhw():
        return MH.ready[15]

    def ffn(wg, gcol, wu, ucol, wd, fin, norm, evg, evu, last_h, acts_free, nfin):
        for half in range(2):
            A = ACTS(BIGt, 0, 22)
            for i in range(11):
                unit(wg, 0, 16, gcol + 256 * (11 * half + i), fin, evg(half, i, A),
                     mid=norm.finish if half == 0 and i == 0 else None)
                unit(wu, 0, 16, ucol + 256 * (11 * half + i), fin, evu(half, i, A, acts_free[half]))
            for i in range(8):
                unit(wd, 2816 * half, 22, 256 * i, A, last_h(i) if half else ev_h(i))
            acts_free[1] = lambda A=A: A.read

    def evg1(half, i, A):
        def f(b, tok):
            z = Z[i % 2][:, :, 30:286]
            fr = v = dve(tt(z, bank(b), two(N3.rb()), MUL), tok, N3.tok)
            s = act(af(TA[:, :, :], z, ACT.Tanh, scale=0.5), v, rd.get("TA"))
            rd["g"] = dve(stt(TA[:, :, :], TA[:, :, :], 1.0, z, ADD, MUL), s)
            return fr
        return f

    def evu1(half, i, A, fr_):
        def f(b, tok):
            fr = v = dve(tt(TC[:, :, :], bank(b), two(N3.rb()), MUL), tok, rd.get("TC"), N3.tok)
            v = dve(tt(TC[:, :, :], TC[:, :, :], TA[:, :, :], MUL), v, rd["g"])
            for m in range(2):
                split_to(A, 2 * i + m, TC[:, m, :], v, 0.5, fr_())
            rd["TC"] = A.ready[2 * i + 1]
            return fr
        return f

    P1H = ACTS(AHt, 0, 16)
    N4 = Norm(1, D, 1e-6)
    ffn(a["w_gate"], 0, a["w_up"], 0, a["w_down"], F1, N3, evg1, evu1,
        lambda i: ev_h(i, (P1H, lambda k: vec("g_ple", k)), [N4], lambda: MH.read), [lambda: YH.read, None], N4)

    PH = ACTS(PHL, 0, 2)

    def load_p(side):
        pt = load("pool", "p", PPT[:, :, :], a["pT"].rearrange("(t p) n -> p t n", p=P), F1.read)
        for k in range(2):
            split_to(PH, k, PPT[:, k, :], pt, 1.0, F1.read)

    def ev_pg(i):
        def f(b, tok):
            fr = v = dve(tt(TA[:, :, :], bank(b), two(N4.rb()), MUL), tok, N4.tok, rd.get("TA"))
            rd["pg"] = act(af(TA[:, :, :], TA[:, :, :], ACT.Tanh, scale=0.5), v)
            return fr
        return f

    U2 = ACTS(BIGt, 0, 16)
    N5, N6 = Norm(0, D, 1e-6), Norm(1, D, 1e-6)

    def ev_pp(i):
        def f(b, tok):
            h = H[:, 2 * i:2 * i + 2, :]
            fr = v = dve(stt(TC[:, :, :], TA[:, :, :], 1.0, bank(b), ADD, MUL), tok, rd["pg"], rd.get("TC"))
            rd["TA"] = v
            v = dve(stt(h, TC[:, :, :], 0.5, h, MUL, ADD), v, rd.get("H"))
            finish_h(i, v, (U2, lambda k: G12[:, k:k + 1]), [], acts_f[0]())
            N5.add(h, v)
            for m in range(2):
                s = act(af(TB[:, m, :], H[:, 2 * i + m, :], ACT.Square, scale=vec("g_fin", 2 * i + m)), v, rd["TB"])
            if i == 0:
                rd["TB"] = sqb[0] = dve(cp(SQB, TB[:, :, :]), s)
            else:
                rd["TB"] = sqb[0] = dve(tt(SQB, SQB, TB[:, :, :], ADD), s, sqb[0])
            return fr
        return f

    sqb = [None]
    SQB = Z[1][:, :, 30:286]
    acts_f = [lambda: dn_read()]

    def dn_read():
        return Q_last_big[0]

    Q_last_big = [None]

    def mark_big(side):
        Q_last_big[0] = units_down[-1]["rhs"].read

    units_down = [units[-1]]
    for i in range(8):
        def bf(side, i=i):
            if i == 0:
                mark_big(side)
                load_p(side)
        unit(a["w_ple_gate"], 0, 16, 256 * i, P1H, ev_pg(i), before=bf if i == 0 else None,
             mid=N4.finish if i == 0 else None)
        unit(a["w_ple_proj"], 0, 2, 256 * i, PH, ev_pp(i))

    st2 = {"q": [None] * 4, "kd": {}, "v": {}}
    RX = RB[0]
    RU = RB[1]

    def join():
        t5 = N5.finish(7)
        o = PS[:, 6, :]
        pe(mm(o[:, 0:T], mat("ones"), SQB[:, 0, :], True, False), sqb[0], free[6])
        pe(mm(o[:, 0:T], mat("ones"), SQB[:, 1, :], False, True))
        for c in range(2):
            pe(mm(o[:, T + c:T + c + 1], SQB[:, 0, c * P:(c + 1) * P], mat("ones")[:, 0:1], False, False))
            t = pe(mm(o[:, T + c:T + c + 1], SQB[:, 1, c * P:(c + 1) * P], mat("ones")[:, 0:1], False, True), inc=True)
        rd["SQB"] = t
        yield
        ta = TA[:, :, :].rearrange("p a b -> p (a b)")[:, 0:T + 2]
        v = dve(tt(ta, RX[:, :], RX[:, :], MUL), t5, rd.get("TA"))
        v = dve(stt(ta, o[:, 0:T + 2], 1.0 / D, ta, MUL, MUL), v, t)
        free[6] = v
        v = dve(ts(ta, ta, 1e-6, None, ADD), v)
        s = act(af(ta, ta, ACT.Sqrt), v)
        v = dve(lambda e: e.reciprocal(ta, ta), s)
        N6.tok = dve(tt(RU[:, :], ta, RX[:, :], MUL), v)
        for k in range(16):
            v = dve(stt(H[:, k, :], H[:, k, :], vec("g_fin", k), RX[:, 0:T], MUL, MUL), t5, U2.ready[15])
        st2["x"] = v
        rd["TA"] = v
        st2["bmr"] = load("pool", "bmr", BMR[:, :, :], bass.AP(scratch.tensor, 0, [[1, P], [384, 16], [1, T]]), bmw,
                          P1H.read)
        w1 = a["cmp_w1"]
        for kv in range(2):
            src = w1[kv].rearrange("(l d) e -> d l e", d=64)
            for hp in range(2):
                st2[f"w1{kv}"] = load("pool", "w1k" if kv == 0 else "w1v", W1[kv][hp * 64:hp * 64 + 64, :, :], src,
                                      P1H.read)
        st2["w2"] = load("pool", "w2c", W2[:, 0:2, :], a["cmp_w2"].rearrange("k d e -> d k e"), P1H.read)
        yield

    def turn_bias():
        for i in range(4):
            for b in range(2):
                h = 4 * i + 2 * b
                tok = pe(mm(PS[:, 3 + b, :], mat("anti"), BMR[:, h:h + 2, :]), st2["bmr"], free[3 + b], inc=True)
            rd["CC"] = tok
            yield
            for b in range(2):
                h = 4 * i + 2 * b
                s = act(af(BM[:, h:h + 2, :], bank(3 + b), ACT.Copy), tok, PH.read)
                free[3 + b] = s
        st2["bm"] = s
        yield

    w_in2 = a["w_in_2"]

    def ev_cmp(kv):
        def f(b, tok):
            v = dve(tt(KTC[:, :, :], bank(b), two(N6.rb()), MUL), tok, N6.tok, rd.get("KTC"))
            blk = BLK[:, :, :].rearrange("p l (t n) -> p l t n", t=2)
            pos = a_pos[kv]
            for t in range(2):
                base = KTC[:, t, :]
                fr2 = dve(tt(blk[:, :, t, :],
                             bass.AP(KTC, t * T, [[2 * T, P], [1, 32], [16, 15]]),
                             last(pos, 15), ADD), v, rd.get("BLK"), *st2["pos"])
            rd["BLK_w"] = fr2
            return v
        return f

    a_pos = [None, None]
    PSC = TB[:, 0, 0:64].rearrange("p (k l) -> p k l", k=2)

    def compress(kv):
        bd = BLK[:, :, :]
        for hp in range(2):
            for l in range(32):
                tok = pe(mm(PS[0:64, 3 + hp, 0:30], W1[kv][hp * 64:hp * 64 + 64, l, :],
                            bd[hp * 64:hp * 64 + 64, l, :], l == 0, l == 31),
                         rd["BLK_w"], st2[f"w1{kv}"], free[3], free[4], inc=l == 31)
        rd["BLK"] = rd["KTC"] = tok
        gv = GTM[:, :].rearrange("p (h n) -> p h n", h=2)
        v = dve(cp(gv, PS[0:64, 3:5, 0:30]), tok, rd.get("GTM"))
        free[3] = free[4] = v
        s = act(af(GCM[:, :], GTM[:, :], ACT.Tanh, scale=0.5), v, rd.get("GCM"))
        v = dve(stt(GCM[:, :], GCM[:, :], 1.0, GTM[:, :], ADD, MUL), s)
        v = dve(ts(GCM[:, :], GCM[:, :], 0.5, None, MUL), v)
        yield
        if kv == 0:
            for hh in range(2):
                tok = pe(mm(PS[hh * 64:hh * 64 + 64, 5, 0:60], W2[:, 0, :], GCM[:, :]), v, st2["w2"], free[5], inc=True)
            o = KDC[:, :, :].rearrange("p (t h) n -> p t h n", h=2)
            x = PS[:, 5, 0:60].rearrange("p (h t n) -> p t h n", h=2, t=2)
            for t in range(2):
                v = dve(cp(o[:, t], x[:, t]), tok, rd.get("KDC"))
            st2["kdc"] = free[5] = v
        else:
            for t in range(2):
                for hp in range(2):
                    c = (2 * t + hp) * 64
                    g = GCM[:, hp * 30 + t * 15:hp * 30 + t * 15 + 15]
                    tok = pe(mm(PS[0:15, 5, c:c + 64], g, W2[:, 1, :]), v, free[5], inc=True)
            st2["vc"] = free[5] = dve(cp(VC[:, :], PS[0:15, 5, 0:T]), tok)
        rd["GCM"] = tok
        st2["w1read"] = tok
        yield

    def ev_k2(br):
        def f(b, tok):
            z = Z[br][:, :, 30:286]
            rd["k2"] = dve(tt(z, bank(b), two(N6.rb()), MUL), tok, N6.tok, rd.get("SQB"))
            return rd["k2"]
        return f

    def dup_k2(br):
        z = Z[br][:, :, 30:286]
        for t in range(2):
            b = 5 + t
            for hp in range(2):
                tok = pe(mm(PS[:, b, hp * T:(hp + 1) * T], mat(f"dup{hp}"), z[:, t, :]), rd["k2"], free[b], inc=True)
        rd[f"Z{br}"] = tok
        yield
        for t in range(2):
            b = 5 + t
            v = dve(cp(KD2[:, br, 2 * t:2 * t + 2, :], bank(b)), tok, PH.read)
            free[b] = v
        st2["kd"][br] = v
        yield

    def ev_v2(br):
        def f(b, tok):
            for c in range(2):
                v = dve(ts(VN2[:, br, c, :], PS[:, b, c * T:(c + 1) * T], RU[:, T + c:T + c + 1], None, MUL), tok,
                        N6.tok, Q_last_big[0])
            st2["v"][br] = v
            return v
        return f

    def ev_q2(i):
        def f(b, tok):
            st2["q"][i] = dve(stt(Q2[:, 2 * i:2 * i + 2, :], bank(b), 0.125, two(N6.rb()), MUL, MUL), tok, N6.tok,
                              PH.read)
            return st2["q"][i]
        return f

    def ev_gate(b, tok):
        for c in range(2):
            v = dve(ts(GAT[:, c, :], PS[:, b, c * 48:(c + 1) * 48], RU[:, T + c:T + c + 1], None, MUL), tok, N6.tok)
        s = act(af(GAT[:, :, :], GAT[:, :, :], ACT.Tanh, scale=0.5), v)
        st2["gate"] = dve(ts(GAT[:, :, :], GAT[:, :, :], 0.5, 0.5, MUL, ADD), s)
        return v

    MX = ACTS(AHt, 0, 16)

    def ev_ca(i):
        def f(b, tok):
            rd["ca"] = dve(tt(TC[:, :, :], bank(b), two(N6.rb()), MUL), tok, N6.tok, rd.get("TC"))
            return rd["ca"]
        return f

    ccr = [None] * 8
    SCC = SQA

    def ev_cg(i):
        def f(b, tok):
            z = Z[i % 2]
            fr = v = dve(tt(TA[:, :, :], bank(b), two(N6.rb()), MUL), tok, rd.get("TA"))
            s = act(af(TA[:, :, :], TA[:, :, :], ACT.Tanh, scale=0.5), v)
            v = dve(stt(TC[:, :, :], TA[:, :, :], 1.0, TC[:, :, :], ADD, MUL), s, rd["ca"])
            v = dve(ts(z[:, :, 30:286], TC[:, :, :], 0.5, None, MUL), v, rd.get(f"Z{i % 2}"))
            rd["TC"] = v
            for k in range(31):
                w = v
                for m in range(2):
                    c = 2 * i + m
                    x = z[:, m, k:k + T]
                    o = CC[c][:, :]
                    if k == 0:
                        v = dve(ts(o, x, vec("cw2", 31 * c), vec("cb2", c), MUL, ADD), w, P1H.read, rd["CC"])
                    else:
                        v = dve(stt(o, x, vec("cw2", 31 * c + k), o, MUL, ADD), w)
            for m in range(2):
                c = 2 * i + m
                if c == 0:
                    v = dve(cp(SCC[:, 0, :], CC[c][:, :]), v, rd.get("SQA"))
                else:
                    v = dve(tt(SCC[:, 0, :], SCC[:, 0, :], CC[c][:, :], ADD), v)
            rd["scc"] = v
            return fr
        return f

    def layer_norm():
        tok = pe(mm(PS[:, 7, 0:T], mat("ones"), SCC[:, 0, :]), rd["scc"], free[7], inc=True)
        yield
        mean = TA[:, 0, :]
        v = dve(ts(mean, PS[:, 7, 0:T], 1.0 / 1024, None, MUL), tok, rd.get("TA"))
        free[7] = v
        for c in range(8):
            x = CC[c][:, :]
            v1 = dve(tt(x, x, mean, SUB), v)
            s = act(af(TB[:, c % 2, :], x, ACT.Square), v1, rd.get("TB"), rd.get(f"TB{c % 2}"))
            if c == 0:
                v2 = dve(cp(SCC[:, 0, :], TB[:, 0, :]), s, tok)
            else:
                v2 = dve(tt(SCC[:, 0, :], SCC[:, 0, :], TB[:, c % 2, :], ADD), s, v2)
            rd[f"TB{c % 2}"] = v2
        tok = pe(mm(PS[:, 7, 0:T], mat("ones"), SCC[:, 0, :]), v2, free[7], inc=True)
        yield
        rs = TA[:, 1, :]
        v = dve(ts(rs, PS[:, 7, 0:T], 1.0 / 1024, 1e-6, MUL, ADD), tok)
        free[7] = v
        s = act(af(rs, rs, ACT.Sqrt), v)
        v0 = dve(lambda e: e.reciprocal(rs, rs), s)
        for c in range(8):
            x = CC[c][:, :]
            z = TC[:, c % 2, :]
            v = dve(tt(x, x, rs, MUL), v0)
            v = dve(ts(x, x, vec("lng", c), vec("lnb", c), MUL, ADD), v)
            s = act(af(TB[:, c % 2, :], x, ACT.Tanh, scale=0.5), v, rd[f"TB{c % 2}"])
            v = dve(stt(z, TB[:, c % 2, :], 1.0, x, ADD, MUL), s, rd.get("TC"), rd.get(f"TC{c % 2}"))
            rd[f"TB{c % 2}"] = v
            rd[f"TC{c % 2}"] = split_to(MX, 8 + c, z, v, 0.5)
        rd["TA"] = rd["TC"] = rd["TB"] = v
        rd["SQA"] = tok
        yield

    def attn2(t):
        j = t // 2
        NM, DEN, RC = (SM[:, 16 + 4 * i:20 + 4 * i].rearrange("p (h b) -> p h b", b=2) for i in range(3))
        first = [True, True]

        def pv(hh, cols, v_, p_, stop):
            r = pe(mm(PS[hh * 64:hh * 64 + 64, 6, cols * P:(cols + 1) * P], v_, p_, first[hh], stop), free[6],
                   inc=True)
            first[hh] = False
            return r

        for br in range(2):
            for hh in range(2):
                q, k = Q2[hh * 64:hh * 64 + 64, t, :], KD2[hh * 64:hh * 64 + 64, br, j, :]
                pe(mm(PS[:, 3 + hh, 0:128], q[:, 0:128], k[:, 0:128]), st2["q"][t // 2], st2["kd"][br], free[3],
                   free[4])
                tok = pe(mm(PS[:, 3 + hh, 128:384], q[:, 128:256], k[:, 0:256]), inc=True)
            v = dve(tt(SX2[:, :, 0:128], PS[:, 3:5, 0:128], BM[:, 2 * t:2 * t + 2, 128:256], ADD), tok, st2["bm"],
                    rd.get("SX2"), rd.get("BLK"))
            v = dve(tt(SX2[:, :, 128:384], PS[:, 3:5, 128:384], BM[:, 2 * t:2 * t + 2, :], ADD))
            free[3] = free[4] = v
            for b, c0, c1_ in ((0, 0, 128), (1, 128, 384)):
                v = dve(lambda e, b=b, c0=c0, c1_=c1_: e.tensor_reduce(NM[:, :, b], SX2[:, :, c0:c1_], AXX, MAX,
                                                                     negate=True), v)
            for hh in range(2):
                for b, c0, c1_ in ((0, 0, 128), (1, 128, 384)):
                    x = SX2[:, hh, c0:c1_]
                    s = act(af(x, x, ACT.Exp, bias=NM[:, hh, b:b + 1], accum_out=DEN[:, hh, b:b + 1]), v)
            v = dve(lambda e: e.reciprocal(RC, DEN), s)
            for hh in range(2):
                v = dve(tt(RC[:, hh, :], RC[:, hh, :], GAT[:, :, 3 * (2 * t + hh) + 1 + br], MUL), v, st2["gate"])
            x0, x1 = SX2[:, :, 0:128], SX2[:, :, 128:384]
            dve(tt(x0, x0, last(RC[:, :, 0], 128), MUL), v)
            v = dve(tt(x1, x1, last(RC[:, :, 1], 256), MUL))
            yield
            for hh in range(2):
                for c in range(3):
                    tok = pe(tr(PS[:, 3 + hh, c * 128:(c + 1) * 128], SX2[:, hh, c * 128:(c + 1) * 128],
                                mat("ident")), v, free[3 + hh], inc=True)
            rd["SX2"] = tok
            s = act(af(PT2[:, :, :], PS[:, 3:5, 0:384], ACT.Copy), tok, rd.get("PT2"), rd.get("BLK"))
            free[3] = free[4] = s
            yield
            for hh in range(2):
                vv = [VN2[:, br, c, j * 64:(j + 1) * 64] for c in range(2)]
                pe_wait = (s, st2["v"][br], free[6])
                pe(mm(PS[hh * 64:hh * 64 + 64, 6, 0:P], vv[0], PT2[:, hh, 0:128], first[hh], False), *pe_wait)
                first[hh] = False
                pe(mm(PS[hh * 64:hh * 64 + 64, 6, P:2 * P], vv[0], PT2[:, hh, 128:256], False, False))
                tok = pe(mm(PS[hh * 64:hh * 64 + 64, 6, P:2 * P], vv[1], PT2[:, hh, 256:384], False, False), inc=True)
            rd["PT2"] = tok
        for hh in range(2):
            for b in range(2):
                tok = pe(mm(PS[:, 3 + hh, b * 15:(b + 1) * 15], Q2[hh * 64:hh * 64 + 64, t, b * P:(b + 1) * P],
                            KDC[hh * 64:hh * 64 + 64, j, :]), st2["kdc"], free[3], free[4], inc=True)
        cb = CBI[:, :, :].rearrange("p (b n) h -> p b n h", b=2)
        for hh in range(2):
            v = dve(tt(SCM[:, hh, :, :], PS[:, 3 + hh, 0:30].rearrange("p (b n) -> p b n", b=2),
                       cb[:, :, :, 2 * t + hh], ADD), tok, rd.get("SCM"))
        free[3] = free[4] = v
        v = dve(lambda e: e.tensor_reduce(NM, SCM[:, :, :, :], AXX, MAX), v)
        for hh in range(2):
            x = SCM[:, hh, :, :]
            v1 = dve(tt(x, x, last(NM[:, hh, :], 15), SUB), v)
        s = act(af(SCM[:, :, :, :], SCM[:, :, :, :], ACT.Exp), v1)
        v = dve(lambda e: e.tensor_reduce(DEN, SCM[:, :, :, :], AXX, ADD), s)
        v = dve(lambda e: e.reciprocal(RC, DEN), v)
        v1 = dve(ts(NM, NM, -1e29, None, ALU.is_gt), v1)
        v = dve(tt(RC, RC, NM, MUL), v, v1)
        for hh in range(2):
            v = dve(tt(RC[:, hh, :], RC[:, hh, :], GAT[:, :, 3 * (2 * t + hh)], MUL), v)
        for hh in range(2):
            x = SCM[:, hh, :, :]
            v1 = dve(tt(x, x, last(RC[:, hh, :], 15), MUL), v)
        yield
        for hh in range(2):
            for b in range(2):
                tok = pe(tr(PS[0:15, 3 + hh, b * P:(b + 1) * P], SCM[:, hh, b, :], mat("ident")), v1, free[3 + hh],
                         inc=True)
        rd["SCM"] = tok
        s = act(af(PT2[0:15, :, 0:256], PS[0:15, 3:5, 0:256], ACT.Copy), tok, rd.get("PT2"))
        free[3] = free[4] = s
        yield
        for hh in range(2):
            for b in range(2):
                tok = pe(mm(PS[hh * 64:hh * 64 + 64, 6, b * P:(b + 1) * P], VC[0:15, j * 64:(j + 1) * 64],
                            PT2[0:15, hh, b * P:(b + 1) * P], False, True), s, st2["vc"], inc=True)
        rd["PT2"] = tok
        free[6] = split_to(MX, t, PS[:, 6, 0:T], tok, 1.0, st2["w1read"])
        yield

    def load_pos():
        post_ = load("pool", "p1", PSC[0:64, :, :], a["cmp_posT"], rd.get("TB"))
        post2 = load("pool", "p2", PSC[64:128, :, :], a["cmp_posT"], rd.get("TB"))
        st2["pos"] = (post_, post2)
        a_pos[0], a_pos[1] = PSC[:, 0, :], PSC[:, 1, :]

    unit(w_in2, 0, 16, 1024, U2, ev_cmp(0), before=lambda side: drain(side), mid=lambda: pre_cmp(), gens=[turn_bias()] + [compress(0)])

    def pre_cmp():
        load_pos()
        for _ in join():
            pass

    unit(w_in2, 0, 16, 1280, U2, ev_cmp(1), before=lambda side: drain(side), gens=[compress(1)])
    for br in range(2):
        unit(w_in2, 0, 16, 1536 + 512 * br, U2, ev_k2(br), before=(lambda side: drain(side)) if br == 0 else None,
             gens=[dup_k2(br)])
        unit(w_in2, 0, 16, 1792 + 512 * br, U2, ev_v2(br), natural=True)
    unit(w_in2, 0, 16, 2560, U2, ev_gate, nc_=48, natural=True)
    for i in range(4):
        unit(w_in2, 0, 16, 2608 + 256 * i, U2, ev_ca(i), before=(lambda side: drain(side)) if i == 0 else None)
        unit(w_in2, 0, 16, 3632 + 256 * i, U2, ev_cg(i), gens=[layer_norm()] if i == 3 else ())
    for i in range(4):
        unit(w_in2, 0, 16, 256 * i, U2, ev_q2(i), before=(lambda side: drain(side)) if i == 1 else None,
             gens=[attn2(2 * i), attn2(2 * i + 1)])

    class View:
        def __init__(self, src, k0):
            self.s, self.k0 = src, k0
            self.read = None

        @property
        def ready(self):
            return self.s.ready[self.k0:]

        def hi(self, k):
            return self.s.hi(self.k0 + k)

        def lo(self, k):
            return self.s.lo(self.k0 + k)

    def ev_add(i):
        h = H[:, 2 * i:2 * i + 2, :]
        return lambda b, tok: dve(tt(h, h, bank(b), ADD), tok, st2["x"])

    MXC, MXA = View(MX, 8), View(MX, 0)
    for i in range(8):
        unit(a["w_out_2"], 1024, 8, 256 * i, MXC, ev_add(i))


    F2 = ACTS(CHt, 0, 16)
    N7 = Norm(0, D, 1e-6)
    for i in range(8):
        unit(a["w_out_2"], 0, 8, 256 * i, MXA, ev_h(i, (F2, lambda k: vec("gf2", k)), [N7], lambda: attn_done()),
             before=(lambda side: drain(side)) if i == 0 else None)

    def attn_done():
        return MX.ready[7]

    def conv3(z, o, col, v, *w):
        for k in range(3):
            w_ = v
            for m in range(2):
                c = col + m
                x = z[:, m, 28 + k:28 + k + T]
                if k == 0:
                    v = dve(ts(o[:, m, :], x, vec("fcw", 3 * c), vec("fcb", c), MUL, ADD), w_, *w)
                else:
                    v = dve(stt(o[:, m, :], x, vec("fcw", 3 * c + k), o[:, m, :], MUL, ADD), w_)
        return v

    def evg2(half, i, A):
        def f(b, tok):
            fr = v = dve(tt(Z[0][:, :, 30:286], bank(b), two(N7.rb()), MUL), tok, N7.tok, rd.get("Z0"))
            v = conv3(Z[0], TA, 44 + 2 * (11 * half + i), v, rd.get("TA"))
            s = act(af(TB[:, :, :], TA[:, :, :], ACT.Tanh, scale=0.5), v, rd.get("TB"))
            rd["g"] = rd["TB"] = dve(stt(TA[:, :, :], TB[:, :, :], 1.0, TA[:, :, :], ADD, MUL), s)
            return fr
        return f

    def evu2(half, i, A, fr_):
        def f(b, tok):
            fr = v = dve(tt(Z[1][:, :, 30:286], bank(b), two(N7.rb()), MUL), tok, N7.tok, rd.get("Z1"))
            v = conv3(Z[1], TC, 2 * (11 * half + i), v, rd.get("TC"))
            v = dve(tt(TC[:, :, :], TC[:, :, :], TA[:, :, :], MUL), v, rd["g"])
            for m in range(2):
                split_to(A, 2 * i + m, TC[:, m, :], v, 0.5, fr_())
            rd["TC"] = A.ready[2 * i + 1]
            return fr
        return f

    N8 = Norm(1, D, 1e-6)

    def ev_fin(i):
        def f(b, tok):
            h = H[:, 2 * i:2 * i + 2, :]
            v = dve(tt(h, h, bank(b), ADD), tok)
            N8.add(h, v)
            return v
        return f

    ffn(a["w_up_2"], FFN, a["w_up_2"], 0, a["w_down_2"], F2, N7, evg2, evu2, ev_fin, [lambda: MXA.read, None], N8)

    run_stream(1)

    N8.finish()
    outv = out.rearrange("(t p) n -> p t n", p=P)
    tok = None
    for i in range(8):
        o = FO[:, i % 2, :, :]
        for m in range(2):
            k = 2 * i + m
            v = dve(stt(FO[:, i % 2, m, :], H[:, k, :], vec("gfin2", k), N8.rb(), MUL, MUL), N8.tok, F2.read,
                    rd.get(f"FO{i % 2}"))
        rd[f"FO{i % 2}"] = load("sp", ("out", "out1")[i % 2], outv[:, 2 * i:2 * i + 2, :], o, v)
    for n in ("out", "out1"):
        Q.q["sp"].append(("wait", sems[n], Q.count[n]))

    with nc.Block() as block:
        @block.sync
        def _(e):
            Q.run("sp", e)

        @block.gpsimd
        def _(e):
            Q.run("pool", e)

        @block.scalar
        def _(e):
            Q.run("act", e)

        @block.vector
        def _(e):
            Q.run("dve", e)

        @block.tensor
        def _(e):
            Q.run("pe", e)


def _cols(v):
    v = np.asarray(v)
    return v.reshape(-1, P).T


def _taps(w):
    w = np.asarray(w)
    k, c = w.shape
    return w.reshape(k, c // P, P).transpose(2, 1, 0).reshape(P, -1)


def _bucket(dist):
    n = np.maximum(dist, 0)
    nf = np.maximum(n, 1).astype(np.float32)
    large = 16 + (np.log(nf / np.float32(16)) / np.float32(np.log(8.0)) * np.float32(16)).astype(np.int32)
    return np.where(n < 16, n, np.minimum(large, 31))


def _constants():
    i = np.arange(P)
    eye = np.eye(P, dtype=np.float32)
    rot = np.zeros((P, P), np.float32)
    for m in range(P):
        if m % 64 < 32:
            rot[m + 32, m] = -1.0
        else:
            rot[m - 32, m] = 1.0
    dup = []
    for hp in range(2):
        e = np.zeros((P, P), np.float32)
        e[hp * 64 + i % 64, i] = 1.0
        dup.append(e)
    rdup = [(rot[:, hp * 64 + i % 64]).copy() for hp in range(2)]
    triu = (i[:, None] <= i[None, :]).astype(np.float32)
    negt = np.where(i[:, None] <= i[None, :], 0.0, NEG).astype(np.float32)
    mats = [eye, rot, dup[0], dup[1], rdup[0], rdup[1], triu, negt, np.ones((P, P), np.float32),
            eye[::-1].copy()]
    mats = np.ascontiguousarray(np.concatenate(mats, 1))
    cur = np.where(i[None, :] <= i[:, None], 0.0, NEG)
    prev = np.where(i[None, :] > i[:, None], 0.0, NEG)
    mask1 = np.concatenate([cur, prev, cur], 1).astype(np.float32)
    dist = 255 - np.arange(384)
    oh = np.zeros((33, 384), np.float32)
    for c, d in enumerate(dist):
        if d >= 0:
            oh[_bucket(np.array(d)), c] = 1.0
        else:
            oh[32, c] = NEG
    ohc = np.zeros((33, 2, 15, P), np.float32)
    for b in range(2):
        for n in range(15):
            for q in range(P):
                d = b * P + q - (16 * n + 31)
                if d >= 0:
                    ohc[_bucket(np.array(d)), b, n, q] = 1.0
                else:
                    ohc[32, b, n, q] = NEG
    invf = (np.float32(10000.0) ** (-np.arange(32, dtype=np.float32) * np.float32(2.0) / np.float32(64))).astype(
        np.float32)
    return mats, mask1, oh, ohc.reshape(33, -1), invf[i % 32][:, None]


def kernel(**inputs):
    import concourse.bacc as bacc
    from concourse.bass_utils import run_bass_kernel_spmd

    x = {k: np.asarray(v) for k, v in inputs.items()}
    mats, mask1, oh, ohc, invf = _constants()
    dsk = np.repeat(x["d_skip"][0], 64).reshape(16, P).T
    parts = dict(
        g_mix=_cols(x["g_mix"][0]), cw=_taps(x["conv_w"][0]), cb=_cols(x["conv_b"][0]), g_ssd=_cols(x["g_ssd"][0]),
        dsk=dsk, g_ffn=_cols(x["g_ffn"][0]), g_ple=_cols(x["g_ple"][0]), g_fin=_cols(x["g_final"]),
        gm2=_cols(x["mix_norm_g_2"][0]), cw2=_taps(x["conv_w_2"][0]), cb2=_cols(x["conv_b_2"][0]),
        lng=_cols(x["conv_ln_g_2"][0]), lnb=_cols(x["conv_ln_b_2"][0]), gf2=_cols(x["ffn_norm_g_2"][0]),
        fcw=_taps(x["ffn_conv_w_2"][0]), fcb=_cols(x["ffn_conv_b_2"][0]), gfin2=_cols(x["final_norm_g_2"]),
        invf=invf)
    arrays = {
        "xT": x["x"][0].T,
        "pT": x["p"][0, 0].T,
        "positions": x["positions"].reshape(1, 256),
        "mats": mats,
        "mask1": mask1,
        "vecs": np.concatenate([parts[n] for n, _ in VECS], 1),
        "rows": np.concatenate([x["sinks"][0], x["dt_bias"][0], x["a_log"][0]])[None, :],
        "c33": np.concatenate([oh, np.concatenate([x["rel_bias_2"], np.ones((1, 16), np.float32)], 0)], 1),
        "ohc": ohc,
        "w_in": x["w_in"][0], "w_attn_br": x["w_attn_br"][0], "w_ssd_br": x["w_ssd_br"][0], "w_o": x["w_o"][0],
        "w_gate": x["w_gate"][0], "w_up": x["w_up"][0], "w_down": x["w_down"][0],
        "w_ple_gate": x["w_ple_gate"][0], "w_ple_proj": x["w_ple_proj"][0],
        "w_in_2": x["w_in_2"][0], "cmp_posT": x["cmp_pos_2"][0].transpose(2, 0, 1),
        "cmp_w1": x["cmp_w1_2"][0], "cmp_w2": x["cmp_w2_2"][0], "w_out_2": x["w_out_2"][0],
        "w_up_2": x["w_up_2"][0], "w_down_2": x["w_down_2"][0],
    }
    nc = bacc.Bacc("TRN2", target_bir_lowering=False, num_devices=1)
    feed, args = {}, {}
    for name, v in arrays.items():
        v = np.ascontiguousarray(v)
        feed[f"in_{name}"] = v
        args[name] = nc.dram_tensor(f"in_{name}", v.shape, mybir.dt.from_np(v.dtype), kind="ExternalInput").ap()
    out = nc.dram_tensor("out_T", (D, T), F32, kind="ExternalOutput").ap()
    hybrid_block_kernel(nc, args, out)
    r = run_bass_kernel_spmd(nc, [feed], core_ids=[0])
    return np.ascontiguousarray(r.results[0]["out_T"].T).reshape(1, T, D)
```

```python
from collections import deque

import numpy as np

import concourse.bass as bass
from concourse import mybir

F32 = mybir.dt.float32
F32R = mybir.dt.float32r
I32 = mybir.dt.int32
ALU = mybir.AluOpType
ACT = mybir.ActivationFunctionType
AXX = mybir.AxisListType.X

P = 128
T = 256
D = 2048
KD = D // P
FFN = 5632
NEG = -1e30

NSUB = 4
NRAW = 6
NHL = 4
LEAD = 3
LAG = 1

MATS = ["ident", "rot", "dup0", "dup1", "rdup0", "rdup1", "triu", "negT", "ones", "anti"]

VECS = [("g_mix", 16), ("cw", 96), ("cb", 24), ("g_ssd", 16), ("dsk", 16), ("g_ffn", 16), ("g_ple", 16),
        ("g_fin", 16), ("gm2", 16), ("cw2", 248), ("cb2", 8), ("lng", 8), ("lnb", 8), ("gf2", 16),
        ("fcw", 264), ("fcb", 88), ("gfin2", 16), ("invf", 1)]
VOFF = {}
_o = 0
for _n, _w in VECS:
    VOFF[_n] = (_o, _w)
    _o += _w
NVEC = _o


class Queues:

    def __init__(self, sems):
        self.sems = sems
        self.q = {k: [] for k in ("pe", "act", "dve", "pool", "sp")}
        self.count = {k: 0 for k in sems}
        self.seen = {}

    def put(self, eng, fn, waits, inc=None, by=1):
        for w in waits:
            if w is None:
                continue
            name, value = w
            if self.seen.get((eng, name), 0) >= value:
                continue
            self.seen[(eng, name)] = value
            self.q[eng].append(("wait", self.sems[name], value))
        if inc is None:
            self.q[eng].append(("op", fn, None, 0))
            return None
        self.count[inc] += by
        self.q[eng].append(("op", fn, self.sems[inc], by))
        return (inc, self.count[inc])

    def run(self, eng, e):
        for item in self.q[eng]:
            if item[0] == "wait":
                e.wait_ge(item[1], item[2])
            else:
                _, fn, sem, by = item
                ins = fn(e)
                if sem is not None:
                    ins.then_inc(sem, by)


class Side:

    def __init__(self):
        self.todo, self.live, self.width = deque(), [], 1

    def extend(self, gens):
        self.todo.extend(gens)

    def step(self):
        while self.todo and len(self.live) < self.width:
            if isinstance(self.todo[0], int):
                if self.live:
                    break
                self.width = self.todo.popleft()
            else:
                self.live.append(self.todo.popleft())
        for g in list(self.live):
            if next(g, "end") == "end":
                self.live.remove(g)

    def drain(self):
        while self.todo or self.live:
            self.step()


class Acts:

    def __init__(self, tensor, base, n):
        self.t, self.base, self.n = tensor, base, n
        self.ready = [None] * n
        self.read = None

    def hi(self, k):
        return self.t[:, self.base + k, 0:T]

    def lo(self, k):
        return self.t[:, self.base + k, T:2 * T]


def hybrid_block_kernel(nc, a, out):
    names = ["pe", "act", "dve", "pool"]
    sems = {n: nc.alloc_semaphore(f"s_{n}") for n in names}
    for i in range(NRAW):
        sems[f"w{i}"] = nc.alloc_semaphore(f"s_w{i}")
    for n in ("cm", "mk", "p1", "p2", "cv", "row", "pos", "x0", "x1", "x2", "x3", "c33", "ohc", "rel", "bmw", "bmr", "p", "w1k", "w1v", "w2c", "out"):
        sems[n] = nc.alloc_semaphore(f"s_d_{n}")
    Q = Queues(sems)

    BASE = 16512
    top = [BASE]

    def place(name, shape, dt=F32, at=None):
        n = 4
        for s in shape[1:]:
            n *= s
        if at is None:
            at = top[0]
            top[0] += (n + 31) // 32 * 32
        return nc.alloc_sbuf_tensor_at(name, shape, dt, offset=at)

    RAW = [place(f"raw{i}", [P, NSUB, 256]) for i in range(NRAW)]
    WH = [place(f"wh{i}", [P, NSUB, 256], F32R) for i in range(NHL)]
    WL = [place(f"wl{i}", [P, NSUB, 256], F32R) for i in range(NHL)]
    at_ah = top[0]
    AHt = place("AHt", [P, 16, 512], F32R)
    at_ch = top[0]
    CHt = place("CHt", [P, 16, 512], F32R)
    at_big = top[0]
    BIGt = place("BIGt", [P, 22, 512], F32R)
    H = place("H", [P, 16, T])
    M9 = place("M9", [P, len(MATS), P])
    CV = place("CV", [P, NVEC])
    RB = [place("RB0", [P, T + 2]), place("RB1", [P, T + 2])]
    SQA = place("SQA", [P, 2, T])
    at_z = top[0]
    Z = [place("Z0", [P, 2, 286]), place("Z1", [P, 2, 286])]
    TA = place("TA", [P, 2, T])
    TB = place("TB", [P, 2, T])
    TC = place("TC", [P, 2, T])
    ROW = place("ROW", [P, 80])
    NAT = place("NAT", [P, 8, 2, 32])
    at_nat = top[0] - 2048
    W2 = nc.alloc_sbuf_tensor_at("W2C", [64, 2, 64], F32, offset=at_nat)
    GAT = nc.alloc_sbuf_tensor_at("GAT", [P, 2, 48], F32, offset=at_nat + 1024)
    CBI = place("CBI", [P, 30, 16])
    SM = place("SM", [P, 64])
    G12 = place("G12", [P, 16])
    assert top[0] <= 229368, top[0]

    XS = place("XS", [P, 16, T], at=at_ch)
    MG = place("MG", [P, 16, T], at=at_ch + 16384)
    QT = place("QT", [P, 8, T], at=at_ch + 16384)
    KDU = place("KDU", [P, 4, T], at=at_ch + 24576)
    VN = place("VN", [P, 2, T], at=at_ch + 28672)
    KT1 = place("KT1", [P, 2, T], at=at_ch + 30720)
    sc = at_big + 16384
    BCT = place("BCT", [P, 8, T], at=sc)
    COS = place("COS", [P, T], at=sc + 8192)
    SIN = place("SIN", [P, T], at=sc + 9216)
    MK1 = place("MK1", [P, 384], at=sc + 10240)
    SX1 = [place("SX1a", [P, 2, 384], at=sc + 12288), place("SX1b", [P, 2, 384], at=sc + 18432)]
    PT1 = [place("PT1a", [P, 2, 384], at=sc + 15360), place("PT1b", [P, 2, 384], at=sc + 21504)]
    RO = place("RO", [P, 2, 2, T], at=sc + 18432)
    PI = place("PI", [P, T], I32, at=sc + 22528)
    XD = place("XD", [P, 2, 512], at=sc + 8192)
    XDS = place("XDS", [P, 512], at=sc + 12288)
    STG = place("STG", [P, 512], at=sc + 14336)
    BNC = place("BNC", [P, 3, P], at=sc + 16384)
    DEC = [place(f"DEC{i}", [P, 4, P], at=sc + 17920 + 2048 * i) for i in range(2)]
    CXE = [place(f"CXE{i}", [P, 4, P], at=sc + 22016 + 2048 * i) for i in range(2)]
    ECS = place("ECS", [P, 4, P], at=sc + 26112)
    C33 = place("C33", [33, 400], at=at_big)
    OHC = place("OHC", [33, 3840], at=sc + 12288)
    RV = place("RV", [16, 384], at=at_big + 2048)
    BM = place("BM", [P, 16, T], at=at_ch)
    Q2 = place("Q2", [P, 8, T], at=at_ch + 16384)
    KD2 = place("KD2", [P, 2, 4, T], at=at_ch + 24576)
    bg = at_big + 32768
    VN2 = place("VN2", [P, 2, 2, T], at=bg)
    VC = place("VC", [15, T], at=bg + 4096)
    KDC = place("KDC", [P, 4, 15], at=bg + 5120)
    SX2 = [place("SX2a", [P, 2, 384], at=bg + 5376), place("SX2b", [P, 2, 384], at=at_z)]
    PT2 = [place("PT2a", [P, 2, 384], at=bg + 8448), place("PT2b", [P, 2, 384], at=at_z + 4576)]
    SCM = [place("SCMa", [P, 2, 2, 15], at=bg + 11520), place("SCMb", [P, 2, 2, 15], at=at_z + 3072)]
    BLK = place("BLK", [P, 32, 30], at=bg + 5376)
    KTC = place("KTC", [P, 2, T], at=bg + 9216)
    PSC = place("PSC", [P, 2, 32], at=bg + 11264)
    GCM = place("GCM", [64, 60], at=bg + 11776)
    GTM = place("GTM", [64, 60], at=bg + 12032)
    W1 = [place("W1K", [P, 32, 64], at=at_ah), place("W1V", [P, 32, 64], at=at_ah + 8192)]
    
    BMR = place("BMR", [P, 16, T], at=at_ah + 16384)
    CC = [place(f"CC{i}", [P, T], at=at_ah + (8 + i) * 2048 + 1024) for i in range(8)]
    PPT = place("PPT", [P, 2, T], at=at_ch)
    PHL = place("PHL", [P, 2, 512], F32R, at=at_ch + 2048)
    PR = place("PR", [P, 16, T], at=at_ch + 8192)

    PS = nc.alloc_psum_tensor("PS", [P, 8, 512], F32)
    scratch = nc.dram_tensor("bias_rows", [16, 384], F32).ap()

    def mat(n):
        return M9[:, MATS.index(n), :]

    def vec(n, i=0, w=1):
        o = VOFF[n][0] + i
        return CV[:, o:o + w]

    def pe(fn, *w, inc=False):
        return Q.put("pe", fn, w, "pe" if inc else None)

    def act(fn, *w):
        return Q.put("act", fn, (*w, ("act", Q.count["act"] + 1 - LAG)), "act")

    def dve(fn, *w):
        return Q.put("dve", fn, (*w, ("dve", Q.count["dve"] + 1 - LAG)), "dve")

    def pool(fn, *w):
        return Q.put("pool", fn, w, "pool")

    def load(eng, name, dst, src, *w):
        return Q.put(eng, lambda e: e.dma_start(dst, src), w, name, 16)

    def mm(o, l, r, start=True, stop=True):
        return lambda e: e.matmul(o, l, r, start=start, stop=stop, skip_group_check=True)

    def tr(o, i, ident):
        return lambda e: e.transpose(o, i, ident)

    def tt(o, x, y, op):
        return lambda e: e.tensor_tensor(o, x, y, op)

    def ts(o, x, s1, s2, o0, o1=None):
        if o1 is None:
            return lambda e: e.tensor_scalar(o, x, s1, None, o0)
        return lambda e: e.tensor_scalar(o, x, s1, s2, o0, o1)

    def stt(o, x, s, y, o0, o1):
        return lambda e: e.scalar_tensor_tensor(out=o, in0=x, scalar=s, in1=y, op0=o0, op1=o1)

    def af(o, x, f, **k):
        return lambda e: e.activation(o, x, f, **k)

    def cp(o, x):
        return lambda e: e.tensor_copy(o, x)

    ADD, SUB, MUL, MAX, MIN = ALU.add, ALU.subtract, ALU.mult, ALU.max, ALU.min

    def two(ap):
        return ap.unsqueeze(1).broadcast_to([ap.shape[0], 2, ap.shape[1]])

    def last(ap, n):
        return ap.unsqueeze(ap.ndim).broadcast_to(list(ap.shape) + [n])

    def bank(b):
        return PS[:, b, :].rearrange("p (m t) -> p m t", m=2)

    free = {b: None for b in range(8)}
    rd = {}

    def f32(ap):
        return ap.bitcast(F32)

    def split_to(dst, k, v, tok, scale=1.0, *w):
        hi = act(af(dst.hi(k), v, ACT.Copy, scale=scale), tok, *w)
        lo = dve(stt(dst.lo(k), v, scale, f32(dst.hi(k)), MUL, SUB), hi, tok, *w)
        dst.ready[k] = lo
        return lo

    units = []

    def unit(w, row0, nk, c0, rhs, evac, nc_=256, natural=False, gens=(), before=None, mid=None,
             banks=(0, 1, 2), pace=1):
        units.append(dict(w=w, row0=row0, nk=nk, c0=c0, rhs=rhs, evac=evac, nc=nc_, nat=natural,
                          gens=list(gens), before=before, mid=mid, banks=banks, pace=pace))

    def run_stream(start):
        subs = []
        for u in units:
            k = 0
            while k < u["nk"]:
                n = min(NSUB, u["nk"] - k)
                subs.append((u, k, n))
                k += n
        hilo = {}
        rawfree = {}
        pesub = {}

        def fetch(s):
            u, k, n = subs[s]
            r0 = u["row0"] + k * P
            src = u["w"][r0:r0 + n * P, u["c0"]:u["c0"] + u["nc"]].rearrange("(t p) n -> p t n", p=P)
            tok = load("sp", f"w{s % NRAW}", RAW[s % NRAW][:, 0:n, 0:u["nc"]], src, rawfree.get(s - NRAW))
            hilo[s] = tok

        def split(s):
            u, k, n = subs[s]
            tok = hilo[s]
            raw = RAW[s % NRAW][:, 0:n, 0:u["nc"]]
            hi = WH[s % NHL][:, 0:n, 0:u["nc"]]
            lo = WL[s % NHL][:, 0:n, 0:u["nc"]]
            h = act(af(hi, raw, ACT.Copy), tok, pesub.get(s - NHL))
            d = dve(tt(lo, raw, f32(hi), SUB), tok, h)
            rawfree[s] = d
            hilo[s] = d

        nf = ns = 0
        gb = 0
        slot = 0
        for s in range(min(NRAW, len(subs))):
            fetch(s)
        nf = NRAW
        for s in range(LEAD + 1):
            next(start)
            split(s)
            ns += 1
        for _ in start:
            pass
        for s, (u, k, n) in enumerate(subs):
            while nf < len(subs) and nf - NRAW < ns:
                fetch(nf)
                nf += 1
            while ns < len(subs) and ns <= s + LEAD:
                split(ns)
                ns += 1
                if nf < len(subs) and nf - NRAW < ns:
                    fetch(nf)
                    nf += 1
            if k == 0:
                if u["before"]:
                    u["before"]()
                b = u["banks"][gb % len(u["banks"])]
                gb += 1
                u["bank"] = b
            b = u["bank"]
            rhs = u["rhs"]
            w = [hilo[s], free[b] if k == 0 else None]
            hi, lo = WH[s % NHL], WL[s % NHL]
            tok = None
            for t in range(n):
                kt = k + t
                w.append(rhs.ready[kt])
                firstk, lastk = kt == 0, kt == u["nk"] - 1
                if u["nat"]:
                    nco = u["nc"]
                    for bb in range(2):
                        o = PS[:, b, bb * nco:(bb + 1) * nco]
                        xh = rhs.hi(kt)[:, bb * P:(bb + 1) * P]
                        xl = rhs.lo(kt)[:, bb * P:(bb + 1) * P]
                        pe(mm(o, xh, hi[:, t, 0:nco], firstk and bb == 0, False), *w)
                        w = []
                        pe(mm(o, xl, hi[:, t, 0:nco], False, False))
                        fin = t == n - 1 and bb == 1
                        tok = pe(mm(o, xh, lo[:, t, 0:nco], False, lastk), inc=fin)
                else:
                    for m in range(2):
                        o = PS[:, b, m * T:(m + 1) * T]
                        wh, wl = hi[:, t, m * P:(m + 1) * P], lo[:, t, m * P:(m + 1) * P]
                        pe(mm(o, wh, rhs.hi(kt), firstk and m == 0, False), *w)
                        w = []
                        pe(mm(o, wh, rhs.lo(kt), False, False))
                        fin = t == n - 1 and m == 1
                        tok = pe(mm(o, wl, rhs.hi(kt), False, lastk), inc=fin)
            pesub[s] = tok
            if k + n == u["nk"]:
                rhs.read = tok
                if u["mid"]:
                    u["mid"]()
                free[b] = u["evac"](b, tok)
                side.extend(u["gens"])
            slot += 1
            if slot % u["pace"] == 0:
                side.step()

    side = Side()

    def drain(_=None):
        side.drain()

    class Norm:

        def __init__(self, i, n, eps):
            self.i, self.n, self.eps = i, n, eps
            self.tok = None
            self.first = True

        def add(self, src, tok, *w):
            s = act(af(TB[:, :, :], src, ACT.Square), tok, rd.get("TB"), *w)
            if self.first:
                t = dve(cp(SQA[:, :, :], TB[:, :, :]), s, rd.get("SQA"))
                self.first = False
            else:
                t = dve(tt(SQA[:, :, :], SQA[:, :, :], TB[:, :, :], ADD), s, self.last)
            rd["TB"] = t
            self.last = t

        def finish(self, b=7):
            o = PS[:, b, :]
            pe(mm(o[:, 0:T], mat("ones"), SQA[:, 0, :], True, False), self.last, free[b], cmt)
            pe(mm(o[:, 0:T], mat("ones"), SQA[:, 1, :], False, True))
            for c in range(2):
                pe(mm(o[:, T + c:T + c + 1], SQA[:, 0, c * P:(c + 1) * P], mat("ones")[:, 0:1], False, False))
                t = pe(mm(o[:, T + c:T + c + 1], SQA[:, 1, c * P:(c + 1) * P], mat("ones")[:, 0:1], False, True),
                       inc=True)
            rd["SQA"] = t
            r = RB[self.i]
            v = dve(ts(r[:, :], o[:, 0:T + 2], 1.0 / self.n, self.eps, MUL, ADD), t)
            free[b] = v
            v = act(af(r[:, :], r[:, :], ACT.Sqrt), v)
            self.tok = dve(lambda e: e.reciprocal(r[:, :], r[:, :]), v)
            return self.tok

        def rb(self):
            return RB[self.i][:, 0:T]

        def rn(self, c):
            return RB[self.i][:, T + c:T + c + 1]

    nload = ["x0", "x1", "x2", "x3"]
    cvt = load("act", "cv", CV[:, :], a["vecs"])
    xts = []
    for i in range(4):
        src = a["xT"][512 * i:512 * (i + 1), :].rearrange("(t p) n -> p t n", p=P)
        xts.append(load("sp" if i % 2 == 0 else "act", nload[i], H[:, 4 * i:4 * i + 4, :], src))
    cmt = load("act", "cm", M9[:, :, :].rearrange("p a b -> p (a b)"), a["mats"])
    post = load("act", "pos", PI[:, :], a["positions"].partition_broadcast(P))
    rowt = load("act", "row", ROW[:, :], a["rows"].partition_broadcast(P))
    mkt = load("act", "mk", MK1[:, :], a["mask1"])
    c33t = load("act", "c33", C33[:, :], a["c33"])
    pads = {}

    def clear_pads(*w):
        for i in range(2):
            pads[i] = pool(lambda e, i=i: e.memset(Z[i][:, :, 0:30], 0.0), *w)

    clear_pads()
    sinks, dtb, alog = ROW[:, 0:16], ROW[:, 16:48], ROW[:, 48:80]
    NSK = SM[:, 0:16]
    U1 = Acts(AHt, 0, 16)
    N1 = Norm(0, D, 1e-6)
    st1 = {"q": [None] * 4, "kd": [None] * 4, "attn": None}

    def start():
        for i in range(4):
            for k in range(4 * i, 4 * i + 4):
                w0 = act(af(U1.hi(k), H[:, k, :], ACT.Copy, scale=vec("g_mix", k)), cvt, xts[i])
                U1.ready[k] = dve(stt(U1.lo(k), H[:, k, :], vec("g_mix", k), f32(U1.hi(k)), MUL, SUB), w0, cvt,
                                  xts[i])
            yield
        for t in range(8):
            N1.add(H[:, 2 * t:2 * t + 2, :], xts[t // 2])
        ang, kk, r0 = RO[:, 0, 0, :], RO[:, 0, 1, :], RO[:, 1, 0, :]
        v = dve(cp(ang, PI[:, :]), post)
        v = dve(ts(ang, ang, vec("invf"), None, MUL), v, cvt)
        BIGM = 12582912.0
        v = dve(ts(kk, ang, float(np.float32(1 / (2 * np.pi))), BIGM, MUL, ADD), v)
        v = dve(ts(kk, kk, -BIGM, None, ADD), v)
        c1, c2 = 6.25, 0.033203125
        c3 = float(np.float32(np.round((2 * np.pi - c1 - c2) * 2 ** 27) / 2 ** 27))
        c4 = float(np.float32(2 * np.pi - c1 - c2 - c3))
        src = ang
        for c in (c1, c2, c3, c4):
            v = dve(stt(r0, kk, -c, src, MUL, ADD), v)
            src = r0
        lim = 3.1415925
        v = dve(ts(r0, r0, lim, -lim, MIN, MAX), v)
        s1 = act(af(SIN[:, :], r0, ACT.Sin), v)
        v = dve(ts(kk, r0, -1.0, None, MUL), v)
        v = dve(tt(kk, kk, r0, MAX), v)
        v = dve(ts(kk, kk, -1.0, float(np.float32(np.pi / 2)), MUL, ADD), v)
        st1["trig"] = act(af(COS[:, :], kk, ACT.Sin), v, s1)
        st1["oh"] = load("pool", "ohc", OHC[:, :], a["ohc"], st1["trig"])
        st1["nsk"] = dve(ts(NSK, sinks, -1.0, None, MUL), rowt)
        st1["aex"] = act(af(alog, alog, ACT.Exp), rowt)
        st1["g12"] = dve(tt(G12[:, :], vec("g_fin", 0, 16), vec("gm2", 0, 16), MUL), cvt)

    def biases():
        bt = pe(mm(PS[0:16, 6, 0:384], C33[:, 384:400], C33[:, 0:384]), c33t, free[6], inc=True)
        for i in range(30):
            ct = pe(mm(PS[:, 5, i * 16:(i + 1) * 16], OHC[:, i * P:(i + 1) * P], C33[:, 384:400]), st1["oh"], free[5],
                    inc=i == 29)
        rd["OHC"] = ct
        yield
        rv = dve(cp(RV[:, :], PS[0:16, 6, 0:384]), bt)
        free[6] = rv
        st1["bmw"] = load("pool", "bmw", scratch, RV[:, :], rv)
        st1["cbi"] = free[5] = dve(cp(CBI[:, :, :].rearrange("p a b -> p (a b)"), PS[:, 5, 0:480]), ct)
        yield

    w_in = a["w_in"]

    def ev_q(i):
        def f(b, tok):
            o = QT[:, 2 * i:2 * i + 2, :]
            v = dve(stt(o, bank(b), 0.125, two(N1.rb()), MUL, MUL), tok, N1.tok)
            st1["q"][i] = v
            return v
        return f

    def rope_q(i):
        o = QT[:, 2 * i:2 * i + 2, :]
        b = 6
        pe(mm(PS[:, b, 0:T], mat("rot"), QT[:, 2 * i, :]), st1["q"][i], free[b], cmt)
        tok = pe(mm(PS[:, b, T:512], mat("rot"), QT[:, 2 * i + 1, :]), inc=True)
        yield
        x = RO[:, 0, :, :]
        v = dve(tt(x, bank(b), two(SIN[:, :]), MUL), tok, st1["trig"], rd["OHC"])
        free[b] = v
        y = dve(tt(o, o, two(COS[:, :]), MUL))
        st1["q"][i] = dve(tt(o, o, x, ADD), y)
        yield

    def ev_k(b, tok):
        v = dve(tt(KT1[:, :, :], bank(b), two(N1.rb()), MUL), tok, N1.tok)
        st1["k"] = v
        return v

    def rope_k(t):
        for b, n in ((5, "dup"), (6, "rdup")):
            for hp in range(2):
                tok = pe(mm(PS[:, b, hp * T:(hp + 1) * T], mat(f"{n}{hp}"), KT1[:, t, :]), st1["k"], free[b], inc=True)
        yield
        x, y = RO[:, 0, :, :], RO[:, 1, :, :]
        v1 = dve(tt(x, bank(5), two(COS[:, :]), MUL), tok, st1["trig"])
        v2 = dve(tt(y, bank(6), two(SIN[:, :]), MUL), tok)
        free[5], free[6] = v1, v2
        v = dve(tt(KDU[:, 2 * t:2 * t + 2, :], x, y, ADD), v2)
        st1["kd"][2 * t] = st1["kd"][2 * t + 1] = v
        yield

    def ev_v(b, tok):
        for c in range(2):
            v = act(af(VN[:, c, :], PS[:, b, c * T:(c + 1) * T], ACT.Copy, scale=N1.rn(c)), tok, N1.tok)
        st1["v"] = v
        return v

    AT = Acts(BIGt, 0, 8)

    def attn1(t):
        j = t // 2
        u = t % 2
        S0, SX, PT = (3, 6)[u], SX1[u], PT1[u]
        kx, kp = f"SX{u}", f"PT{u}"
        for hh in range(2):
            q, k = QT[hh * 64:hh * 64 + 64, t, :], KDU[hh * 64:hh * 64 + 64, j, :]
            pe(mm(PS[:, S0 + hh, 0:128], q[:, 0:128], k[:, 0:128]), st1["q"][t // 2], st1["kd"][j], free[S0], free[S0 + 1])
            tok = pe(mm(PS[:, S0 + hh, 128:384], q[:, 128:256], k[:, 0:256]), inc=True)
        v = dve(tt(SX[:, :, :], PS[:, S0:S0 + 2, 0:384], two(MK1[:, :]), ADD), tok, mkt, rd.get(kx))
        free[S0] = free[S0 + 1] = v
        NM, DEN, ES, RC = (SM[:, 16 + 16 * u + 4 * i:20 + 16 * u + 4 * i].rearrange("p (h b) -> p h b", b=2) for i in range(4))
        for b, c0, c1_ in ((0, 0, 128), (1, 128, 384)):
            v = dve(lambda e, b=b, c0=c0, c1_=c1_: e.tensor_reduce(NM[:, :, b], SX[:, :, c0:c1_], AXX, MAX,
                                                                 negate=True), v)
        v = dve(tt(NM, NM, last(NSK[:, 2 * t:2 * t + 2], 2), MIN), v, st1["nsk"])
        es = dve(tt(ES, NM, last(sinks[:, 2 * t:2 * t + 2], 2), ADD), v)
        for hh in range(2):
            for b, c0, c1_ in ((0, 0, 128), (1, 128, 384)):
                x = SX[:, hh, c0:c1_]
                s = act(af(x, x, ACT.Exp, bias=NM[:, hh, b:b + 1], accum_out=DEN[:, hh, b:b + 1]), v)
        s = act(af(ES, ES, ACT.Exp), es)
        v = dve(tt(DEN, DEN, ES, ADD), s)
        v = dve(lambda e: e.reciprocal(RC, DEN), v)
        for hh in range(2):
            for b, c0, c1_ in ((0, 0, 128), (1, 128, 384)):
                x = SX[:, hh, c0:c1_]
                s = act(af(x, x, ACT.Copy, scale=RC[:, hh, b:b + 1]), v)
        yield
        for hh in range(2):
            for c in range(3):
                tok = pe(tr(PS[:, S0 + hh, c * 128:(c + 1) * 128], SX[:, hh, c * 128:(c + 1) * 128], mat("ident")),
                         s, free[S0 + hh], inc=True)
        rd[kx] = tok
        s = act(af(PT[:, :, :], PS[:, S0:S0 + 2, 0:384], ACT.Copy), tok, rd.get(kp))
        free[S0] = free[S0 + 1] = s
        yield
        for hh in range(2):
            o = PS[hh * 64:hh * 64 + 64, 5, :]
            vv = [VN[:, c, j * 64:(j + 1) * 64] for c in range(2)]
            pe(mm(o[:, 0:128], vv[0], PT[:, hh, 0:128]), s, free[5], st1["v"])
            pe(mm(o[:, 128:256], vv[0], PT[:, hh, 128:256], True, False))
            tok = pe(mm(o[:, 128:256], vv[1], PT[:, hh, 256:384], False, True), inc=True)
        rd[kp] = tok
        free[5] = split_to(AT, t, PS[:, 5, 0:T], tok, 1.0, st1["bmw"])
        st1["attn"] = tok
        yield

    def n_(i):
        return NAT[:, i, :, :]

    DT, AN, NCS, DSE = n_(0), n_(1), n_(2), n_(3)[:, 0, :]

    def ev_dt(b, tok):
        x, ax, e_, s_, q_, w_ = DT, n_(4), n_(5), n_(6), n_(7), AN
        for c in range(2):
            v = dve(stt(x[:, c, :], PS[:, b, c * 32:(c + 1) * 32], N1.rn(c), dtb, MUL, ADD), tok, N1.tok, rowt)
        fr = v
        v = dve(ts(ax, x, -1.0, None, MUL), v)
        v = dve(tt(ax, ax, x, MAX), v)
        s = act(af(e_, ax, ACT.Exp, scale=-1.0), v)
        v = dve(ts(s_, e_, 2.0, None, ADD), s)
        v = dve(lambda e: e.reciprocal(s_, s_), v)
        v = dve(tt(s_, s_, e_, MUL), v)
        v = dve(tt(q_, s_, s_, MUL), v)
        v = dve(ts(w_, q_, 1.0 / 17, 1.0 / 15, MUL, ADD), v)
        for c in (13, 11, 9, 7, 5, 3, 1):
            v = dve(tt(w_, w_, q_, MUL), v)
            v = dve(ts(w_, w_, 1.0 / c, None, ADD), v)
        v = dve(tt(w_, w_, s_, MUL), v)
        v = dve(ts(x, x, 0.0, None, MAX), v)
        v = dve(stt(x, w_, 2.0, x, MUL, ADD), v)
        v = dve(stt(AN, x, -1.0, alog.unsqueeze(1).broadcast_to([P, 2, 32]), MUL, MUL), v, st1["aex"])
        st1["dt"] = v
        return fr

    def cums():
        o = PS[:, 7, :]
        for c in range(2):
            pe(mm(o[:, c * 32:(c + 1) * 32], mat("triu"), AN[:, c, :]), st1["dt"], free[7])
        tok = pe(mm(o[:, 64:96], mat("ones"), AN[:, 0, :]), inc=True)
        yield
        v = dve(ts(NCS, o[:, 0:64].rearrange("p (c h) -> p c h", c=2), -1.0, None, MUL), tok)
        v = dve(tt(DSE, o[:, 64:96], NCS[:, 0, :], ADD), v)
        free[7] = v
        st1["cs"] = act(af(DSE, DSE, ACT.Exp), v)
        yield

    xbc_ready = [None] * 12

    def ev_xbc(i):
        def f(b, tok):
            z = Z[i % 2]
            fr = v = dve(tt(z[:, :, 30:286], bank(b), two(N1.rb()), MUL), tok, N1.tok, pads[i % 2], rd.get(f"Z{i % 2}"))
            for k in range(4):
                w = v
                for m in range(2):
                    c = 2 * i + m
                    x = z[:, m, 27 + k:27 + k + T]
                    if k == 0:
                        v = dve(ts(TA[:, m, :], x, vec("cw", 4 * c), vec("cb", c), MUL, ADD), w, rd.get("TA"))
                    else:
                        v = dve(stt(TA[:, m, :], x, vec("cw", 4 * c + k), TA[:, m, :], MUL, ADD), w)
            s = act(af(TB[:, :, :], TA[:, :, :], ACT.Tanh, scale=0.5), v, rd.get("TB"))
            v = dve(stt(TC[:, :, :], TB[:, :, :], 1.0, TA[:, :, :], ADD, MUL), s, rd.get("TC"))
            rd["TB"] = v
            dst = XS[:, 2 * i:2 * i + 2, :] if i < 8 else BCT[:, 2 * (i - 8):2 * (i - 8) + 2, :]
            xbc_ready[i] = rd["TC"] = act(af(dst, TC[:, :, :], ACT.Copy, scale=0.5), v)
            return fr
        return f

    y_ready = [None] * 8

    def ssd(g):
        rdy = [xbc_ready[2 * g], xbc_ready[2 * g + 1], xbc_ready[8 + g // 2], xbc_ready[10 + g // 2], st1["cs"]]
        Bt, Ct = BCT[:, g, :], BCT[:, 4 + g, :]
        for c in range(2):
            for i in range(4):
                tok = pe(tr(PS[:, 3 + c, i * P:(i + 1) * P], XS[:, 4 * g + i, c * P:(c + 1) * P], mat("ident")),
                         *rdy, free[3], free[4], inc=True)
        pe(tr(PS[:, 5, 0:P], Bt[:, 0:P], mat("ident")), free[5])
        for c in range(2):
            tk2 = pe(mm(PS[:, 5, (1 + c) * P:(2 + c) * P], Bt[:, c * P:(c + 1) * P], Ct[:, c * P:(c + 1) * P]),
                     inc=True)
        s0 = act(af(BNC[:, :, :].rearrange("p a b -> p (a b)"), PS[:, 5, 0:384], ACT.Copy), tk2, st1["attn"],
                 rd.get("BNC"))
        free[5] = s0
        for c in range(2):
            v = dve(tt(XD[:, c, :].rearrange("p (h d) -> p h d", d=64),
                       PS[:, 3 + c, :].rearrange("p (h d) -> p h d", d=64),
                       last(DT[:, c, 8 * g:8 * g + 8], 64), MUL), tok, st1["attn"], rd.get("XD"))
        free[3] = free[4] = v
        xd = v
        xds = dve(tt(XDS[:, :].rearrange("p (h d) -> p h d", d=64), XD[:, 0, :].rearrange("p (h d) -> p h d", d=64),
                     last(DSE[:, 8 * g:8 * g + 8], 64), MUL), v)
        yield
        tok = pe(mm(PS[:, 5, :], BNC[:, 0, :], XDS[:, :]), xds, s0, inc=True)
        stt_ = act(af(STG[:, :], PS[:, 5, :], ACT.Copy), tok, rd.get("STG"))
        free[5] = stt_

        def decays(n):
            c, hf = n // 2, n % 2
            h0 = 8 * g + 4 * hf
            bb = 3 + hf
            dk = DEC[n % 2]
            for i in range(4):
                tok = pe(mm(PS[:, bb, i * P:(i + 1) * P], AN[:, c, h0 + i:h0 + i + 1].broadcast_to([P, P]),
                            mat("triu")), free[bb], inc=True)
            bv = PS[:, bb, :].rearrange("p (i l) -> p i l", l=P)
            v = dve(tt(dk[:, :, :], bv, mat("negT").unsqueeze(1).broadcast_to([P, 4, P]), ADD), tok,
                    rd.get(f"DEC{n % 2}"))
            free[bb] = v
            for i in range(4):
                s = act(af(dk[:, i, :], dk[:, i, :], ACT.Exp, bias=NCS[:, c, h0 + i:h0 + i + 1]), v)
            if c == 1:
                e = act(af(ECS[:, :, :], bv, ACT.Exp), v, rd.get("ECS"))
                free[bb] = e
            mt = dve(tt(dk[:, :, :], dk[:, :, :], BNC[:, 1 + c, :].unsqueeze(1).broadcast_to([P, 4, P]), MUL), s, s0)
            if c == 1:
                mt = rd["ECS"] = dve(tt(CXE[hf][:, :, :], ECS[:, :, :],
                                        Ct[:, P:2 * P].unsqueeze(1).broadcast_to([P, 4, P]), MUL), e,
                                     rd.get(f"CXE{hf}"))
            return mt

        mt = decays(0)
        yield
        for n in range(4):
            c, hf = n // 2, n % 2
            mt, now = (decays(n + 1) if n < 3 else None), mt
            for i in range(4):
                hh = 4 * hf + i
                o = PS[(i % 2) * 64:(i % 2) * 64 + 64, 6, (i // 2) * P:(i // 2 + 1) * P]
                tok = pe(mm(o, XD[:, c, hh * 64:(hh + 1) * 64], DEC[n % 2][:, i, :], True, c == 0), now, free[6],
                         stt_, inc=True)
                if c == 1:
                    tok = pe(mm(o, STG[:, hh * 64:(hh + 1) * 64], CXE[hf][:, i, :], False, True), inc=True)
            rd[f"DEC{n % 2}"] = tok
            if c == 1:
                rd[f"CXE{hf}"] = tok
            for i in range(2):
                tile = 4 * g + 2 * hf + i
                y = XS[:, tile, c * P:(c + 1) * P]
                v = dve(stt(y, y, vec("dsk", tile), PS[:, 6, i * P:(i + 1) * P], MUL, ADD), tok)
            free[6] = v
            if c == 1:
                y_ready[2 * g + hf] = v
            yield
        rd["XD"] = rd["STG"] = rd["BNC"] = tok

    for i in range(4):
        unit(w_in, 0, 16, 256 * i, U1, ev_q(i), mid=N1.finish if i == 0 else None,
             gens=([biases()] if i == 0 else []) + [rope_q(i)])
    unit(w_in, 0, 16, 1024, U1, ev_k, gens=[rope_k(0), rope_k(1)])
    unit(w_in, 0, 16, 1280, U1, ev_v, natural=True, gens=[2] + [attn1(t) for t in range(8)] + [1])
    unit(w_in, 0, 16, 6656, U1, ev_dt, nc_=32, natural=True, gens=[cums()], pace=2)
    for i in range(12):
        unit(w_in, 0, 16, 3584 + 256 * i, U1, ev_xbc(i), pace=3)

    mg = [None] * 8

    def ev_ga(i):
        def f(b, tok):
            v = dve(tt(TA[:, :, :], bank(b), two(N1.rb()), MUL), tok, rd.get("TA"))
            rd["TA"] = s = act(af(MG[:, 2 * i:2 * i + 2, :], TA[:, :, :], ACT.Tanh, scale=0.5), v)
            mg[i] = s
            return v
        return f

    def ev_oa(i):
        def f(b, tok):
            o = MG[:, 2 * i:2 * i + 2, :]
            mg[i] = dve(stt(o, o, 1.0, bank(b), ADD, MUL), tok, mg[i])
            return mg[i]
        return f

    for i in range(8):
        unit(w_in, 0, 16, 6688 + 256 * i, U1, ev_ga(i), before=drain if i == 0 else None,
             gens=[ssd(g) for g in range(4)] if i == 0 else (), pace=2)
        unit(a["w_attn_br"], 0, 8, 256 * i, AT, ev_oa(i), pace=2)

    YH = Acts(BIGt, 0, 16)
    N2 = Norm(1, D, 1e-5)

    def ev_z(i):
        def f(b, tok):
            z = Z[i % 2][:, :, 30:286]
            fr = v = dve(tt(z, bank(b), two(N1.rb()), MUL), tok)
            s = act(af(TA[:, :, :], z, ACT.Tanh, scale=0.5), v, rd.get("TA"))
            v = dve(stt(TA[:, :, :], TA[:, :, :], 1.0, z, ADD, MUL), s)
            v = dve(stt(TC[:, :, :], TA[:, :, :], 0.5, XS[:, 2 * i:2 * i + 2, :], MUL, MUL), v, rd.get("TC"),
                    y_ready[i])
            N2.add(TC[:, :, :], v)
            for m in range(2):
                k = 2 * i + m
                rd["TC"] = act(af(YH.hi(k), TC[:, m, :], ACT.Copy, scale=vec("g_ssd", k)), v, AT.read, st1["ssd"])
                YH.ready[k] = dve(stt(YH.lo(k), TC[:, m, :], vec("g_ssd", k), f32(YH.hi(k)), MUL, SUB), rd["TC"],
                                  AT.read, st1["ssd"])
            return fr
        return f

    def before_z():
        drain()
        st1["ssd"] = rd["XD"]

    for i in range(8):
        unit(w_in, 0, 16, 1536 + 256 * i, U1, ev_z(i), before=before_z if i == 0 else None)
    GSB = XS
    gs = [None] * 8

    def ev_gs(i):
        def f(b, tok):
            v = dve(tt(TA[:, :, :], bank(b), two(N1.rb()), MUL), tok, rd.get("TA"))
            rd["TA"] = gs[i] = act(af(GSB[:, 2 * i:2 * i + 2, :], TA[:, :, :], ACT.Tanh, scale=0.5), v)
            return v
        return f

    for i in range(8):
        unit(w_in, 0, 16, 8736 + 256 * i, U1, ev_gs(i), mid=N2.finish if i == 0 else None)
    MH = Acts(AHt, 0, 16)

    def ev_os(i):
        def f(b, tok):
            s_ = slice(2 * i, 2 * i + 2)
            fr = v = dve(tt(TA[:, :, :], bank(b), two(N2.rb()), MUL), tok, N2.tok, rd.get("TA"))
            v = dve(stt(TA[:, :, :], GSB[:, s_, :], 1.0, TA[:, :, :], ADD, MUL), v, gs[i])
            v = dve(tt(TA[:, :, :], TA[:, :, :], MG[:, s_, :], ADD), v)
            for m in range(2):
                split_to(MH, 2 * i + m, TA[:, m, :], v, 0.5, U1.read)
            rd["TA"] = MH.ready[2 * i + 1]
            return fr
        return f

    for i in range(8):
        unit(a["w_ssd_br"], 0, 16, 256 * i, YH, ev_os(i))

    def ev_h(i, nxt=None, norms=(), prev=lambda: None):
        def f(b, tok):
            h = H[:, 2 * i:2 * i + 2, :]
            fr = v = dve(tt(h, h, bank(b), ADD), tok, rd.get("H"))
            if nxt is not None:
                finish_h(i, v, nxt, norms, prev())
            return fr
        return f

    def finish_h(i, v, nxt, norms, pw):
        h = H[:, 2 * i:2 * i + 2, :]
        dst, gv = nxt
        for m in range(2):
            k = 2 * i + m
            s = act(af(dst.hi(k), H[:, k, :], ACT.Copy, scale=gv(k)), v, pw)
            dst.ready[k] = dve(stt(dst.lo(k), H[:, k, :], gv(k), f32(dst.hi(k)), MUL, SUB), s, pw)
        for n in norms:
            n.add(h, v)

    F1 = Acts(CHt, 0, 16)
    N3 = Norm(0, D, 1e-6)
    for i in range(8):
        unit(a["w_o"], 0, 16, 256 * i, MH, ev_h(i, (F1, lambda k: vec("g_ffn", k)), [N3], lambda: mhw()))

    def mhw():
        return MH.ready[15]

    WIDE = (0, 1, 2, 3, 4)

    def ffn(wg, gcol, wu, ucol, wd, fin, norm, evg, evu, last_h, free0, between=None):
        fr = free0
        for half in range(2):
            A = Acts(BIGt, 0, 22)
            for i in range(11):
                unit(wg, 0, 16, gcol + 256 * (11 * half + i), fin, evg(half, i, A), banks=WIDE,
                     mid=norm.finish if half == 0 and i == 0 else None)
                unit(wu, 0, 16, ucol + 256 * (11 * half + i), fin, evu(half, i, A, fr), banks=WIDE)
            for i in range(8):
                if between and half and i == 3:
                    between()
                unit(wd, 2816 * half, 22, 256 * i, A, last_h(i) if half else ev_h(i), banks=WIDE)
            fr = lambda A=A: A.read
        return A

    def evg1(half, i, A):
        def f(b, tok):
            z = Z[i % 2][:, :, 30:286]
            fr = v = dve(tt(z, bank(b), two(N3.rb()), MUL), tok, N3.tok)
            s = act(af(TA[:, :, :], z, ACT.Tanh, scale=0.5), v, rd.get("TA"))
            rd["g"] = dve(stt(TA[:, :, :], TA[:, :, :], 1.0, z, ADD, MUL), s)
            return fr
        return f

    def evu1(half, i, A, fr_):
        def f(b, tok):
            fr = v = dve(tt(TC[:, :, :], bank(b), two(N3.rb()), MUL), tok, rd.get("TC"), N3.tok)
            v = dve(tt(TC[:, :, :], TC[:, :, :], TA[:, :, :], MUL), v, rd["g"])
            for m in range(2):
                split_to(A, 2 * i + m, TC[:, m, :], v, 0.5, fr_())
            rd["TC"] = A.ready[2 * i + 1]
            return fr
        return f

    P1H = Acts(AHt, 0, 16)
    N4 = Norm(1, D, 1e-6)

    PH = Acts(PHL, 0, 2)
    pr = [None] * 8

    def load_p():
        pt = load("pool", "p", PPT[:, :, :], a["pT"].rearrange("(t p) n -> p t n", p=P), F1.read)
        for k in range(2):
            split_to(PH, k, PPT[:, k, :], pt, 1.0, F1.read)

    def ev_pp(i):
        def f(b, tok):
            pr[i] = act(af(PR[:, 2 * i:2 * i + 2, :], bank(b), ACT.Copy), tok, F1.read)
            return pr[i]
        return f

    def p_units():
        units[-2]["mid"] = load_p
        for i in range(8):
            unit(a["w_ple_proj"], 0, 2, 256 * i, PH, ev_pp(i), banks=WIDE)

    A1 = ffn(a["w_gate"], 0, a["w_up"], 0, a["w_down"], F1, N3, evg1, evu1,
             lambda i: ev_h(i, (P1H, lambda k: vec("g_ple", k)), [N4], lambda: MH.read), lambda: YH.read, p_units)

    U2 = Acts(BIGt, 0, 16)
    N5, N6 = Norm(0, D, 1e-6), Norm(1, D, 1e-6)
    sqb = [None]

    def ev_pg(i):
        def f(b, tok):
            h = H[:, 2 * i:2 * i + 2, :]
            fr = v = dve(tt(TA[:, :, :], bank(b), two(N4.rb()), MUL), tok, N4.tok, rd.get("TA"))
            s = act(af(TA[:, :, :], TA[:, :, :], ACT.Tanh, scale=0.5), v)
            v = dve(stt(TC[:, :, :], TA[:, :, :], 1.0, PR[:, 2 * i:2 * i + 2, :], ADD, MUL), s, pr[i], rd.get("TC"))
            rd["TA"] = v
            v = dve(stt(h, TC[:, :, :], 0.5, h, MUL, ADD), v, rd.get("H"))
            finish_h(i, v, (U2, lambda k: G12[:, k:k + 1]), [], A1.read)
            N5.add(h, v)
            for m in range(2):
                s = act(af(TB[:, m, :], H[:, 2 * i + m, :], ACT.Square, scale=vec("g_fin", 2 * i + m)), v, rd["TB"])
            if i == 0:
                rd["TB"] = sqb[0] = dve(cp(SQB, TB[:, :, :]), s)
            else:
                rd["TB"] = sqb[0] = dve(tt(SQB, SQB, TB[:, :, :], ADD), s, sqb[0])
            return fr
        return f

    SQB = Z[1][:, :, 30:286]
    for i in range(8):
        unit(a["w_ple_gate"], 0, 16, 256 * i, P1H, ev_pg(i), mid=N4.finish if i == 0 else None, banks=WIDE)

    st2 = {"q": [None] * 4, "kd": {}, "v": {}}
    RX = RB[0]
    RU = RB[1]

    def join():
        t5 = N5.finish(7)
        o = PS[:, 6, :]
        pe(mm(o[:, 0:T], mat("ones"), SQB[:, 0, :], True, False), sqb[0], free[6])
        pe(mm(o[:, 0:T], mat("ones"), SQB[:, 1, :], False, True))
        for c in range(2):
            pe(mm(o[:, T + c:T + c + 1], SQB[:, 0, c * P:(c + 1) * P], mat("ones")[:, 0:1], False, False))
            t = pe(mm(o[:, T + c:T + c + 1], SQB[:, 1, c * P:(c + 1) * P], mat("ones")[:, 0:1], False, True), inc=True)
        rd["SQB"] = t
        yield
        ta = TA[:, :, :].rearrange("p a b -> p (a b)")[:, 0:T + 2]
        v = dve(tt(ta, RX[:, :], RX[:, :], MUL), t5, rd.get("TA"))
        v = dve(stt(ta, o[:, 0:T + 2], 1.0 / D, ta, MUL, MUL), v, t)
        free[6] = v
        v = dve(ts(ta, ta, 1e-6, None, ADD), v)
        s = act(af(ta, ta, ACT.Sqrt), v)
        v = dve(lambda e: e.reciprocal(ta, ta), s)
        N6.tok = dve(tt(RU[:, :], ta, RX[:, :], MUL), v)
        for k in range(16):
            v = dve(stt(H[:, k, :], H[:, k, :], vec("g_fin", k), RX[:, 0:T], MUL, MUL), t5, U2.ready[15])
        st2["x"] = v
        rd["TA"] = v
        st2["bmr"] = load("pool", "bmr", BMR[:, :, :], bass.AP(scratch.tensor, 0, [[1, P], [384, 16], [1, T]]), st1["bmw"],
                          P1H.read)
        w1 = a["cmp_w1"]
        for kv in range(2):
            src = w1[kv].rearrange("(l d) e -> d l e", d=64)
            for hp in range(2):
                st2[f"w1{kv}"] = load("pool", "w1k" if kv == 0 else "w1v", W1[kv][hp * 64:hp * 64 + 64, :, :], src,
                                      P1H.read)
        st2["w2"] = load("pool", "w2c", W2[:, 0:2, :], a["cmp_w2"].rearrange("k d e -> d k e"), P1H.read)
        yield

    def turn_bias():
        for i in range(4):
            for b in range(2):
                h = 4 * i + 2 * b
                tok = pe(mm(PS[:, 3 + b, :], mat("anti"), BMR[:, h:h + 2, :]), st2["bmr"], free[3 + b], inc=True)
            rd["CC"] = tok
            yield
            for b in range(2):
                h = 4 * i + 2 * b
                s = act(af(BM[:, h:h + 2, :], bank(3 + b), ACT.Copy), tok, st2["x"])
                free[3 + b] = s
        st2["bm"] = s
        yield

    w_in2 = a["w_in_2"]

    def ev_cmp(kv):
        def f(b, tok):
            v = dve(tt(KTC[:, :, :], bank(b), two(N6.rb()), MUL), tok, N6.tok, rd.get("KTC"))
            blk = BLK[:, :, :].rearrange("p l (t n) -> p l t n", t=2)
            pos = a_pos[kv]
            for t in range(2):
                base = KTC[:, t, :]
                fr2 = dve(tt(blk[:, :, t, :],
                             bass.AP(KTC, t * T, [[2 * T, P], [1, 32], [16, 15]]),
                             last(pos, 15), ADD), v, rd.get("BLK"), *st2["pos"])
            rd["BLK_w"] = fr2
            return v
        return f

    a_pos = [None, None]

    def compress(kv):
        bd = BLK[:, :, :]
        for hp in range(2):
            for l in range(32):
                tok = pe(mm(PS[0:64, 3 + hp, 0:30], W1[kv][hp * 64:hp * 64 + 64, l, :],
                            bd[hp * 64:hp * 64 + 64, l, :], l == 0, l == 31),
                         rd["BLK_w"], st2[f"w1{kv}"], free[3], free[4], inc=l == 31)
        rd["BLK"] = rd["KTC"] = tok
        gv = GTM[:, :].rearrange("p (h n) -> p h n", h=2)
        v = dve(cp(gv, PS[0:64, 3:5, 0:30]), tok, rd.get("GTM"))
        free[3] = free[4] = v
        s = act(af(GCM[:, :], GTM[:, :], ACT.Tanh, scale=0.5), v, rd.get("GCM"))
        v = dve(stt(GCM[:, :], GCM[:, :], 1.0, GTM[:, :], ADD, MUL), s)
        v = dve(ts(GCM[:, :], GCM[:, :], 0.5, None, MUL), v)
        yield
        if kv == 0:
            for hh in range(2):
                tok = pe(mm(PS[hh * 64:hh * 64 + 64, 5, 0:60], W2[:, 0, :], GCM[:, :]), v, st2["w2"], free[5], inc=True)
            o = KDC[:, :, :].rearrange("p (t h) n -> p t h n", h=2)
            x = PS[:, 5, 0:60].rearrange("p (h t n) -> p t h n", h=2, t=2)
            for t in range(2):
                v = dve(cp(o[:, t], x[:, t]), tok, rd.get("KDC"))
            st2["kdc"] = free[5] = v
        else:
            for t in range(2):
                for hp in range(2):
                    c = (2 * t + hp) * 64
                    g = GCM[:, hp * 30 + t * 15:hp * 30 + t * 15 + 15]
                    tok = pe(mm(PS[0:15, 5, c:c + 64], g, W2[:, 1, :]), v, free[5], inc=True)
            st2["vc"] = free[5] = dve(cp(VC[:, :], PS[0:15, 5, 0:T]), tok)
        rd["GCM"] = tok
        st2["w1read"] = tok
        yield

    def ev_k2(br):
        def f(b, tok):
            z = Z[br][:, :, 30:286]
            rd["k2"] = dve(tt(z, bank(b), two(N6.rb()), MUL), tok, N6.tok, rd.get("SQB"))
            return rd["k2"]
        return f

    def dup_k2(br):
        z = Z[br][:, :, 30:286]
        for t in range(2):
            b = 5 + t
            for hp in range(2):
                tok = pe(mm(PS[:, b, hp * T:(hp + 1) * T], mat(f"dup{hp}"), z[:, t, :]), rd["k2"], free[b], inc=True)
        rd["SX21"] = tok
        yield
        for t in range(2):
            b = 5 + t
            v = dve(cp(KD2[:, br, 2 * t:2 * t + 2, :], bank(b)), tok, st2["x"])
            free[b] = v
        st2["kd"][br] = v
        yield

    def ev_v2(br):
        def f(b, tok):
            for c in range(2):
                v = act(af(VN2[:, br, c, :], PS[:, b, c * T:(c + 1) * T], ACT.Copy, scale=RU[:, T + c:T + c + 1]),
                        tok, N6.tok, A1.read)
            st2["v"][br] = v
            return v
        return f

    def ev_q2(i):
        def f(b, tok):
            st2["q"][i] = dve(stt(Q2[:, 2 * i:2 * i + 2, :], bank(b), 0.125, two(N6.rb()), MUL, MUL), tok, N6.tok,
                              st2["x"])
            return st2["q"][i]
        return f

    def ev_gate(b, tok):
        for c in range(2):
            v = dve(ts(GAT[:, c, :], PS[:, b, c * 48:(c + 1) * 48], RU[:, T + c:T + c + 1], None, MUL), tok, N6.tok)
        s = act(af(GAT[:, :, :], GAT[:, :, :], ACT.Tanh, scale=0.5), v)
        st2["gate"] = dve(ts(GAT[:, :, :], GAT[:, :, :], 0.5, 0.5, MUL, ADD), s)
        return v

    MX = Acts(AHt, 0, 16)

    def ev_ca(i):
        def f(b, tok):
            rd["ca"] = dve(tt(TC[:, :, :], bank(b), two(N6.rb()), MUL), tok, N6.tok, rd.get("TC"))
            return rd["ca"]
        return f

    cvin = [None] * 4
    SCC = SQA

    def ev_cg(i):
        def f(b, tok):
            z = Z[i % 2]
            fr = v = dve(tt(TA[:, :, :], bank(b), two(N6.rb()), MUL), tok, rd.get("TA"))
            s = act(af(TA[:, :, :], TA[:, :, :], ACT.Tanh, scale=0.5), v)
            v = dve(stt(TC[:, :, :], TA[:, :, :], 1.0, TC[:, :, :], ADD, MUL), s, rd["ca"])
            v = dve(ts(z[:, :, 30:286], TC[:, :, :], 0.5, None, MUL), v, rd.get(f"Z{i % 2}"),
                    rd.get("SQB") if i else None, pads[i % 2])
            rd["TC"] = v
            cvin[i] = v
            return fr
        return f

    def conv31(i):
        z = Z[i % 2]
        v = cvin[i]
        for k in range(31):
            w = v
            for m in range(2):
                c = 2 * i + m
                x = z[:, m, k:k + T]
                o = CC[c][:, :]
                if k == 0:
                    v = dve(ts(o, x, vec("cw2", 31 * c), vec("cb2", c), MUL, ADD), w, P1H.read, rd["CC"])
                else:
                    v = dve(stt(o, x, vec("cw2", 31 * c + k), o, MUL, ADD), w)
            if k % 8 == 7:
                yield
        for m in range(2):
            c = 2 * i + m
            if c == 0:
                v = dve(cp(SCC[:, 0, :], CC[c][:, :]), v, rd.get("SQA"))
            else:
                v = dve(tt(SCC[:, 0, :], SCC[:, 0, :], CC[c][:, :], ADD), v)
        rd["scc"] = v
        yield

    def layer_norm():
        tok = pe(mm(PS[:, 7, 0:T], mat("ones"), SCC[:, 0, :]), rd["scc"], free[7], inc=True)
        yield
        mean = TA[:, 0, :]
        v = dve(ts(mean, PS[:, 7, 0:T], 1.0 / 1024, None, MUL), tok, rd.get("TA"))
        free[7] = v
        for c in range(8):
            x = CC[c][:, :]
            v1 = dve(tt(x, x, mean, SUB), v)
            s = act(af(TB[:, c % 2, :], x, ACT.Square), v1, rd.get("TB"), rd.get(f"TB{c % 2}"))
            if c == 0:
                v2 = dve(cp(SCC[:, 0, :], TB[:, 0, :]), s, tok)
            else:
                v2 = dve(tt(SCC[:, 0, :], SCC[:, 0, :], TB[:, c % 2, :], ADD), s, v2)
            rd[f"TB{c % 2}"] = v2
        tok = pe(mm(PS[:, 7, 0:T], mat("ones"), SCC[:, 0, :]), v2, free[7], inc=True)
        yield
        rs = TA[:, 1, :]
        v = dve(ts(rs, PS[:, 7, 0:T], 1.0 / 1024, 1e-6, MUL, ADD), tok)
        free[7] = v
        s = act(af(rs, rs, ACT.Sqrt), v)
        v0 = dve(lambda e: e.reciprocal(rs, rs), s)
        for c in range(8):
            x = CC[c][:, :]
            z = TC[:, c % 2, :]
            v = dve(tt(x, x, rs, MUL), v0)
            v = dve(ts(x, x, vec("lng", c), vec("lnb", c), MUL, ADD), v)
            s = act(af(TB[:, c % 2, :], x, ACT.Tanh, scale=0.5), v, rd[f"TB{c % 2}"])
            v = dve(stt(z, TB[:, c % 2, :], 1.0, x, ADD, MUL), s, rd.get("TC"), rd.get(f"TC{c % 2}"))
            rd[f"TB{c % 2}"] = v
            rd[f"TC{c % 2}"] = split_to(MX, 8 + c, z, v, 0.5)
        rd["TA"] = rd["TC"] = rd["TB"] = rd["PT21"] = rd["TC1"]
        rd["SQA"] = tok
        yield

    def attn2(t):
        j = t // 2
        u = t % 2
        S0, OB, SX, PT, SC = (3, 6)[u], (5, 2)[u], SX2[u], PT2[u], SCM[u]
        kx, kp, kc = f"SX2{u}", f"PT2{u}", f"SCM{u}"
        NM, DEN, RC = (SM[:, 16 + 16 * u + 4 * i:20 + 16 * u + 4 * i].rearrange("p (h b) -> p h b", b=2) for i in range(3))
        first = [True, True]

        for br in range(2):
            for hh in range(2):
                q, k = Q2[hh * 64:hh * 64 + 64, t, :], KD2[hh * 64:hh * 64 + 64, br, j, :]
                pe(mm(PS[:, S0 + hh, 0:128], q[:, 0:128], k[:, 0:128]), st2["q"][t // 2], st2["kd"][br], free[S0],
                   free[S0 + 1])
                tok = pe(mm(PS[:, S0 + hh, 128:384], q[:, 128:256], k[:, 0:256]), inc=True)
            v = dve(tt(SX[:, :, 0:128], PS[:, S0:S0 + 2, 0:128], BM[:, 2 * t:2 * t + 2, 128:256], ADD), tok, st2["bm"],
                    rd.get(kx), rd.get("BLK"))
            v = dve(tt(SX[:, :, 128:384], PS[:, S0:S0 + 2, 128:384], BM[:, 2 * t:2 * t + 2, :], ADD))
            free[S0] = free[S0 + 1] = v
            for b, c0, c1_ in ((0, 0, 128), (1, 128, 384)):
                v = dve(lambda e, b=b, c0=c0, c1_=c1_: e.tensor_reduce(NM[:, :, b], SX[:, :, c0:c1_], AXX, MAX,
                                                                     negate=True), v)
            for hh in range(2):
                for b, c0, c1_ in ((0, 0, 128), (1, 128, 384)):
                    x = SX[:, hh, c0:c1_]
                    s = act(af(x, x, ACT.Exp, bias=NM[:, hh, b:b + 1], accum_out=DEN[:, hh, b:b + 1]), v)
            v = dve(lambda e: e.reciprocal(RC, DEN), s)
            for hh in range(2):
                v = dve(tt(RC[:, hh, :], RC[:, hh, :], GAT[:, :, 3 * (2 * t + hh) + 1 + br], MUL), v, st2["gate"])
            for hh in range(2):
                for b, c0, c1_ in ((0, 0, 128), (1, 128, 384)):
                    x = SX[:, hh, c0:c1_]
                    v = act(af(x, x, ACT.Copy, scale=RC[:, hh, b:b + 1]), v)
            yield
            for hh in range(2):
                for c in range(3):
                    tok = pe(tr(PS[:, S0 + hh, c * 128:(c + 1) * 128], SX[:, hh, c * 128:(c + 1) * 128],
                                mat("ident")), v, free[S0 + hh], inc=True)
            rd[kx] = tok
            s = act(af(PT[:, :, :], PS[:, S0:S0 + 2, 0:384], ACT.Copy), tok, rd.get(kp), rd.get("BLK"))
            free[S0] = free[S0 + 1] = s
            yield
            for hh in range(2):
                vv = [VN2[:, br, c, j * 64:(j + 1) * 64] for c in range(2)]
                pe_wait = (s, st2["v"][br], free[OB])
                pe(mm(PS[hh * 64:hh * 64 + 64, OB, 0:P], vv[0], PT[:, hh, 0:128], first[hh], False), *pe_wait)
                first[hh] = False
                pe(mm(PS[hh * 64:hh * 64 + 64, OB, P:2 * P], vv[0], PT[:, hh, 128:256], False, False))
                tok = pe(mm(PS[hh * 64:hh * 64 + 64, OB, P:2 * P], vv[1], PT[:, hh, 256:384], False, False), inc=True)
            rd[kp] = tok
        for hh in range(2):
            for b in range(2):
                tok = pe(mm(PS[:, S0 + hh, b * 15:(b + 1) * 15], Q2[hh * 64:hh * 64 + 64, t, b * P:(b + 1) * P],
                            KDC[hh * 64:hh * 64 + 64, j, :]), st2["kdc"], free[S0], free[S0 + 1], inc=True)
        cb = CBI[:, :, :].rearrange("p (b n) h -> p b n h", b=2)
        for hh in range(2):
            v = dve(tt(SC[:, hh, :, :], PS[:, S0 + hh, 0:30].rearrange("p (b n) -> p b n", b=2),
                       cb[:, :, :, 2 * t + hh], ADD), tok, rd.get(kc))
        free[S0] = free[S0 + 1] = v
        v = dve(lambda e: e.tensor_reduce(NM, SC[:, :, :, :], AXX, MAX), v)
        for hh in range(2):
            x = SC[:, hh, :, :]
            v1 = dve(tt(x, x, last(NM[:, hh, :], 15), SUB), v)
        s = act(af(SC[:, :, :, :], SC[:, :, :, :], ACT.Exp), v1)
        v = dve(lambda e: e.tensor_reduce(DEN, SC[:, :, :, :], AXX, ADD), s)
        v = dve(lambda e: e.reciprocal(RC, DEN), v)
        v1 = dve(ts(NM, NM, -1e29, None, ALU.is_gt), v1)
        v = dve(tt(RC, RC, NM, MUL), v, v1)
        for hh in range(2):
            v = dve(tt(RC[:, hh, :], RC[:, hh, :], GAT[:, :, 3 * (2 * t + hh)], MUL), v)
        for hh in range(2):
            x = SC[:, hh, :, :]
            v1 = dve(tt(x, x, last(RC[:, hh, :], 15), MUL), v)
        yield
        for hh in range(2):
            for b in range(2):
                tok = pe(tr(PS[0:15, S0 + hh, b * P:(b + 1) * P], SC[:, hh, b, :], mat("ident")), v1, free[S0 + hh],
                         inc=True)
        rd[kc] = tok
        s = act(af(PT[0:15, :, 0:256], PS[0:15, S0:S0 + 2, 0:256], ACT.Copy), tok, rd.get(kp))
        free[S0] = free[S0 + 1] = s
        yield
        for hh in range(2):
            for b in range(2):
                tok = pe(mm(PS[hh * 64:hh * 64 + 64, OB, b * P:(b + 1) * P], VC[0:15, j * 64:(j + 1) * 64],
                            PT[0:15, hh, b * P:(b + 1) * P], False, True), s, st2["vc"], inc=True)
        rd[kp] = tok
        free[OB] = split_to(MX, t, PS[:, OB, 0:T], tok, 1.0, st2["w1read"])
        yield

    def load_pos():
        post_ = load("pool", "p1", PSC[0:64, :, :], a["cmp_posT"], A1.read)
        post2 = load("pool", "p2", PSC[64:128, :, :], a["cmp_posT"], A1.read)
        st2["pos"] = (post_, post2)
        a_pos[0], a_pos[1] = PSC[:, 0, :], PSC[:, 1, :]

    def pre_cmp():
        load_pos()
        for _ in join():
            pass

    for i in range(4):
        unit(w_in2, 0, 16, 2608 + 256 * i, U2, ev_ca(i), mid=pre_cmp if i == 0 else None,
             gens=[turn_bias()] if i == 0 else ())
        unit(w_in2, 0, 16, 3632 + 256 * i, U2, ev_cg(i), before=drain if i == 0 else None, gens=[conv31(i)])
    for br in range(2):
        unit(w_in2, 0, 16, 1536 + 512 * br, U2, ev_k2(br), before=drain,
             gens=([layer_norm()] if br == 0 else []) + [dup_k2(br)])
        unit(w_in2, 0, 16, 1792 + 512 * br, U2, ev_v2(br), natural=True)
    unit(w_in2, 0, 16, 1024, U2, ev_cmp(0), before=drain, gens=[compress(0)])
    unit(w_in2, 0, 16, 1280, U2, ev_cmp(1), before=drain, gens=[compress(1)])
    unit(w_in2, 0, 16, 2560, U2, ev_gate, nc_=48, natural=True)
    for i in range(4):
        unit(w_in2, 0, 16, 256 * i, U2, ev_q2(i), before=drain if i == 1 else None, banks=(0, 1),
             gens=([2] if i == 0 else []) + [attn2(2 * i), attn2(2 * i + 1)] + ([1] if i == 3 else []))

    class View:
        def __init__(self, src, k0):
            self.s, self.k0 = src, k0
            self.read = None

        @property
        def ready(self):
            return self.s.ready[self.k0:]

        def hi(self, k):
            return self.s.hi(self.k0 + k)

        def lo(self, k):
            return self.s.lo(self.k0 + k)

    def ev_add(i):
        h = H[:, 2 * i:2 * i + 2, :]
        return lambda b, tok: dve(tt(h, h, bank(b), ADD), tok, st2["x"])

    MXC, MXA = View(MX, 8), View(MX, 0)
    for i in range(8):
        unit(a["w_out_2"], 1024, 8, 256 * i, MXC, ev_add(i), banks=(0, 1))


    F2 = Acts(CHt, 0, 16)
    N7 = Norm(0, D, 1e-6)
    for i in range(8):
        unit(a["w_out_2"], 0, 8, 256 * i, MXA, ev_h(i, (F2, lambda k: vec("gf2", k)), [N7], lambda: attn_done()),
             before=drain if i == 0 else None,
             mid=(lambda: clear_pads(MX.ready[7], rd["SX21"], rd["PT21"], rd["SCM1"])) if i == 0 else None)

    def attn_done():
        return MX.ready[7]

    def conv3(z, o, col, v, *w):
        first = [act(af(o[:, m, :], z[:, m, 28:28 + T], ACT.Identity, scale=vec("fcw", 3 * (col + m)),
                        bias=vec("fcb", col + m)), v, *w) for m in range(2)]
        for k in (1, 2):
            for m in range(2):
                x = z[:, m, 28 + k:28 + k + T]
                v = dve(stt(o[:, m, :], x, vec("fcw", 3 * (col + m) + k), o[:, m, :], MUL, ADD), first[m])
        return v

    def evg2(half, i, A):
        def f(b, tok):
            fr = v = dve(tt(Z[0][:, :, 30:286], bank(b), two(N7.rb()), MUL), tok, N7.tok, rd.get("Z0"), pads[0])
            v = conv3(Z[0], TA, 44 + 2 * (11 * half + i), v, rd.get("TA"))
            s = act(af(TB[:, :, :], TA[:, :, :], ACT.Tanh, scale=0.5), v, rd.get("TB"))
            rd["g"] = rd["TB"] = dve(stt(TA[:, :, :], TB[:, :, :], 1.0, TA[:, :, :], ADD, MUL), s)
            return fr
        return f

    def evu2(half, i, A, fr_):
        def f(b, tok):
            fr = v = dve(tt(Z[1][:, :, 30:286], bank(b), two(N7.rb()), MUL), tok, N7.tok, rd.get("Z1"), pads[1])
            v = conv3(Z[1], TC, 2 * (11 * half + i), v, rd.get("TC"))
            v = dve(tt(TC[:, :, :], TC[:, :, :], TA[:, :, :], MUL), v, rd["g"])
            for m in range(2):
                split_to(A, 2 * i + m, TC[:, m, :], v, 0.5, fr_())
            rd["TC"] = A.ready[2 * i + 1]
            return fr
        return f

    N8 = Norm(1, D, 1e-6)

    def ev_fin(i):
        def f(b, tok):
            h = H[:, 2 * i:2 * i + 2, :]
            v = dve(tt(h, h, bank(b), ADD), tok)
            N8.add(h, v)
            return v
        return f

    ffn(a["w_up_2"], FFN, a["w_up_2"], 0, a["w_down_2"], F2, N7, evg2, evu2, ev_fin, lambda: MXA.read)

    run_stream(start())

    N8.finish()
    outv = out.rearrange("(t p) n -> p t n", p=P)
    for i in range(8):
        for k in (2 * i, 2 * i + 1):
            v = dve(stt(H[:, k, :], H[:, k, :], vec("gfin2", k), N8.rb(), MUL, MUL), N8.tok)
        load("sp", "out", outv[:, 2 * i:2 * i + 2, :], H[:, 2 * i:2 * i + 2, :], v)
    Q.q["sp"].append(("wait", sems["out"], Q.count["out"]))

    with nc.Block() as block:
        @block.sync
        def _(e):
            Q.run("sp", e)

        @block.gpsimd
        def _(e):
            Q.run("pool", e)

        @block.scalar
        def _(e):
            Q.run("act", e)

        @block.vector
        def _(e):
            Q.run("dve", e)

        @block.tensor
        def _(e):
            Q.run("pe", e)


def _cols(v):
    v = np.asarray(v)
    return v.reshape(-1, P).T


def _taps(w):
    w = np.asarray(w)
    k, c = w.shape
    return w.reshape(k, c // P, P).transpose(2, 1, 0).reshape(P, -1)


def _bucket(dist):
    n = np.maximum(dist, 0)
    nf = np.maximum(n, 1).astype(np.float32)
    large = 16 + (np.log(nf / np.float32(16)) / np.float32(np.log(8.0)) * np.float32(16)).astype(np.int32)
    return np.where(n < 16, n, np.minimum(large, 31))


def _constants():
    i = np.arange(P)
    eye = np.eye(P, dtype=np.float32)
    rot = np.zeros((P, P), np.float32)
    for m in range(P):
        if m % 64 < 32:
            rot[m + 32, m] = -1.0
        else:
            rot[m - 32, m] = 1.0
    dup = []
    for hp in range(2):
        e = np.zeros((P, P), np.float32)
        e[hp * 64 + i % 64, i] = 1.0
        dup.append(e)
    rdup = [(rot[:, hp * 64 + i % 64]).copy() for hp in range(2)]
    triu = (i[:, None] <= i[None, :]).astype(np.float32)
    negt = np.where(i[:, None] <= i[None, :], 0.0, NEG).astype(np.float32)
    mats = [eye, rot, dup[0], dup[1], rdup[0], rdup[1], triu, negt, np.ones((P, P), np.float32),
            eye[::-1].copy()]
    mats = np.ascontiguousarray(np.concatenate(mats, 1))
    cur = np.where(i[None, :] <= i[:, None], 0.0, NEG)
    prev = np.where(i[None, :] > i[:, None], 0.0, NEG)
    mask1 = np.concatenate([cur, prev, cur], 1).astype(np.float32)
    dist = 255 - np.arange(384)
    oh = np.zeros((33, 384), np.float32)
    for c, d in enumerate(dist):
        if d >= 0:
            oh[_bucket(np.array(d)), c] = 1.0
        else:
            oh[32, c] = NEG
    ohc = np.zeros((33, 2, 15, P), np.float32)
    for b in range(2):
        for n in range(15):
            for q in range(P):
                d = b * P + q - (16 * n + 31)
                if d >= 0:
                    ohc[_bucket(np.array(d)), b, n, q] = 1.0
                else:
                    ohc[32, b, n, q] = NEG
    invf = (np.float32(10000.0) ** (-np.arange(32, dtype=np.float32) * np.float32(2.0) / np.float32(64))).astype(
        np.float32)
    return mats, mask1, oh, ohc.reshape(33, -1), invf[i % 32][:, None]


def kernel(**inputs):
    import concourse.bacc as bacc
    from concourse.bass_utils import run_bass_kernel_spmd

    x = {k: np.asarray(v) for k, v in inputs.items()}
    mats, mask1, oh, ohc, invf = _constants()
    dsk = np.repeat(x["d_skip"][0], 64).reshape(16, P).T
    parts = dict(
        g_mix=_cols(x["g_mix"][0]), cw=_taps(x["conv_w"][0]), cb=_cols(x["conv_b"][0]), g_ssd=_cols(x["g_ssd"][0]),
        dsk=dsk, g_ffn=_cols(x["g_ffn"][0]), g_ple=_cols(x["g_ple"][0]), g_fin=_cols(x["g_final"]),
        gm2=_cols(x["mix_norm_g_2"][0]), cw2=_taps(x["conv_w_2"][0]), cb2=_cols(x["conv_b_2"][0]),
        lng=_cols(x["conv_ln_g_2"][0]), lnb=_cols(x["conv_ln_b_2"][0]), gf2=_cols(x["ffn_norm_g_2"][0]),
        fcw=_taps(x["ffn_conv_w_2"][0]), fcb=_cols(x["ffn_conv_b_2"][0]), gfin2=_cols(x["final_norm_g_2"]),
        invf=invf)
    arrays = {
        "xT": x["x"][0].T,
        "pT": x["p"][0, 0].T,
        "positions": x["positions"].reshape(1, 256),
        "mats": mats,
        "mask1": mask1,
        "vecs": np.concatenate([parts[n] for n, _ in VECS], 1),
        "rows": np.concatenate([x["sinks"][0], x["dt_bias"][0], x["a_log"][0]])[None, :],
        "c33": np.concatenate([oh, np.concatenate([x["rel_bias_2"], np.ones((1, 16), np.float32)], 0)], 1),
        "ohc": ohc,
        "w_in": x["w_in"][0], "w_attn_br": x["w_attn_br"][0], "w_ssd_br": x["w_ssd_br"][0], "w_o": x["w_o"][0],
        "w_gate": x["w_gate"][0], "w_up": x["w_up"][0], "w_down": x["w_down"][0],
        "w_ple_gate": x["w_ple_gate"][0], "w_ple_proj": x["w_ple_proj"][0],
        "w_in_2": x["w_in_2"][0], "cmp_posT": x["cmp_pos_2"][0].transpose(2, 0, 1),
        "cmp_w1": x["cmp_w1_2"][0], "cmp_w2": x["cmp_w2_2"][0], "w_out_2": x["w_out_2"][0],
        "w_up_2": x["w_up_2"][0], "w_down_2": x["w_down_2"][0],
    }
    nc = bacc.Bacc("TRN2", target_bir_lowering=False, num_devices=1)
    feed, args = {}, {}
    for name, v in arrays.items():
        v = np.ascontiguousarray(v)
        feed[f"in_{name}"] = v
        args[name] = nc.dram_tensor(f"in_{name}", v.shape, mybir.dt.from_np(v.dtype), kind="ExternalInput").ap()
    out = nc.dram_tensor("out_T", (D, T), F32, kind="ExternalOutput").ap()
    hybrid_block_kernel(nc, args, out)
    r = run_bass_kernel_spmd(nc, [feed], core_ids=[0])
    return np.ascontiguousarray(r.results[0]["out_T"].T).reshape(1, T, D)
```

```python
from collections import deque

import numpy as np

import concourse.bass as bass
from concourse import mybir

F32 = mybir.dt.float32
F32R = mybir.dt.float32r
I32 = mybir.dt.int32
ALU = mybir.AluOpType
ACT = mybir.ActivationFunctionType
AXX = mybir.AxisListType.X

P = 128
T = 256
D = 2048
KD = D // P
FFN = 5632
NEG = -1e30

NSUB = 4
NRAW = 4
NHL = 5
LEAD = 4
LAG = 2
HOLD = 2
LATE = 3

MATS = ["rot", "rdup0", "rdup1", "triu", "negT", "dup0", "dup1", "anti", "ident", "ones"]

VECS = [("g_mix", 16), ("cw", 96), ("cb", 24), ("g_ssd", 16), ("dsk", 16), ("g_ffn", 16), ("g_ple", 16),
        ("g_fin", 16), ("gm2", 16), ("cw2", 248), ("cb2", 8), ("lng", 8), ("lnb", 8), ("gf2", 16),
        ("fcw", 264), ("fcb", 88), ("gfin2", 16), ("invf", 1)]
VOFF = {}
_o = 0
for _n, _w in VECS:
    VOFF[_n] = (_o, _w)
    _o += _w
NVEC = _o


class Queues:

    def __init__(self, sems):
        self.sems = sems
        self.q = {k: [] for k in ("pe", "act", "dve", "pool", "sp")}
        self.count = {k: 0 for k in sems}
        self.seen = {}

    def put(self, eng, fn, waits, inc=None, by=1):
        for w in waits:
            if w is None:
                continue
            name, value = w
            if self.seen.get((eng, name), 0) >= value:
                continue
            self.seen[(eng, name)] = value
            self.q[eng].append(("wait", self.sems[name], value))
        if inc is None:
            self.q[eng].append(("op", fn, None, 0))
            return None
        self.count[inc] += by
        self.q[eng].append(("op", fn, self.sems[inc], by))
        return (inc, self.count[inc])

    def run(self, eng, e):
        for item in self.q[eng]:
            if item[0] == "wait":
                e.wait_ge(item[1], item[2])
            else:
                _, fn, sem, by = item
                ins = fn(e)
                if sem is not None:
                    ins.then_inc(sem, by)


class Side:

    def __init__(self):
        self.todo, self.live, self.width = deque(), [], 1

    def extend(self, gens):
        self.todo.extend(gens)

    def step(self):
        while self.todo and len(self.live) < self.width:
            if isinstance(self.todo[0], int):
                if self.live:
                    break
                self.width = self.todo.popleft()
            else:
                self.live.append(self.todo.popleft())
        for g in list(self.live):
            if next(g, "end") == "end":
                self.live.remove(g)

    def drain(self):
        while self.todo or self.live:
            self.step()


class Acts:

    def __init__(self, tensor, base, n):
        self.t, self.base, self.n = tensor, base, n
        self.ready = [None] * n
        self.read = None

    def hi(self, k):
        return self.t[:, self.base + k, 0:T]

    def lo(self, k):
        return self.t[:, self.base + k, T:2 * T]


def hybrid_block_kernel(nc, a, out):
    names = ["pe", "act", "dve", "pool"]
    sems = {n: nc.alloc_semaphore(f"s_{n}") for n in names}
    for i in range(NRAW):
        sems[f"w{i}"] = nc.alloc_semaphore(f"s_w{i}")
    for n in ("cm", "mk", "p1", "p2", "cv", "row", "pos", "x0", "x1", "x2", "x3", "c33", "ohc", "rel", "bmw", "bmr", "p", "w1k", "w1v", "w2c", "out"):
        sems[n] = nc.alloc_semaphore(f"s_d_{n}")
    Q = Queues(sems)

    BASE = 16512
    top = [BASE]

    def place(name, shape, dt=F32, at=None):
        n = 4
        for s in shape[1:]:
            n *= s
        if at is None:
            at = top[0]
            top[0] += (n + 31) // 32 * 32
        return nc.alloc_sbuf_tensor_at(name, shape, dt, offset=at)

    RAW = [place(f"raw{i}", [P, NSUB, 256]) for i in range(NRAW)]
    WH = [place(f"wh{i}", [P, NSUB, 256], F32R) for i in range(NHL)]
    WL = [place(f"wl{i}", [P, NSUB, 256], F32R) for i in range(NHL)]
    at_ah = top[0]
    AHt = place("AHt", [P, 16, 512], F32R)
    at_ch = top[0]
    CHt = place("CHt", [P, 16, 512], F32R)
    at_big = top[0]
    BIGt = place("BIGt", [P, 22, 512], F32R)
    H = place("H", [P, 16, T])
    at_x = top[0]
    ROW = place("ROW", [P, 80])
    RB = [place("RB0", [P, T + 2])]
    M9 = place("M9", [P, 8, P])
    CV = place("CV", [P, NVEC])
    RB.append(place("RB1", [P, T + 2]))
    M2 = place("M2", [P, 2, P])
    SQA = place("SQA", [P, 2, T])
    at_z = top[0]
    Z = [place("Z0", [P, 2, 286]), place("Z1", [P, 2, 286])]
    TA = place("TA", [P, 2, T])
    TB = place("TB", [P, 2, T])
    TC = place("TC", [P, 2, T])
    NAT = place("NAT", [P, 8, 2, 32])
    at_nat = top[0] - 2048
    W2 = nc.alloc_sbuf_tensor_at("W2C", [64, 2, 64], F32, offset=at_nat)
    GAT = nc.alloc_sbuf_tensor_at("GAT", [P, 2, 48], F32, offset=at_nat + 1024)
    CBI = place("CBI", [P, 30, 16])
    SM = place("SM", [P, 64])
    G12 = place("G12", [P, 16])
    assert top[0] <= 229368, top[0]

    XS = place("XS", [P, 16, T], at=at_ch)
    MG = place("MG", [P, 16, T], at=at_ch + 16384)
    QT = place("QT", [P, 8, T], at=at_ch + 16384)
    KDU = place("KDU", [P, 4, T], at=at_ch + 24576)
    VN = place("VN", [P, 2, T], at=at_ch + 28672)
    KT1 = place("KT1", [P, 2, T], at=at_ch + 30720)
    sc = at_big + 16384
    BCT = place("BCT", [P, 8, T], at=sc)
    COS = place("COS", [P, T], at=sc + 8192)
    SIN = place("SIN", [P, T], at=sc + 9216)
    MK1 = place("MK1", [P, 384], at=sc + 10240)
    SX1 = [place("SX1a", [P, 2, 384], at=sc + 12288), place("SX1b", [P, 2, 384], at=sc + 18432)]
    PT1 = [place("PT1a", [P, 2, 384], at=sc + 15360), place("PT1b", [P, 2, 384], at=sc + 21504)]
    RO = place("RO", [P, 2, 2, T], at=sc + 18432)
    PI = place("PI", [P, T], I32, at=sc + 22528)
    XD = place("XD", [P, 2, 512], at=sc + 8192)
    XDS = place("XDS", [P, 512], at=sc + 12288)
    STG = place("STG", [P, 512], at=sc + 14336)
    BNC = place("BNC", [P, 3, P], at=sc + 16384)
    DEC = [place(f"DEC{i}", [P, 4, P], at=sc + 17920 + 2048 * i) for i in range(2)]
    CXE = [place(f"CXE{i}", [P, 4, P], at=sc + 22016 + 2048 * i) for i in range(2)]
    ECS = place("ECS", [P, 4, P], at=sc + 26112)
    C33 = place("C33", [33, 400], at=at_big)
    OHC = place("OHC", [33, 3840], at=sc + 12288)
    RV = place("RV", [16, 384], at=at_big + 2048)
    BM = place("BM", [P, 16, T], at=at_ch)
    Q2 = place("Q2", [P, 8, T], at=at_ch + 16384)
    KD2 = place("KD2", [P, 2, 4, T], at=at_ch + 24576)
    bg = at_big + 32768
    VN2 = place("VN2", [P, 2, 2, T], at=bg)
    VC = place("VC", [15, T], at=bg + 4096)
    KDC = place("KDC", [P, 4, 15], at=bg + 5120)
    SX2 = [place("SX2a", [P, 2, 384], at=bg + 5376), place("SX2b", [P, 2, 384], at=at_x)]
    PT2 = [place("PT2a", [P, 2, 384], at=bg + 8448), place("PT2b", [P, 2, 384], at=at_x + 3072)]
    SCM = [place("SCMa", [P, 2, 2, 15], at=bg + 11520), place("SCMb", [P, 2, 2, 15], at=at_x + 6144)]
    BLK = place("BLK", [P, 32, 30], at=bg + 5376)
    KTC = place("KTC", [P, 2, T], at=bg + 9216)
    PSC = place("PSC", [P, 2, 32], at=bg + 11264)
    GCM = place("GCM", [64, 60], at=bg + 11776)
    GTM = place("GTM", [64, 60], at=bg + 12032)
    W1 = [place("W1K", [P, 32, 64], at=at_ah), place("W1V", [P, 32, 64], at=at_ah + 8192)]

    BMR = place("BMR", [P, 16, T], at=at_ah + 16384)
    CC = [place(f"CC{i}", [P, T], at=at_ah + (8 + i) * 2048 + 1024) for i in range(8)]
    Z2, Z3 = place("Z2", [P, 2, 286], at=at_ah + 4 * 2048), place("Z3", [P, 2, 286], at=at_ah + 6 * 2048)
    PPT = place("PPT", [P, 2, T], at=at_ch)
    PHL = place("PHL", [P, 2, 512], F32R, at=at_ch + 2048)
    PR = place("PR", [P, 16, T], at=at_ch + 8192)

    PS = nc.alloc_psum_tensor("PS", [P, 8, 512], F32)
    scratch = nc.dram_tensor("bias_rows", [16, 384], F32).ap()

    def mat(n):
        i = MATS.index(n)
        return M9[:, i, :] if i < 8 else M2[:, i - 8, :]

    def vec(n, i=0, w=1):
        o = VOFF[n][0] + i
        return CV[:, o:o + w]

    def pe(fn, *w, inc=False):
        return Q.put("pe", fn, w, "pe" if inc else None)

    def act(fn, *w):
        return Q.put("act", fn, (*w, ("act", Q.count["act"] + 1 - LAG)), "act")

    def dve(fn, *w):
        return Q.put("dve", fn, (*w, ("dve", Q.count["dve"] + 1 - LAG)), "dve")

    def pool(fn, *w):
        return Q.put("pool", fn, w, "pool")

    def load(eng, name, dst, src, *w):
        return Q.put(eng, lambda e: e.dma_start(dst, src), w, name, 16)

    def mm(o, l, r, start=True, stop=True):
        return lambda e: e.matmul(o, l, r, start=start, stop=stop, skip_group_check=True)

    def tr(o, i, ident):
        return lambda e: e.transpose(o, i, ident)

    def tt(o, x, y, op):
        return lambda e: e.tensor_tensor(o, x, y, op)

    def ts(o, x, s1, s2, o0, o1=None):
        if o1 is None:
            return lambda e: e.tensor_scalar(o, x, s1, None, o0)
        return lambda e: e.tensor_scalar(o, x, s1, s2, o0, o1)

    def stt(o, x, s, y, o0, o1):
        return lambda e: e.scalar_tensor_tensor(out=o, in0=x, scalar=s, in1=y, op0=o0, op1=o1)

    def af(o, x, f, **k):
        return lambda e: e.activation(o, x, f, **k)

    def cp(o, x):
        return lambda e: e.tensor_copy(o, x)

    ADD, SUB, MUL, MAX, MIN = ALU.add, ALU.subtract, ALU.mult, ALU.max, ALU.min

    def two(ap):
        return ap.unsqueeze(1).broadcast_to([ap.shape[0], 2, ap.shape[1]])

    def last(ap, n):
        return ap.unsqueeze(ap.ndim).broadcast_to(list(ap.shape) + [n])

    def bank(b):
        return PS[:, b, :].rearrange("p (m t) -> p m t", m=2)

    free = {b: None for b in range(8)}
    rd = {}

    def f32(ap):
        return ap.bitcast(F32)

    def split_to(dst, k, v, tok, scale=1.0, *w):
        hi = act(af(dst.hi(k), v, ACT.Copy, scale=scale), tok, *w)
        lo = dve(stt(dst.lo(k), v, scale, f32(dst.hi(k)), MUL, SUB), hi, tok, *w)
        dst.ready[k] = lo
        return lo

    units = []

    def unit(w, row0, nk, c0, rhs, evac, nc_=256, natural=False, gens=(), gens2=(), before=None, mid=None,
             banks=(0, 1, 2), pace=1, hold=0):
        units.append(dict(w=w, row0=row0, nk=nk, c0=c0, rhs=rhs, evac=evac, nc=nc_, nat=natural,
                          gens=list(gens), gens2=list(gens2), before=before, mid=mid, banks=banks, pace=pace, hold=hold))

    def run_stream(start):
        subs = []
        for u in units:
            k = 0
            while k < u["nk"]:
                n = min(NSUB, u["nk"] - k)
                subs.append((u, k, n))
                k += n
        hilo = {}
        rawfree = {}
        pesub = {}

        def fetch(s):
            u, k, n = subs[s]
            r0 = u["row0"] + k * P
            src = u["w"][r0:r0 + n * P, u["c0"]:u["c0"] + u["nc"]].rearrange("(t p) n -> p t n", p=P)
            tok = load("sp", f"w{s % NRAW}", RAW[s % NRAW][:, 0:n, 0:u["nc"]], src, rawfree.get(s - NRAW))
            hilo[s] = tok

        def split(s):
            u, k, n = subs[s]
            tok = hilo[s]
            raw = RAW[s % NRAW][:, 0:n, 0:u["nc"]]
            hi = WH[s % NHL][:, 0:n, 0:u["nc"]]
            lo = WL[s % NHL][:, 0:n, 0:u["nc"]]
            h = act(af(hi, raw, ACT.Copy), tok, pesub.get(s - NHL))
            d = dve(tt(lo, raw, f32(hi), SUB), tok, h)
            rawfree[s] = d
            hilo[s] = d

        nf = ns = 0
        gb = 0
        slot = 0
        for s in range(min(NRAW, len(subs))):
            fetch(s)
        nf = NRAW
        for s in range(4):
            next(start)
            split(s)
            ns += 1
        for _ in start:
            pass
        held, gens_at = [], []

        def end(u, b, tok):
            if u["mid"]:
                u["mid"]()
            free[b] = u["evac"](b, tok)

        for s, (u, k, n) in enumerate(subs):
            while nf < len(subs) and nf - NRAW < ns:
                fetch(nf)
                nf += 1
            while ns < len(subs) and ns <= s + LEAD:
                split(ns)
                ns += 1
                if nf < len(subs) and nf - NRAW < ns:
                    fetch(nf)
                    nf += 1
            if k == 0:
                if u["before"]:
                    u["before"]()
                b = u["banks"][gb % len(u["banks"])]
                gb += 1
                u["bank"] = b
            b = u["bank"]
            rhs = u["rhs"]
            w = [hilo[s], free[b] if k == 0 else None]
            hi, lo = WH[s % NHL], WL[s % NHL]
            tok = None
            for t in range(n):
                kt = k + t
                w.append(rhs.ready[kt])
                firstk, lastk = kt == 0, kt == u["nk"] - 1
                if u["nat"]:
                    nco = u["nc"]
                    for bb in range(2):
                        o = PS[:, b, bb * nco:(bb + 1) * nco]
                        xh = rhs.hi(kt)[:, bb * P:(bb + 1) * P]
                        xl = rhs.lo(kt)[:, bb * P:(bb + 1) * P]
                        pe(mm(o, xh, hi[:, t, 0:nco], firstk and bb == 0, False), *w)
                        w = []
                        pe(mm(o, xl, hi[:, t, 0:nco], False, False))
                        fin = t == n - 1 and bb == 1
                        tok = pe(mm(o, xh, lo[:, t, 0:nco], False, lastk), inc=fin)
                else:
                    for m in range(2):
                        o = PS[:, b, m * T:(m + 1) * T]
                        wh, wl = hi[:, t, m * P:(m + 1) * P], lo[:, t, m * P:(m + 1) * P]
                        pe(mm(o, wh, rhs.hi(kt), firstk and m == 0, False), *w)
                        w = []
                        pe(mm(o, wh, rhs.lo(kt), False, False))
                        fin = t == n - 1 and m == 1
                        tok = pe(mm(o, wl, rhs.hi(kt), False, lastk), inc=fin)
            pesub[s] = tok
            if k + n == u["nk"]:
                rhs.read = tok
                held.append((s + u["hold"], u, b, tok))
                gens_at.append((s + u["hold"], u))
            while held and held[0][0] <= s:
                end(*held.pop(0)[1:])
            slot += 1
            conv.step()
            if slot % u["pace"] == 0:
                side.step()
            for g in [x for x in gens_at if x[0] <= s]:
                gens_at.remove(g)
                side.extend(g[1]["gens"])
                conv.extend(g[1]["gens2"])

    side, conv = Side(), Side()

    def drain():
        side.drain()

    def drain_all():
        conv.drain()
        side.drain()

    class Norm:

        def __init__(self, i, n, eps):
            self.i, self.n, self.eps = i, n, eps
            self.tok = None
            self.first = True

        def square(self, src, tok, buf=0):
            self.buf, self.key = ((TB, "TB"), (TC, "TC"))[buf]
            return act(af(self.buf[:, :, :], src, ACT.Square), tok, rd.get(self.key))

        def gather(self, s):
            if self.first:
                t = dve(cp(SQA[:, :, :], self.buf[:, :, :]), s, rd.get("SQA"))
                self.first = False
            else:
                t = dve(tt(SQA[:, :, :], SQA[:, :, :], self.buf[:, :, :], ADD), s, self.last)
            rd[self.key] = t
            self.last = t

        def add(self, src, tok, buf=0):
            self.gather(self.square(src, tok, buf))

        def finish(self, b=7):
            o = PS[:, b, :]
            pe(mm(o[:, 0:T], mat("ones"), SQA[:, 0, :], True, False), self.last, free[b], cmt)
            pe(mm(o[:, 0:T], mat("ones"), SQA[:, 1, :], False, True))
            for c in range(2):
                pe(mm(o[:, T + c:T + c + 1], SQA[:, 0, c * P:(c + 1) * P], mat("ones")[:, 0:1], False, False))
                t = pe(mm(o[:, T + c:T + c + 1], SQA[:, 1, c * P:(c + 1) * P], mat("ones")[:, 0:1], False, True),
                       inc=True)
            rd["SQA"] = t
            r = RB[self.i]
            v = dve(ts(r[:, :], o[:, 0:T + 2], 1.0 / self.n, self.eps, MUL, ADD), t)
            free[b] = v
            v = act(af(r[:, :], r[:, :], ACT.Sqrt), v)
            self.tok = dve(lambda e: e.reciprocal(r[:, :], r[:, :]), v)
            return self.tok

        def rb(self):
            return RB[self.i][:, 0:T]

        def rn(self, c):
            return RB[self.i][:, T + c:T + c + 1]

    nload = ["x0", "x1", "x2", "x3"]
    cvt = load("act", "cv", CV[:, :], a["vecs"])
    xts = []
    for i in range(4):
        src = a["xT"][512 * i:512 * (i + 1), :].rearrange("(t p) n -> p t n", p=P)
        xts.append(load("sp" if i % 2 == 0 else "act", nload[i], H[:, 4 * i:4 * i + 4, :], src))
    load("act", "cm", M9[:, :, :].rearrange("p a b -> p (a b)"), a["mats"][:, 0:8 * P])
    cmt = load("act", "cm", M2[:, :, :].rearrange("p a b -> p (a b)"), a["mats"][:, 8 * P:])
    post = load("act", "pos", PI[:, :], a["positions"].partition_broadcast(P))
    rowt = load("act", "row", ROW[:, :], a["rows"].partition_broadcast(P))
    mkt = load("act", "mk", MK1[:, :], a["mask1"])
    c33t = load("act", "c33", C33[:, :], a["c33"])
    pads = {}

    def clear_pad(i, z, *w):
        pads[i] = pool(lambda e: e.memset(z[:, :, 0:30], 0.0), *w)

    clear_pad(0, Z[0])
    clear_pad(1, Z[1])
    sinks, dtb, alog = ROW[:, 0:16], ROW[:, 16:48], ROW[:, 48:80]
    NSK = SM[:, 0:16]
    U1 = Acts(AHt, 0, 16)
    N1 = Norm(0, D, 1e-6)
    st1 = {"q": [None] * 4, "kd": [None] * 4, "attn": None}

    def start():
        for i in range(4):
            for k in range(4 * i, 4 * i + 4):
                w0 = act(af(U1.hi(k), H[:, k, :], ACT.Copy, scale=vec("g_mix", k)), cvt, xts[i])
                U1.ready[k] = dve(stt(U1.lo(k), H[:, k, :], vec("g_mix", k), f32(U1.hi(k)), MUL, SUB), w0, cvt,
                                  xts[i])
            yield

    def sum_x():
        for t in range(8):
            N1.add(H[:, 2 * t:2 * t + 2, :], xts[t // 2], t % 2)
            if t % 2:
                yield

    def rotary():
        ang, kk, r0 = RO[:, 0, 0, :], RO[:, 0, 1, :], RO[:, 1, 0, :]
        v = dve(cp(ang, PI[:, :]), post)
        v = dve(ts(ang, ang, vec("invf"), None, MUL), v, cvt)
        BIGM = 12582912.0
        v = dve(ts(kk, ang, float(np.float32(1 / (2 * np.pi))), BIGM, MUL, ADD), v)
        v = dve(ts(kk, kk, -BIGM, None, ADD), v)
        c1, c2 = 6.25, 0.033203125
        c3 = float(np.float32(np.round((2 * np.pi - c1 - c2) * 2 ** 27) / 2 ** 27))
        c4 = float(np.float32(2 * np.pi - c1 - c2 - c3))
        src = ang
        yield
        for c in (c1, c2, c3, c4):
            v = dve(stt(r0, kk, -c, src, MUL, ADD), v)
            src = r0
        lim = 3.1415925
        v = dve(ts(r0, r0, lim, -lim, MIN, MAX), v)
        yield
        s1 = act(af(SIN[:, :], r0, ACT.Sin), v)
        v = dve(ts(kk, r0, -1.0, None, MUL), v)
        v = dve(tt(kk, kk, r0, MAX), v)
        v = dve(ts(kk, kk, -1.0, float(np.float32(np.pi / 2)), MUL, ADD), v)
        st1["trig"] = act(af(COS[:, :], kk, ACT.Sin), v, s1)
        st1["oh"] = load("pool", "ohc", OHC[:, :], a["ohc"], st1["trig"])
        st1["nsk"] = dve(ts(NSK, sinks, -1.0, None, MUL), rowt)
        st1["aex"] = act(af(alog, alog, ACT.Exp), rowt)
        st1["g12"] = dve(tt(G12[:, :], vec("g_fin", 0, 16), vec("gm2", 0, 16), MUL), cvt)
        yield

    def biases():
        bt = pe(mm(PS[0:16, 6, 0:384], C33[:, 384:400], C33[:, 0:384]), c33t, free[6], inc=True)
        for i in range(30):
            ct = pe(mm(PS[:, 5, i * 16:(i + 1) * 16], OHC[:, i * P:(i + 1) * P], C33[:, 384:400]), st1["oh"], free[5],
                    inc=i == 29)
        rd["OHC"] = ct
        yield
        rv = dve(cp(RV[:, :], PS[0:16, 6, 0:384]), bt)
        free[6] = rv
        st1["bmw"] = load("pool", "bmw", scratch, RV[:, :], rv)
        st1["cbi"] = free[5] = dve(cp(CBI[:, :, :].rearrange("p a b -> p (a b)"), PS[:, 5, 0:480]), ct)
        yield

    w_in = a["w_in"]

    def ev_q(i):
        def f(b, tok):
            o = QT[:, 2 * i:2 * i + 2, :]
            v = dve(stt(o, bank(b), 0.125, two(N1.rb()), MUL, MUL), tok, N1.tok)
            st1["q"][i] = v
            return v
        return f

    def rope_q(i):
        o = QT[:, 2 * i:2 * i + 2, :]
        b = 6
        pe(mm(PS[:, b, 0:T], mat("rot"), QT[:, 2 * i, :]), st1["q"][i], free[b], cmt)
        tok = pe(mm(PS[:, b, T:512], mat("rot"), QT[:, 2 * i + 1, :]), inc=True)
        yield
        x = RO[:, 0, :, :]
        v = dve(tt(x, bank(b), two(SIN[:, :]), MUL), tok, st1["trig"], rd["OHC"])
        free[b] = v
        y = dve(tt(o, o, two(COS[:, :]), MUL))
        st1["q"][i] = dve(tt(o, o, x, ADD), y)
        yield

    def ev_k(b, tok):
        v = dve(tt(KT1[:, :, :], bank(b), two(N1.rb()), MUL), tok, N1.tok)
        st1["k"] = v
        return v

    def rope_k(t):
        for b, n in ((5, "dup"), (6, "rdup")):
            for hp in range(2):
                tok = pe(mm(PS[:, b, hp * T:(hp + 1) * T], mat(f"{n}{hp}"), KT1[:, t, :]), st1["k"], free[b], inc=True)
        yield
        x, y = RO[:, 0, :, :], RO[:, 1, :, :]
        v1 = dve(tt(x, bank(5), two(COS[:, :]), MUL), tok, st1["trig"])
        v2 = dve(tt(y, bank(6), two(SIN[:, :]), MUL), tok)
        free[5], free[6] = v1, v2
        v = dve(tt(KDU[:, 2 * t:2 * t + 2, :], x, y, ADD), v2)
        st1["kd"][2 * t] = st1["kd"][2 * t + 1] = v
        yield

    def ev_v(b, tok):
        for c in range(2):
            v = act(af(VN[:, c, :], PS[:, b, c * T:(c + 1) * T], ACT.Copy, scale=N1.rn(c)), tok, N1.tok)
        st1["v"] = v
        return v

    AT = Acts(BIGt, 0, 8)

    def attn1(t, late):
        for _ in range(late):
            yield
        j = t // 2
        u = t % 2
        S0, SX, PT = (3, 6)[u], SX1[u], PT1[u]
        kx, kp = f"SX{u}", f"PT{u}"
        for hh in range(2):
            q, k = QT[hh * 64:hh * 64 + 64, t, :], KDU[hh * 64:hh * 64 + 64, j, :]
            pe(mm(PS[:, S0 + hh, 0:128], q[:, 0:128], k[:, 0:128]), st1["q"][t // 2], st1["kd"][j], free[S0], free[S0 + 1])
            tok = pe(mm(PS[:, S0 + hh, 128:384], q[:, 128:256], k[:, 0:256]), inc=True)
        v = dve(tt(SX[:, :, :], PS[:, S0:S0 + 2, 0:384], two(MK1[:, :]), ADD), tok, mkt, rd.get(kx))
        free[S0] = free[S0 + 1] = v
        NM, DEN, ES, RC = (SM[:, 16 + 16 * u + 4 * i:20 + 16 * u + 4 * i].rearrange("p (h b) -> p h b", b=2) for i in range(4))
        for b, c0, c1_ in ((0, 0, 128), (1, 128, 384)):
            v = dve(lambda e, b=b, c0=c0, c1_=c1_: e.tensor_reduce(NM[:, :, b], SX[:, :, c0:c1_], AXX, MAX,
                                                                 negate=True), v)
        v = dve(tt(NM, NM, last(NSK[:, 2 * t:2 * t + 2], 2), MIN), v, st1["nsk"])
        es = dve(tt(ES, NM, last(sinks[:, 2 * t:2 * t + 2], 2), ADD), v)
        for hh in range(2):
            for b, c0, c1_ in ((0, 0, 128), (1, 128, 384)):
                x = SX[:, hh, c0:c1_]
                s = act(af(x, x, ACT.Exp, bias=NM[:, hh, b:b + 1], accum_out=DEN[:, hh, b:b + 1]), v)
        s = act(af(ES, ES, ACT.Exp), es)
        yield
        v = dve(tt(DEN, DEN, ES, ADD), s)
        v = dve(lambda e: e.reciprocal(RC, DEN), v)
        for hh in range(2):
            for b, c0, c1_ in ((0, 0, 128), (1, 128, 384)):
                x = SX[:, hh, c0:c1_]
                s = act(af(x, x, ACT.Copy, scale=RC[:, hh, b:b + 1]), v)
        yield
        yield
        for hh in range(2):
            for c in range(3):
                tok = pe(tr(PS[:, S0 + hh, c * 128:(c + 1) * 128], SX[:, hh, c * 128:(c + 1) * 128], mat("ident")),
                         s, free[S0 + hh], inc=True)
        rd[kx] = tok
        s = act(af(PT[:, :, :], PS[:, S0:S0 + 2, 0:384], ACT.Copy), tok, rd.get(kp))
        free[S0] = free[S0 + 1] = s
        yield
        yield
        for hh in range(2):
            o = PS[hh * 64:hh * 64 + 64, 5, :]
            vv = [VN[:, c, j * 64:(j + 1) * 64] for c in range(2)]
            pe(mm(o[:, 0:128], vv[0], PT[:, hh, 0:128]), s, free[5], st1["v"])
            pe(mm(o[:, 128:256], vv[0], PT[:, hh, 128:256], True, False))
            tok = pe(mm(o[:, 128:256], vv[1], PT[:, hh, 256:384], False, True), inc=True)
        rd[kp] = tok
        free[5] = split_to(AT, t, PS[:, 5, 0:T], tok, 1.0, st1["bmw"])
        st1["attn"] = tok
        yield

    def n_(i):
        return NAT[:, i, :, :]

    DT, AN, NCS, DSE = n_(0), n_(1), n_(2), n_(3)[:, 0, :]

    def ev_dt(b, tok):
        x, ax, e_, s_, q_, w_ = DT, n_(4), n_(5), n_(6), n_(7), AN
        for c in range(2):
            v = dve(stt(x[:, c, :], PS[:, b, c * 32:(c + 1) * 32], N1.rn(c), dtb, MUL, ADD), tok, N1.tok, rowt)
        fr = v
        v = dve(ts(ax, x, -1.0, None, MUL), v)
        v = dve(tt(ax, ax, x, MAX), v)
        s = act(af(e_, ax, ACT.Exp, scale=-1.0), v)
        v = dve(ts(s_, e_, 2.0, None, ADD), s)
        v = dve(lambda e: e.reciprocal(s_, s_), v)
        v = dve(tt(s_, s_, e_, MUL), v)
        v = dve(tt(q_, s_, s_, MUL), v)
        v = dve(ts(w_, q_, 1.0 / 17, 1.0 / 15, MUL, ADD), v)
        for c in (13, 11, 9, 7, 5, 3, 1):
            v = dve(tt(w_, w_, q_, MUL), v)
            v = dve(ts(w_, w_, 1.0 / c, None, ADD), v)
        v = dve(tt(w_, w_, s_, MUL), v)
        v = dve(ts(x, x, 0.0, None, MAX), v)
        v = dve(stt(x, w_, 2.0, x, MUL, ADD), v)
        v = dve(stt(AN, x, -1.0, alog.unsqueeze(1).broadcast_to([P, 2, 32]), MUL, MUL), v, st1["aex"])
        st1["dt"] = v
        return fr

    def cums():
        o = PS[:, 7, :]
        for c in range(2):
            pe(mm(o[:, c * 32:(c + 1) * 32], mat("triu"), AN[:, c, :]), st1["dt"], free[7])
        tok = pe(mm(o[:, 64:96], mat("ones"), AN[:, 0, :]), inc=True)
        yield
        v = dve(ts(NCS, o[:, 0:64].rearrange("p (c h) -> p c h", c=2), -1.0, None, MUL), tok)
        v = dve(tt(DSE, o[:, 64:96], NCS[:, 0, :], ADD), v)
        free[7] = v
        st1["cs"] = act(af(DSE, DSE, ACT.Exp), v)
        yield

    xbc_ready, xbc_in = [None] * 12, [None] * 12

    def ev_xbc(i):
        def f(b, tok):
            z = Z[i % 2]
            xbc_in[i] = dve(tt(z[:, :, 30:286], bank(b), two(N1.rb()), MUL), tok, N1.tok, pads[i % 2], rd.get(f"Z{i % 2}"))
            return xbc_in[i]
        return f

    def conv4(i):
        z = Z[i % 2]
        w = [xbc_in[i]] * 2
        for k in range(4):
            for m in range(2):
                c = 2 * i + m
                x = z[:, m, 27 + k:27 + k + T]
                if k == 0:
                    v = dve(ts(TA[:, m, :], x, vec("cw", 4 * c), vec("cb", c), MUL, ADD), w[m], rd.get("TA"))
                else:
                    v = dve(stt(TA[:, m, :], x, vec("cw", 4 * c + k), TA[:, m, :], MUL, ADD), w[m])
                w[m] = v
            if k == 1:
                yield
        s = act(af(TB[:, :, :], TA[:, :, :], ACT.Tanh, scale=0.5), v, rd.get("TB"))
        yield
        v = dve(stt(TC[:, :, :], TB[:, :, :], 1.0, TA[:, :, :], ADD, MUL), s, rd.get("TC"))
        rd["TB"] = v
        dst = XS[:, 2 * i:2 * i + 2, :] if i < 8 else BCT[:, 2 * (i - 8):2 * (i - 8) + 2, :]
        xbc_ready[i] = rd["TC"] = act(af(dst, TC[:, :, :], ACT.Copy, scale=0.5), v)
        yield

    y_ready = [None] * 8

    def ssd(g):
        rdy = [xbc_ready[2 * g], xbc_ready[2 * g + 1], xbc_ready[8 + g // 2], xbc_ready[10 + g // 2], st1["cs"]]
        Bt, Ct = BCT[:, g, :], BCT[:, 4 + g, :]
        for c in range(2):
            for i in range(4):
                tok = pe(tr(PS[:, 3 + c, i * P:(i + 1) * P], XS[:, 4 * g + i, c * P:(c + 1) * P], mat("ident")),
                         *rdy, free[3], free[4], inc=True)
        pe(tr(PS[:, 5, 0:P], Bt[:, 0:P], mat("ident")), free[5])
        for c in range(2):
            tk2 = pe(mm(PS[:, 5, (1 + c) * P:(2 + c) * P], Bt[:, c * P:(c + 1) * P], Ct[:, c * P:(c + 1) * P]),
                     inc=True)
        s0 = act(af(BNC[:, :, :].rearrange("p a b -> p (a b)"), PS[:, 5, 0:384], ACT.Copy), tk2, st1["attn"],
                 rd.get("BNC"))
        free[5] = s0
        for c in range(2):
            v = dve(tt(XD[:, c, :].rearrange("p (h d) -> p h d", d=64),
                       PS[:, 3 + c, :].rearrange("p (h d) -> p h d", d=64),
                       last(DT[:, c, 8 * g:8 * g + 8], 64), MUL), tok, st1["attn"], rd.get("XD"))
        free[3] = free[4] = v
        xd = v
        xds = dve(tt(XDS[:, :].rearrange("p (h d) -> p h d", d=64), XD[:, 0, :].rearrange("p (h d) -> p h d", d=64),
                     last(DSE[:, 8 * g:8 * g + 8], 64), MUL), v)
        yield
        tok = pe(mm(PS[:, 5, :], BNC[:, 0, :], XDS[:, :]), xds, s0, inc=True)
        stt_ = act(af(STG[:, :], PS[:, 5, :], ACT.Copy), tok, rd.get("STG"))
        free[5] = stt_

        def decays(n):
            c, hf = n // 2, n % 2
            h0 = 8 * g + 4 * hf
            bb = 3 + hf
            dk = DEC[n % 2]
            for i in range(4):
                tok = pe(mm(PS[:, bb, i * P:(i + 1) * P], AN[:, c, h0 + i:h0 + i + 1].broadcast_to([P, P]),
                            mat("triu")), free[bb], inc=True)
            bv = PS[:, bb, :].rearrange("p (i l) -> p i l", l=P)
            v = dve(tt(dk[:, :, :], bv, mat("negT").unsqueeze(1).broadcast_to([P, 4, P]), ADD), tok,
                    rd.get(f"DEC{n % 2}"))
            free[bb] = v
            for i in range(4):
                s = act(af(dk[:, i, :], dk[:, i, :], ACT.Exp, bias=NCS[:, c, h0 + i:h0 + i + 1]), v)
            if c == 1:
                e = act(af(ECS[:, :, :], bv, ACT.Exp), v, rd.get("ECS"))
                free[bb] = e
            mt = dve(tt(dk[:, :, :], dk[:, :, :], BNC[:, 1 + c, :].unsqueeze(1).broadcast_to([P, 4, P]), MUL), s, s0)
            if c == 1:
                mt = rd["ECS"] = dve(tt(CXE[hf][:, :, :], ECS[:, :, :],
                                        Ct[:, P:2 * P].unsqueeze(1).broadcast_to([P, 4, P]), MUL), e,
                                     rd.get(f"CXE{hf}"))
            return mt

        mt = decays(0)
        yield
        for n in range(4):
            c, hf = n // 2, n % 2
            mt, now = (decays(n + 1) if n < 3 else None), mt
            for i in range(4):
                hh = 4 * hf + i
                o = PS[(i % 2) * 64:(i % 2) * 64 + 64, 6, (i // 2) * P:(i // 2 + 1) * P]
                tok = pe(mm(o, XD[:, c, hh * 64:(hh + 1) * 64], DEC[n % 2][:, i, :], True, c == 0), now, free[6],
                         stt_, inc=True)
                if c == 1:
                    tok = pe(mm(o, STG[:, hh * 64:(hh + 1) * 64], CXE[hf][:, i, :], False, True), inc=True)
            rd[f"DEC{n % 2}"] = tok
            if c == 1:
                rd[f"CXE{hf}"] = tok
            for i in range(2):
                tile = 4 * g + 2 * hf + i
                y = XS[:, tile, c * P:(c + 1) * P]
                v = dve(stt(y, y, vec("dsk", tile), PS[:, 6, i * P:(i + 1) * P], MUL, ADD), tok)
            free[6] = v
            if c == 1:
                y_ready[2 * g + hf] = v
            yield
        rd["XD"] = rd["STG"] = rd["BNC"] = tok

    for i in range(4):
        unit(w_in, 0, 16, 256 * i, U1, ev_q(i), mid=N1.finish if i == 0 else None, hold=2 if i == 0 else 0,
             gens=([rotary(), biases()] if i == 0 else []) + [rope_q(i)])
    unit(w_in, 0, 16, 1024, U1, ev_k, gens=[rope_k(0), rope_k(1)])
    unit(w_in, 0, 16, 1280, U1, ev_v, natural=True, gens=[2] + [attn1(t, LATE if t == 1 else 0) for t in range(8)] + [1])
    unit(w_in, 0, 16, 6656, U1, ev_dt, nc_=32, natural=True, gens=[cums()], pace=2)
    for i in range(12):
        unit(w_in, 0, 16, 3584 + 256 * i, U1, ev_xbc(i), gens2=[conv4(i)])

    mg = [None] * 8

    def ev_ga(i):
        def f(b, tok):
            v = dve(tt(TA[:, :, :], bank(b), two(N1.rb()), MUL), tok, rd.get("TA"))
            rd["TA"] = s = act(af(MG[:, 2 * i:2 * i + 2, :], TA[:, :, :], ACT.Tanh, scale=0.5), v)
            mg[i] = s
            return v
        return f

    def ev_oa(i):
        def f(b, tok):
            o = MG[:, 2 * i:2 * i + 2, :]
            mg[i] = dve(stt(o, o, 1.0, bank(b), ADD, MUL), tok, mg[i])
            return mg[i]
        return f

    for i in range(8):
        unit(w_in, 0, 16, 6688 + 256 * i, U1, ev_ga(i), before=drain_all if i == 0 else None,
             gens=[ssd(g) for g in range(4)] if i == 0 else (), pace=2)
        unit(a["w_attn_br"], 0, 8, 256 * i, AT, ev_oa(i), pace=2)

    YH = Acts(BIGt, 0, 16)
    N2 = Norm(1, D, 1e-5)

    def ev_z(i):
        def f(b, tok):
            z = Z[i % 2][:, :, 30:286]
            fr = v = dve(tt(z, bank(b), two(N1.rb()), MUL), tok)
            s = act(af(TA[:, :, :], z, ACT.Tanh, scale=0.5), v, rd.get("TA"))
            v = dve(stt(TA[:, :, :], TA[:, :, :], 1.0, z, ADD, MUL), s)
            v = dve(stt(TC[:, :, :], TA[:, :, :], 0.5, XS[:, 2 * i:2 * i + 2, :], MUL, MUL), v, rd.get("TC"),
                    y_ready[i])
            N2.add(TC[:, :, :], v)
            for m in range(2):
                k = 2 * i + m
                rd["TC"] = act(af(YH.hi(k), TC[:, m, :], ACT.Copy, scale=vec("g_ssd", k)), v, AT.read, st1["ssd"])
                YH.ready[k] = dve(stt(YH.lo(k), TC[:, m, :], vec("g_ssd", k), f32(YH.hi(k)), MUL, SUB), rd["TC"],
                                  AT.read, st1["ssd"])
            return fr
        return f

    def before_z():
        drain()
        st1["ssd"] = rd["XD"]

    for i in range(8):
        unit(w_in, 0, 16, 1536 + 256 * i, U1, ev_z(i), before=before_z if i == 0 else None)
    GSB = XS
    gs = [None] * 8

    def ev_gs(i):
        def f(b, tok):
            v = dve(tt(TA[:, :, :], bank(b), two(N1.rb()), MUL), tok, rd.get("TA"))
            rd["TA"] = gs[i] = act(af(GSB[:, 2 * i:2 * i + 2, :], TA[:, :, :], ACT.Tanh, scale=0.5), v)
            return v
        return f

    for i in range(8):
        unit(w_in, 0, 16, 8736 + 256 * i, U1, ev_gs(i), mid=N2.finish if i == 0 else None, hold=HOLD if i == 0 else 0)
    MH = Acts(AHt, 0, 16)

    def ev_os(i):
        def f(b, tok):
            s_ = slice(2 * i, 2 * i + 2)
            fr = v = dve(tt(TA[:, :, :], bank(b), two(N2.rb()), MUL), tok, N2.tok, rd.get("TA"))
            v = dve(stt(TA[:, :, :], GSB[:, s_, :], 1.0, TA[:, :, :], ADD, MUL), v, gs[i])
            v = dve(tt(TA[:, :, :], TA[:, :, :], MG[:, s_, :], ADD), v)
            for m in range(2):
                split_to(MH, 2 * i + m, TA[:, m, :], v, 0.5, U1.read)
            rd["TA"] = MH.ready[2 * i + 1]
            return fr
        return f

    for i in range(8):
        unit(a["w_ssd_br"], 0, 16, 256 * i, YH, ev_os(i))

    def ev_h(i, nxt=None, norms=(), prev=lambda: None):
        def f(b, tok):
            h = H[:, 2 * i:2 * i + 2, :]
            fr = v = dve(tt(h, h, bank(b), ADD), tok, rd.get("H"))
            if nxt is not None:
                finish_h(i, v, nxt, norms, prev())
            return fr
        return f

    def finish_h(i, v, nxt, norms, pw):
        h = H[:, 2 * i:2 * i + 2, :]
        dst, gv = nxt
        ks = (2 * i, 2 * i + 1)
        hi = [act(af(dst.hi(k), H[:, k, :], ACT.Copy, scale=gv(k)), v, pw) for k in ks]
        sq = [n.square(h, v) for n in norms]
        for k, s in zip(ks, hi):
            dst.ready[k] = dve(stt(dst.lo(k), H[:, k, :], gv(k), f32(dst.hi(k)), MUL, SUB), s, pw)
        for n, s in zip(norms, sq):
            n.gather(s)

    F1 = Acts(CHt, 0, 16)
    N3 = Norm(0, D, 1e-6)
    for i in range(8):
        unit(a["w_o"], 0, 16, 256 * i, MH, ev_h(i, (F1, lambda k: vec("g_ffn", k)), [N3], lambda: mhw()))

    def mhw():
        return MH.ready[15]

    WIDE = (0, 1, 2, 3, 4)

    def ffn(wg, gcol, wu, ucol, wd, fin, norm, evg, evu, last_h, free0, between=None):
        fr = free0
        for half in range(2):
            A = Acts(BIGt, 0, 22)
            for i in range(11):
                unit(wg, 0, 16, gcol + 256 * (11 * half + i), fin, evg(half, i, A), banks=WIDE,
                     mid=norm.finish if half == 0 and i == 0 else None, hold=HOLD if half == 0 and i == 0 else 0)
                unit(wu, 0, 16, ucol + 256 * (11 * half + i), fin, evu(half, i, A, fr), banks=WIDE)
            for i in range(8):
                if between and half and i == 3:
                    between()
                unit(wd, 2816 * half, 22, 256 * i, A, last_h(i) if half else ev_h(i), banks=WIDE)
            fr = lambda A=A: A.read
        return A

    def evg1(half, i, A):
        def f(b, tok):
            z = Z[i % 2][:, :, 30:286]
            fr = v = dve(tt(z, bank(b), two(N3.rb()), MUL), tok, N3.tok)
            s = act(af(TA[:, :, :], z, ACT.Tanh, scale=0.5), v, rd.get("TA"))
            rd["g"] = dve(stt(TA[:, :, :], TA[:, :, :], 1.0, z, ADD, MUL), s)
            return fr
        return f

    def evu1(half, i, A, fr_):
        def f(b, tok):
            fr = v = dve(tt(TC[:, :, :], bank(b), two(N3.rb()), MUL), tok, rd.get("TC"), N3.tok)
            v = dve(tt(TC[:, :, :], TC[:, :, :], TA[:, :, :], MUL), v, rd["g"])
            for m in range(2):
                split_to(A, 2 * i + m, TC[:, m, :], v, 0.5, fr_())
            rd["TC"] = A.ready[2 * i + 1]
            return fr
        return f

    P1H = Acts(AHt, 0, 16)
    N4 = Norm(1, D, 1e-6)

    PH = Acts(PHL, 0, 2)
    pr = [None] * 8

    def load_p():
        pt = load("pool", "p", PPT[:, :, :], a["pT"].rearrange("(t p) n -> p t n", p=P), F1.read)
        for k in range(2):
            split_to(PH, k, PPT[:, k, :], pt, 1.0, F1.read)

    def ev_pp(i):
        def f(b, tok):
            pr[i] = act(af(PR[:, 2 * i:2 * i + 2, :], bank(b), ACT.Copy), tok, F1.read)
            return pr[i]
        return f

    def p_units():
        units[-2]["mid"] = load_p
        for i in range(8):
            unit(a["w_ple_proj"], 0, 2, 256 * i, PH, ev_pp(i), banks=WIDE)

    A1 = ffn(a["w_gate"], 0, a["w_up"], 0, a["w_down"], F1, N3, evg1, evu1,
             lambda i: ev_h(i, (P1H, lambda k: vec("g_ple", k)), [N4], lambda: MH.read), lambda: YH.read, p_units)

    U2 = Acts(BIGt, 0, 16)
    N5, N6 = Norm(0, D, 1e-6), Norm(1, D, 1e-6)
    sqb = [None]

    def ev_pg(i):
        def f(b, tok):
            h = H[:, 2 * i:2 * i + 2, :]
            fr = v = dve(tt(TA[:, :, :], bank(b), two(N4.rb()), MUL), tok, N4.tok, rd.get("TA"))
            s = act(af(TA[:, :, :], TA[:, :, :], ACT.Tanh, scale=0.5), v)
            v = dve(stt(TC[:, :, :], TA[:, :, :], 1.0, PR[:, 2 * i:2 * i + 2, :], ADD, MUL), s, pr[i], rd.get("TC"))
            rd["TA"] = v
            v = dve(stt(h, TC[:, :, :], 0.5, h, MUL, ADD), v, rd.get("H"))
            rd["TC"] = v
            s5 = N5.square(h, v, 1)
            for m in range(2):
                s = act(af(TB[:, m, :], H[:, 2 * i + m, :], ACT.Square, scale=vec("g_fin", 2 * i + m)), v, rd["TB"])
            finish_h(i, v, (U2, lambda k: G12[:, k:k + 1]), [], A1.read)
            N5.gather(s5)
            if i == 0:
                rd["TB"] = sqb[0] = dve(cp(SQB, TB[:, :, :]), s)
            else:
                rd["TB"] = sqb[0] = dve(tt(SQB, SQB, TB[:, :, :], ADD), s, sqb[0])
            return fr
        return f

    SQB = Z[1][:, :, 30:286]
    for i in range(8):
        unit(a["w_ple_gate"], 0, 16, 256 * i, P1H, ev_pg(i), mid=N4.finish if i == 0 else None, hold=HOLD if i == 0 else 0, banks=WIDE)

    st2 = {"q": [None] * 4, "kd": {}, "v": {}}
    RX = RB[0]
    RU = RB[1]

    def join():
        t5 = N5.finish(7)
        o = PS[:, 6, :]
        pe(mm(o[:, 0:T], mat("ones"), SQB[:, 0, :], True, False), sqb[0], free[6])
        pe(mm(o[:, 0:T], mat("ones"), SQB[:, 1, :], False, True))
        for c in range(2):
            pe(mm(o[:, T + c:T + c + 1], SQB[:, 0, c * P:(c + 1) * P], mat("ones")[:, 0:1], False, False))
            t = pe(mm(o[:, T + c:T + c + 1], SQB[:, 1, c * P:(c + 1) * P], mat("ones")[:, 0:1], False, True), inc=True)
        rd["SQB"] = t
        yield
        ta = TA[:, :, :].rearrange("p a b -> p (a b)")[:, 0:T + 2]
        v = dve(tt(ta, RX[:, :], RX[:, :], MUL), t5, rd.get("TA"))
        v = dve(stt(ta, o[:, 0:T + 2], 1.0 / D, ta, MUL, MUL), v, t)
        free[6] = v
        v = dve(ts(ta, ta, 1e-6, None, ADD), v)
        s = act(af(ta, ta, ACT.Sqrt), v)
        v = dve(lambda e: e.reciprocal(ta, ta), s)
        N6.tok = dve(tt(RU[:, :], ta, RX[:, :], MUL), v)
        rd["TA"] = N6.tok
        st2["t5"] = t5
        st2["bmr"] = load("pool", "bmr", BMR[:, :, :], bass.AP(scratch.tensor, 0, [[1, P], [384, 16], [1, T]]), st1["bmw"],
                          P1H.read)
        w1 = a["cmp_w1"]
        for kv in range(2):
            src = w1[kv].rearrange("(l d) e -> d l e", d=64)
            for hp in range(2):
                st2[f"w1{kv}"] = load("pool", "w1k" if kv == 0 else "w1v", W1[kv][hp * 64:hp * 64 + 64, :, :], src,
                                      P1H.read)
        st2["w2"] = load("pool", "w2c", W2[:, 0:2, :], a["cmp_w2"].rearrange("k d e -> d k e"), P1H.read)
        yield

    def scale_h():
        for k in range(16):
            st2["x"] = dve(stt(H[:, k, :], H[:, k, :], vec("g_fin", k), RX[:, 0:T], MUL, MUL), st2["t5"],
                           U2.ready[15])
            if k % 2:
                yield

    def turn_bias():
        for i in range(4):
            for b in range(2):
                h = 4 * i + 2 * b
                tok = pe(mm(PS[:, 3 + b, :], mat("anti"), BMR[:, h:h + 2, :]), st2["bmr"], free[3 + b], inc=True)
            rd["CC"] = tok
            for b in range(2):
                h = 4 * i + 2 * b
                s = act(af(BM[:, h:h + 2, :], bank(3 + b), ACT.Copy), tok, U2.ready[15])
                free[3 + b] = s
            st2["bm"] = s
            yield

    w_in2 = a["w_in_2"]

    def ev_cmp(kv):
        def f(b, tok):
            v = dve(tt(KTC[:, :, :], bank(b), two(N6.rb()), MUL), tok, N6.tok, rd.get("KTC"))
            blk = BLK[:, :, :].rearrange("p l (t n) -> p l t n", t=2)
            pos = a_pos[kv]
            for t in range(2):
                base = KTC[:, t, :]
                fr2 = dve(tt(blk[:, :, t, :],
                             bass.AP(KTC, t * T, [[2 * T, P], [1, 32], [16, 15]]),
                             last(pos, 15), ADD), v, rd.get("BLK"), *st2["pos"])
            rd["BLK_w"] = fr2
            return v
        return f

    a_pos = [None, None]

    def compress(kv):
        bd = BLK[:, :, :]
        for hp in range(2):
            for l in range(32):
                tok = pe(mm(PS[0:64, 3 + hp, 0:30], W1[kv][hp * 64:hp * 64 + 64, l, :],
                            bd[hp * 64:hp * 64 + 64, l, :], l == 0, l == 31),
                         rd["BLK_w"], st2[f"w1{kv}"], free[3], free[4], inc=l == 31)
        rd["BLK"] = rd["KTC"] = tok
        gv = GTM[:, :].rearrange("p (h n) -> p h n", h=2)
        v = dve(cp(gv, PS[0:64, 3:5, 0:30]), tok, rd.get("GTM"))
        free[3] = free[4] = v
        s = act(af(GCM[:, :], GTM[:, :], ACT.Tanh, scale=0.5), v, rd.get("GCM"))
        v = dve(stt(GCM[:, :], GCM[:, :], 1.0, GTM[:, :], ADD, MUL), s)
        v = dve(ts(GCM[:, :], GCM[:, :], 0.5, None, MUL), v)
        yield
        if kv == 0:
            for hh in range(2):
                tok = pe(mm(PS[hh * 64:hh * 64 + 64, 5, 0:60], W2[:, 0, :], GCM[:, :]), v, st2["w2"], free[5], inc=True)
            o = KDC[:, :, :].rearrange("p (t h) n -> p t h n", h=2)
            x = PS[:, 5, 0:60].rearrange("p (h t n) -> p t h n", h=2, t=2)
            for t in range(2):
                v = dve(cp(o[:, t], x[:, t]), tok, rd.get("KDC"))
            st2["kdc"] = free[5] = v
        else:
            for t in range(2):
                for hp in range(2):
                    c = (2 * t + hp) * 64
                    g = GCM[:, hp * 30 + t * 15:hp * 30 + t * 15 + 15]
                    tok = pe(mm(PS[0:15, 5, c:c + 64], g, W2[:, 1, :]), v, free[5], inc=True)
            st2["vc"] = free[5] = dve(cp(VC[:, :], PS[0:15, 5, 0:T]), tok)
        rd["GCM"] = tok
        st2["w1read"] = tok
        if kv == 1:
            clear_pad(2, Z2, tok)
            clear_pad(3, Z3, tok)
        yield

    def ev_k2(br):
        def f(b, tok):
            rd["k2"] = dve(tt(KTC[:, :, :], bank(b), two(N6.rb()), MUL), tok, N6.tok, rd.get("KTC"), A1.read)
            return rd["k2"]
        return f

    def dup_k2(br):
        for t in range(2):
            b = 5 + t
            for hp in range(2):
                tok = pe(mm(PS[:, b, hp * T:(hp + 1) * T], mat(f"dup{hp}"), KTC[:, t, :]), rd["k2"], free[b], inc=True)
        rd["KTC"] = tok
        yield
        for t in range(2):
            b = 5 + t
            v = dve(cp(KD2[:, br, 2 * t:2 * t + 2, :], bank(b)), tok, U2.ready[15])
            free[b] = v
        st2["kd"][br] = v
        yield

    def ev_v2(br):
        def f(b, tok):
            for c in range(2):
                v = act(af(VN2[:, br, c, :], PS[:, b, c * T:(c + 1) * T], ACT.Copy, scale=RU[:, T + c:T + c + 1]),
                        tok, N6.tok, A1.read)
            st2["v"][br] = v
            return v
        return f

    def ev_q2(i):
        def f(b, tok):
            st2["q"][i] = dve(stt(Q2[:, 2 * i:2 * i + 2, :], bank(b), 0.125, two(N6.rb()), MUL, MUL), tok, N6.tok,
                              U2.ready[15])
            return st2["q"][i]
        return f

    def ev_gate(b, tok):
        for c in range(2):
            v = dve(ts(GAT[:, c, :], PS[:, b, c * 48:(c + 1) * 48], RU[:, T + c:T + c + 1], None, MUL), tok, N6.tok)
        s = act(af(GAT[:, :, :], GAT[:, :, :], ACT.Tanh, scale=0.5), v)
        st2["gate"] = dve(ts(GAT[:, :, :], GAT[:, :, :], 0.5, 0.5, MUL, ADD), s)
        return v

    MX = Acts(AHt, 0, 16)

    def ev_ca(i):
        def f(b, tok):
            rd["ca"] = dve(tt(TC[:, :, :], bank(b), two(N6.rb()), MUL), tok, N6.tok, rd.get("TC"))
            return rd["ca"]
        return f

    cvin = [None] * 4
    ZC = Z + [Z2, Z3]
    rd["cv"] = {}
    SCC = SQA

    def ev_cg(i):
        def f(b, tok):
            z = ZC[i]
            fr = v = dve(tt(TA[:, :, :], bank(b), two(N6.rb()), MUL), tok, N6.tok, rd.get("TA"))
            s = act(af(TA[:, :, :], TA[:, :, :], ACT.Tanh, scale=0.5), v)
            v = dve(stt(TC[:, :, :], TA[:, :, :], 1.0, TC[:, :, :], ADD, MUL), s, rd["ca"])
            v = dve(ts(z[:, :, 30:286], TC[:, :, :], 0.5, None, MUL), v, rd.get("SQB"), pads[i])
            rd["TC"] = v
            cvin[i] = v
            return fr
        return f

    def conv31(i):
        z = ZC[i]
        w = [cvin[i]] * 2
        for k in range(31):
            for m in range(2):
                c = 2 * i + m
                x = z[:, m, k:k + T]
                o = CC[c][:, :]
                if k == 0:
                    v = dve(ts(o, x, vec("cw2", 31 * c), vec("cb2", c), MUL, ADD), w[m], P1H.read, rd["CC"])
                else:
                    v = dve(stt(o, x, vec("cw2", 31 * c + k), o, MUL, ADD), w[m])
                w[m] = v
            if k % (2 if i < 2 else 3) == 1:
                yield
        for m in range(2):
            c = 2 * i + m
            if c == 0:
                v = dve(cp(SCC[:, 0, :], CC[c][:, :]), v, rd.get("SQA"))
            else:
                v = dve(tt(SCC[:, 0, :], SCC[:, 0, :], CC[c][:, :], ADD), v)
        rd["scc"] = rd["cv"][i] = v
        yield

    def layer_norm():
        tok = pe(mm(PS[:, 7, 0:T], mat("ones"), SCC[:, 0, :]), rd["scc"], free[7], inc=True)
        mean = TA[:, 0, :]
        v = dve(ts(mean, PS[:, 7, 0:T], 1.0 / 1024, None, MUL), tok, rd.get("TA"))
        free[7] = v
        sq = {}
        for c in range(9):
            if c < 8:
                x = CC[c][:, :]
                v1 = dve(tt(x, x, mean, SUB), v)
                sq[c] = act(af(TB[:, c % 2, :], x, ACT.Square), v1, rd.get("TB"), rd.get(f"TB{c % 2}"))
            if c > 0:
                o = TB[:, (c - 1) % 2, :]
                if c == 1:
                    v2 = dve(cp(SCC[:, 0, :], o), sq[0], tok)
                else:
                    v2 = dve(tt(SCC[:, 0, :], SCC[:, 0, :], o, ADD), sq[c - 1], v2)
                rd[f"TB{(c - 1) % 2}"] = v2
            if c == 4:
                yield
        tok = pe(mm(PS[:, 7, 0:T], mat("ones"), SCC[:, 0, :]), v2, free[7], inc=True)
        rs = TA[:, 1, :]
        v = dve(ts(rs, PS[:, 7, 0:T], 1.0 / 1024, 1e-6, MUL, ADD), tok)
        free[7] = v
        s = act(af(rs, rs, ACT.Sqrt), v)
        v0 = dve(lambda e: e.reciprocal(rs, rs), s)
        th, zz, hi = {}, {}, {}
        for c in range(10):
            if c < 8:
                x = CC[c][:, :]
                v = dve(tt(x, x, rs, MUL), v0)
                v = dve(ts(x, x, vec("lng", c), vec("lnb", c), MUL, ADD), v)
                th[c] = act(af(TB[:, c % 2, :], x, ACT.Tanh, scale=0.5), v, rd[f"TB{c % 2}"])
            if 0 < c < 9:
                i = c - 1
                z = TC[:, i % 2, :]
                zz[i] = rd[f"TB{i % 2}"] = dve(stt(z, TB[:, i % 2, :], 1.0, CC[i][:, :], ADD, MUL), th[i],
                                               rd.get("TC"), rd.get(f"TC{i % 2}"))
                hi[i] = act(af(MX.hi(8 + i), z, ACT.Copy, scale=0.5), zz[i])
            if c > 1:
                i = c - 2
                MX.ready[8 + i] = rd[f"TC{i % 2}"] = dve(
                    stt(MX.lo(8 + i), TC[:, i % 2, :], 0.5, f32(MX.hi(8 + i)), MUL, SUB), hi[i], zz[i])
            if c % 2 == 1:
                yield
        rd["TA"] = rd["TC"] = rd["TB"] = rd["TC1"]
        rd["SQA"] = tok
        yield

    def attn2(t, late):
        for _ in range(late):
            yield
        j = t // 2
        u = t % 2
        S0, OB, SX, PT, SC = (3, 6)[u], (5, 2)[u], SX2[u], PT2[u], SCM[u]
        kx, kp, kc = f"SX2{u}", f"PT2{u}", f"SCM{u}"
        NM, DEN, RC = (SM[:, 16 + 16 * u + 4 * i:20 + 16 * u + 4 * i].rearrange("p (h b) -> p h b", b=2) for i in range(3))
        CM, CD, CR = (SM[:, 48 * u + 4 * i:4 + 48 * u + 4 * i].rearrange("p (h b) -> p h b", b=2) for i in range(3))
        halves = ((0, 0, 128), (1, 128, 384))

        def scores(br):
            for hh in range(2):
                q, k = Q2[hh * 64:hh * 64 + 64, t, :], KD2[hh * 64:hh * 64 + 64, br, j, :]
                pe(mm(PS[:, S0 + hh, 0:128], q[:, 0:128], k[:, 0:128]), st2["q"][t // 2], st2["kd"][br], free[S0],
                   free[S0 + 1])
                tok = pe(mm(PS[:, S0 + hh, 128:384], q[:, 128:256], k[:, 0:256]), inc=True)
            va = dve(tt(SX[:, :, 0:128], PS[:, S0:S0 + 2, 0:128], BM[:, 2 * t:2 * t + 2, 128:256], ADD), tok, st2["bm"],
                     rd.get(kx), rd.get("BLK"))
            vb = dve(tt(SX[:, :, 128:384], PS[:, S0:S0 + 2, 128:384], BM[:, 2 * t:2 * t + 2, :], ADD))
            free[S0] = free[S0 + 1] = vb
            for (b, c0, c1_), v in zip(halves, (va, vb)):
                v = dve(lambda e, b=b, c0=c0, c1_=c1_: e.tensor_reduce(NM[:, :, b], SX[:, :, c0:c1_], AXX, MAX,
                                                                     negate=True), v)
            for hh in range(2):
                for b, c0, c1_ in halves:
                    x = SX[:, hh, c0:c1_]
                    s = act(af(x, x, ACT.Exp, bias=NM[:, hh, b:b + 1], accum_out=DEN[:, hh, b:b + 1]), v)
            return s

        def scale(br, s):
            v = dve(lambda e: e.reciprocal(RC, DEN), s)
            for hh in range(2):
                v1 = dve(tt(RC[:, hh, :], RC[:, hh, :], GAT[:, :, 3 * (2 * t + hh) + 1 + br], MUL), v, st2["gate"])
            for hh in range(2):
                for b, c0, c1_ in halves:
                    x = SX[:, hh, c0:c1_]
                    s = act(af(x, x, ACT.Copy, scale=RC[:, hh, b:b + 1]), v1)
            return s

        def turn(v):
            for hh in range(2):
                for c in range(3):
                    tok = pe(tr(PS[:, S0 + hh, c * 128:(c + 1) * 128], SX[:, hh, c * 128:(c + 1) * 128],
                                mat("ident")), v, free[S0 + hh], inc=True)
            rd[kx] = tok
            s = act(af(PT[:, :, :], PS[:, S0:S0 + 2, 0:384], ACT.Copy), tok, rd.get(kp), rd.get("BLK"))
            free[S0] = free[S0 + 1] = s
            return s

        def values(br, s):
            for hh in range(2):
                vv = [VN2[:, br, c, j * 64:(j + 1) * 64] for c in range(2)]
                o = PS[hh * 64:hh * 64 + 64, OB, :]
                pe(mm(o[:, 0:P], vv[0], PT[:, hh, 0:128], br == 0, br == 1), s, st2["v"][br], free[OB])
                pe(mm(o[:, P:2 * P], vv[0], PT[:, hh, 128:256], False, False))
                tok = pe(mm(o[:, P:2 * P], vv[1], PT[:, hh, 256:384], False, br == 1), inc=True)
            rd[kp] = tok
            return tok

        def compressed():
            for hh in range(2):
                for b in range(2):
                    tok = pe(mm(PS[:, S0 + hh, b * 15:(b + 1) * 15], Q2[hh * 64:hh * 64 + 64, t, b * P:(b + 1) * P],
                                KDC[hh * 64:hh * 64 + 64, j, :]), st2["kdc"], free[S0], free[S0 + 1], inc=True)
            cb = CBI[:, :, :].rearrange("p (b n) h -> p b n h", b=2)
            for hh in range(2):
                v = dve(tt(SC[:, hh, :, :], PS[:, S0 + hh, 0:30].rearrange("p (b n) -> p b n", b=2),
                           cb[:, :, :, 2 * t + hh], ADD), tok, rd.get(kc))
            free[S0] = free[S0 + 1] = v
            v = dve(lambda e: e.tensor_reduce(CM, SC[:, :, :, :], AXX, MAX), v)
            for hh in range(2):
                x = SC[:, hh, :, :]
                v1 = dve(tt(x, x, last(CM[:, hh, :], 15), SUB), v)
            v2 = dve(ts(CM, CM, -1e29, None, ALU.is_gt), v1)
            return act(af(SC[:, :, :, :], SC[:, :, :, :], ACT.Exp), v1), v2

        def scale_compressed(s, v2):
            v = dve(lambda e: e.tensor_reduce(CD, SC[:, :, :, :], AXX, ADD), s)
            v = dve(lambda e: e.reciprocal(CR, CD), v)
            v = dve(tt(CR, CR, CM, MUL), v, v2)
            for hh in range(2):
                v1 = dve(tt(CR[:, hh, :], CR[:, hh, :], GAT[:, :, 3 * (2 * t + hh)], MUL), v, st2["gate"])
            for hh in range(2):
                x = SC[:, hh, :, :]
                v = dve(tt(x, x, last(CR[:, hh, :], 15), MUL), v1)
            return v

        def turn_compressed(v):
            for hh in range(2):
                for b in range(2):
                    tok = pe(tr(PS[0:15, S0 + hh, b * P:(b + 1) * P], SC[:, hh, b, :], mat("ident")), v, free[S0 + hh],
                             inc=True)
            rd[kc] = tok
            s = act(af(PT[0:15, :, 0:256], PS[0:15, S0:S0 + 2, 0:256], ACT.Copy), tok, rd.get(kp))
            free[S0] = free[S0 + 1] = s
            return s

        def values_compressed(s):
            for hh in range(2):
                for b in range(2):
                    tok = pe(mm(PS[hh * 64:hh * 64 + 64, OB, b * P:(b + 1) * P], VC[0:15, j * 64:(j + 1) * 64],
                                PT[0:15, hh, b * P:(b + 1) * P], False, False), s, st2["vc"], inc=True)
            rd[kp] = tok

        a0 = scores(0)
        yield
        c0 = compressed()
        a0 = scale(0, a0)
        yield
        c0 = scale_compressed(*c0)
        yield
        p0 = turn(a0)
        yield
        values(0, p0)
        a1 = scores(1)
        yield
        pc = turn_compressed(c0)
        a1 = scale(1, a1)
        yield
        values_compressed(pc)
        yield
        p1 = turn(a1)
        yield
        tok = values(1, p1)
        conv_read = None
        if t >= 4:
            while t // 2 not in rd["cv"]:
                conv.step()
            conv_read = rd["cv"][t // 2]
        free[OB] = split_to(MX, t, PS[:, OB, 0:T], tok, 1.0, st2["w1read"], conv_read)
        yield

    def load_pos():
        post_ = load("pool", "p1", PSC[0:64, :, :], a["cmp_posT"], A1.read)
        post2 = load("pool", "p2", PSC[64:128, :, :], a["cmp_posT"], A1.read)
        st2["pos"] = (post_, post2)
        a_pos[0], a_pos[1] = PSC[:, 0, :], PSC[:, 1, :]

    def before_attn():
        drain()
        side.width = 2

    def pre_cmp():
        load_pos()
        for _ in join():
            pass

    def ca_cg(i, **k):
        unit(w_in2, 0, 16, 2608 + 256 * i, U2, ev_ca(i), gens2=[turn_bias()] if i == 0 else [], **k)
        unit(w_in2, 0, 16, 3632 + 256 * i, U2, ev_cg(i),
             gens2=[conv31(i)] + ([layer_norm()] if i == 3 else []),
             banks=k.get("banks", (0, 1, 2)))

    def k2_v2(br, **k):
        unit(w_in2, 0, 16, 1536 + 512 * br, U2, ev_k2(br), gens=[dup_k2(br)] + ([scale_h()] if br else []),
             before=drain)
        unit(w_in2, 0, 16, 1792 + 512 * br, U2, ev_v2(br), natural=True)

    def q_(i, **k):
        unit(w_in2, 0, 16, 256 * i, U2, ev_q2(i), gens=[attn2(2 * i, 0), attn2(2 * i + 1, 2 if i == 0 else 0)],
             banks=(0, 1), **k)

    ca_cg(0, mid=pre_cmp, hold=HOLD)
    unit(w_in2, 0, 16, 1024, U2, ev_cmp(0), gens=[compress(0)])
    ca_cg(1)
    unit(w_in2, 0, 16, 1280, U2, ev_cmp(1), before=drain, gens=[compress(1)])
    k2_v2(0)
    k2_v2(1)
    ca_cg(2)
    unit(w_in2, 0, 16, 2560, U2, ev_gate, nc_=48, natural=True)
    q_(0, before=before_attn)
    ca_cg(3, banks=(0, 1))
    q_(1)
    q_(2)
    q_(3)

    class View:
        def __init__(self, src, k0):
            self.s, self.k0 = src, k0
            self.read = None

        @property
        def ready(self):
            return self.s.ready[self.k0:]

        def hi(self, k):
            return self.s.hi(self.k0 + k)

        def lo(self, k):
            return self.s.lo(self.k0 + k)

    def ev_add(i):
        h = H[:, 2 * i:2 * i + 2, :]
        return lambda b, tok: dve(tt(h, h, bank(b), ADD), tok, st2["x"])

    MXC, MXA = View(MX, 8), View(MX, 0)
    for i in range(8):
        unit(a["w_out_2"], 1024, 8, 256 * i, MXC, ev_add(i), banks=(0, 1), before=conv.drain if i == 0 else None)


    F2 = Acts(CHt, 0, 16)
    N7 = Norm(0, D, 1e-6)
    for i in range(8):
        unit(a["w_out_2"], 0, 8, 256 * i, MXA, ev_h(i, (F2, lambda k: vec("gf2", k)), [N7], lambda: attn_done()),
             before=drain if i == 0 else None)

    def attn_done():
        return MX.ready[7]

    def conv3(z, o, col, v, *w):
        first = [act(af(o[:, m, :], z[:, m, 28:28 + T], ACT.Identity, scale=vec("fcw", 3 * (col + m)),
                        bias=vec("fcb", col + m)), v, *w) for m in range(2)]
        for k in (1, 2):
            for m in range(2):
                x = z[:, m, 28 + k:28 + k + T]
                v = first[m] = dve(stt(o[:, m, :], x, vec("fcw", 3 * (col + m) + k), o[:, m, :], MUL, ADD), first[m])
        return v

    def evg2(half, i, A):
        def f(b, tok):
            fr = v = dve(tt(Z[0][:, :, 30:286], bank(b), two(N7.rb()), MUL), tok, N7.tok, rd.get("Z0"), pads[0])
            v = conv3(Z[0], TA, 44 + 2 * (11 * half + i), v, rd.get("TA"))
            s = act(af(TB[:, :, :], TA[:, :, :], ACT.Tanh, scale=0.5), v, rd.get("TB"))
            rd["g"] = rd["TB"] = dve(stt(TA[:, :, :], TB[:, :, :], 1.0, TA[:, :, :], ADD, MUL), s)
            return fr
        return f

    def evu2(half, i, A, fr_):
        def f(b, tok):
            fr = v = dve(tt(Z[1][:, :, 30:286], bank(b), two(N7.rb()), MUL), tok, N7.tok, rd.get("Z1"), pads[1])
            v = conv3(Z[1], TC, 2 * (11 * half + i), v, rd.get("TC"))
            v = dve(tt(TC[:, :, :], TC[:, :, :], TA[:, :, :], MUL), v, rd["g"])
            for m in range(2):
                split_to(A, 2 * i + m, TC[:, m, :], v, 0.5, fr_())
            rd["TC"] = A.ready[2 * i + 1]
            return fr
        return f

    N8 = Norm(1, D, 1e-6)

    def ev_fin(i):
        def f(b, tok):
            h = H[:, 2 * i:2 * i + 2, :]
            v = dve(tt(h, h, bank(b), ADD), tok)
            N8.add(h, v)
            return v
        return f

    ffn(a["w_up_2"], FFN, a["w_up_2"], 0, a["w_down_2"], F2, N7, evg2, evu2, ev_fin, lambda: MXA.read)

    side.extend([sum_x()])
    run_stream(start())

    N8.finish()
    outv = out.rearrange("(t p) n -> p t n", p=P)
    for i in range(8):
        for k in (2 * i, 2 * i + 1):
            v = dve(stt(H[:, k, :], H[:, k, :], vec("gfin2", k), N8.rb(), MUL, MUL), N8.tok)
        load("sp", "out", outv[:, 2 * i:2 * i + 2, :], H[:, 2 * i:2 * i + 2, :], v)
    Q.q["sp"].append(("wait", sems["out"], Q.count["out"]))

    with nc.Block() as block:
        @block.sync
        def _(e):
            Q.run("sp", e)

        @block.gpsimd
        def _(e):
            Q.run("pool", e)

        @block.scalar
        def _(e):
            Q.run("act", e)

        @block.vector
        def _(e):
            Q.run("dve", e)

        @block.tensor
        def _(e):
            Q.run("pe", e)


def _cols(v):
    v = np.asarray(v)
    return v.reshape(-1, P).T


def _taps(w):
    w = np.asarray(w)
    k, c = w.shape
    return w.reshape(k, c // P, P).transpose(2, 1, 0).reshape(P, -1)


def _bucket(dist):
    n = np.maximum(dist, 0)
    nf = np.maximum(n, 1).astype(np.float32)
    large = 16 + (np.log(nf / np.float32(16)) / np.float32(np.log(8.0)) * np.float32(16)).astype(np.int32)
    return np.where(n < 16, n, np.minimum(large, 31))


def _constants():
    i = np.arange(P)
    eye = np.eye(P, dtype=np.float32)
    rot = np.zeros((P, P), np.float32)
    for m in range(P):
        if m % 64 < 32:
            rot[m + 32, m] = -1.0
        else:
            rot[m - 32, m] = 1.0
    dup = []
    for hp in range(2):
        e = np.zeros((P, P), np.float32)
        e[hp * 64 + i % 64, i] = 1.0
        dup.append(e)
    rdup = [(rot[:, hp * 64 + i % 64]).copy() for hp in range(2)]
    triu = (i[:, None] <= i[None, :]).astype(np.float32)
    negt = np.where(i[:, None] <= i[None, :], 0.0, NEG).astype(np.float32)
    mats = [rot, rdup[0], rdup[1], triu, negt, dup[0], dup[1], eye[::-1], eye, np.ones((P, P), np.float32)]
    mats = np.ascontiguousarray(np.concatenate(mats, 1))
    cur = np.where(i[None, :] <= i[:, None], 0.0, NEG)
    prev = np.where(i[None, :] > i[:, None], 0.0, NEG)
    mask1 = np.concatenate([cur, prev, cur], 1).astype(np.float32)
    dist = 255 - np.arange(384)
    oh = np.zeros((33, 384), np.float32)
    for c, d in enumerate(dist):
        if d >= 0:
            oh[_bucket(np.array(d)), c] = 1.0
        else:
            oh[32, c] = NEG
    ohc = np.zeros((33, 2, 15, P), np.float32)
    for b in range(2):
        for n in range(15):
            for q in range(P):
                d = b * P + q - (16 * n + 31)
                if d >= 0:
                    ohc[_bucket(np.array(d)), b, n, q] = 1.0
                else:
                    ohc[32, b, n, q] = NEG
    invf = (np.float32(10000.0) ** (-np.arange(32, dtype=np.float32) * np.float32(2.0) / np.float32(64))).astype(
        np.float32)
    return mats, mask1, oh, ohc.reshape(33, -1), invf[i % 32][:, None]


def kernel(**inputs):
    import concourse.bacc as bacc
    from concourse.bass_utils import run_bass_kernel_spmd

    x = {k: np.asarray(v) for k, v in inputs.items()}
    mats, mask1, oh, ohc, invf = _constants()
    dsk = np.repeat(x["d_skip"][0], 64).reshape(16, P).T
    parts = dict(
        g_mix=_cols(x["g_mix"][0]), cw=_taps(x["conv_w"][0]), cb=_cols(x["conv_b"][0]), g_ssd=_cols(x["g_ssd"][0]),
        dsk=dsk, g_ffn=_cols(x["g_ffn"][0]), g_ple=_cols(x["g_ple"][0]), g_fin=_cols(x["g_final"]),
        gm2=_cols(x["mix_norm_g_2"][0]), cw2=_taps(x["conv_w_2"][0]), cb2=_cols(x["conv_b_2"][0]),
        lng=_cols(x["conv_ln_g_2"][0]), lnb=_cols(x["conv_ln_b_2"][0]), gf2=_cols(x["ffn_norm_g_2"][0]),
        fcw=_taps(x["ffn_conv_w_2"][0]), fcb=_cols(x["ffn_conv_b_2"][0]), gfin2=_cols(x["final_norm_g_2"]),
        invf=invf)
    arrays = {
        "xT": x["x"][0].T,
        "pT": x["p"][0, 0].T,
        "positions": x["positions"].reshape(1, 256),
        "mats": mats,
        "mask1": mask1,
        "vecs": np.concatenate([parts[n] for n, _ in VECS], 1),
        "rows": np.concatenate([x["sinks"][0], x["dt_bias"][0], x["a_log"][0]])[None, :],
        "c33": np.concatenate([oh, np.concatenate([x["rel_bias_2"], np.ones((1, 16), np.float32)], 0)], 1),
        "ohc": ohc,
        "w_in": x["w_in"][0], "w_attn_br": x["w_attn_br"][0], "w_ssd_br": x["w_ssd_br"][0], "w_o": x["w_o"][0],
        "w_gate": x["w_gate"][0], "w_up": x["w_up"][0], "w_down": x["w_down"][0],
        "w_ple_gate": x["w_ple_gate"][0], "w_ple_proj": x["w_ple_proj"][0],
        "w_in_2": x["w_in_2"][0], "cmp_posT": x["cmp_pos_2"][0].transpose(2, 0, 1),
        "cmp_w1": x["cmp_w1_2"][0], "cmp_w2": x["cmp_w2_2"][0], "w_out_2": x["w_out_2"][0],
        "w_up_2": x["w_up_2"][0], "w_down_2": x["w_down_2"][0],
    }
    nc = bacc.Bacc("TRN2", target_bir_lowering=False, num_devices=1)
    feed, args = {}, {}
    for name, v in arrays.items():
        v = np.ascontiguousarray(v)
        feed[f"in_{name}"] = v
        args[name] = nc.dram_tensor(f"in_{name}", v.shape, mybir.dt.from_np(v.dtype), kind="ExternalInput").ap()
    out = nc.dram_tensor("out_T", (D, T), F32, kind="ExternalOutput").ap()
    hybrid_block_kernel(nc, args, out)
    r = run_bass_kernel_spmd(nc, [feed], core_ids=[0])
    return np.ascontiguousarray(r.results[0]["out_T"].T).reshape(1, T, D)
```
